# Optimizing a Trainium2 kernel written in Bass

```python
import jax, jax.numpy as jnp
from jax import lax
import numpy as np

D_MODEL = 1024
BATCH = 1
SEQ = 1024
DEPTH = 2
DEC_BATCH = 8
DEC_SEQ = 8
PAST_LEN = 512
PAGE_SIZE = 128

N_MIXERS = 2
N_GDN = (DEPTH + 1) // 2
N_NSA = DEPTH // 2
GDN_HEADS = 8
GDN_DK = 128
GDN_DV = 128
GDN_CONV = 4
GDN_CHUNK = 64
GDN_QKV = GDN_HEADS * (2 * GDN_DK + GDN_DV)
GDN_IN = GDN_QKV + GDN_HEADS * GDN_DV + 2 * GDN_HEADS
NSA_HEADS = 16
NSA_KV_GROUPS = 2
NSA_HPG = NSA_HEADS // NSA_KV_GROUPS
NSA_DH = 64
NSA_KV_DIM = NSA_KV_GROUPS * NSA_DH
CMP_LEN = 32
CMP_STRIDE = 16
CMP_HID = 256
SEL_BLOCK = 64
SEL_TOP = 16
WINDOW = 512
Q_BLOCK = 128
NSA_IN = NSA_HEADS * NSA_DH + 6 * NSA_KV_DIM + 3 * NSA_HEADS
D_FF = ((-(-8 * D_MODEL // 3) + 255) // 256) * 256
RMS_EPS = 1e-6
L2_EPS = 1e-6
NEG_BIG = -1e30

kernel_name = 'hybrid_gdn_nsa_decoder_step'

def rmsnorm(x, w):
    xf = x.astype(jnp.float32)
    y = xf * lax.rsqrt(jnp.mean(xf * xf, axis=-1, keepdims=True) + RMS_EPS)
    return (y * w.astype(jnp.float32)).astype(x.dtype)

def l2norm(x):
    xf = x.astype(jnp.float32)
    return xf * lax.rsqrt(jnp.sum(xf * xf, axis=-1, keepdims=True) + L2_EPS)

def masked_softmax(s, mask):
    p = jax.nn.softmax(jnp.where(mask, s, NEG_BIG), axis=-1)
    return jnp.where(mask, p, 0.0)

def swiglu_ffn(x, w_in, w_out):
    g, u = jnp.split(x @ w_in, 2, axis=-1)
    return (jax.nn.silu(g) * u) @ w_out

def causal_short_conv(x, buf, w):
    xp = jnp.concatenate([buf, x], axis=1)
    T = x.shape[1]
    y = xp[:, 0:T] * w[0]
    for i in range(1, GDN_CONV):
        y = y + xp[:, i:i + T] * w[i]
    return jax.nn.silu(y), xp[:, T:]

def gated_delta_chunked(q, k, v, log_a, beta, S0, chunk):
    B, T, H, dk = q.shape
    dv = v.shape[-1]
    n = T // chunk

    def to_chunks(t):
        t = t.reshape((B, n, chunk, H) + t.shape[3:])
        return jnp.moveaxis(t, (1, 3), (0, 2))

    tri = jnp.tril(jnp.ones((chunk, chunk), bool))
    strict = jnp.tril(jnp.ones((chunk, chunk), bool), -1)
    eye = jnp.eye(chunk, dtype=jnp.float32)

    def step(S, inp):
        qc, kc, vc, gc, bc = inp
        G = jnp.cumsum(gc, axis=-1)
        decay = jnp.exp(jnp.where(tri, G[..., :, None] - G[..., None, :], -jnp.inf))
        lmat = jnp.where(strict, bc[..., :, None] * jnp.einsum('bhik,bhjk->bhij', kc, kc) * decay, 0.0)
        eg = jnp.exp(G)
        rhs = bc[..., None] * (vc - eg[..., None] * jnp.einsum('bhck,bhkv->bhcv', kc, S))
        u = lax.linalg.triangular_solve(eye + lmat, rhs, left_side=True, lower=True, unit_diagonal=True)
        o = eg[..., None] * jnp.einsum('bhck,bhkv->bhcv', qc, S) + jnp.einsum(
            'bhij,bhjv->bhiv', jnp.einsum('bhik,bhjk->bhij', qc, kc) * decay, u)
        tail = jnp.exp(G[..., -1:] - G)
        S_new = jnp.exp(G[..., -1])[..., None, None] * S + jnp.einsum('bhck,bhcv->bhkv', kc * tail[..., None], u)
        return S_new, o

    S, o = lax.scan(step, S0, (to_chunks(q), to_chunks(k), to_chunks(v), to_chunks(log_a), to_chunks(beta)))
    o = jnp.moveaxis(o, (0, 2), (1, 3)).reshape(B, T, H, dv)
    return o, S

def gdn_mixer(x, S0, conv_buf, chunk, w_in, conv_w, A_log, dt_bias, norm_w, w_out):
    B, T, _ = x.shape
    h = x @ w_in
    z_end = GDN_QKV + GDN_HEADS * GDN_DV
    qkv, z, b, a = jnp.split(h, [GDN_QKV, z_end, z_end + GDN_HEADS], axis=-1)
    qkv, new_buf = causal_short_conv(qkv, conv_buf, conv_w)
    q, k, v = jnp.split(qkv, [GDN_HEADS * GDN_DK, 2 * GDN_HEADS * GDN_DK], axis=-1)
    q = l2norm(q.reshape(B, T, GDN_HEADS, GDN_DK)) * GDN_DK ** -0.5
    k = l2norm(k.reshape(B, T, GDN_HEADS, GDN_DK))
    v = v.reshape(B, T, GDN_HEADS, GDN_DV).astype(jnp.float32)
    beta = jax.nn.sigmoid(b.astype(jnp.float32))
    log_a = -jnp.exp(A_log.astype(jnp.float32)) * jax.nn.softplus(a.astype(jnp.float32) + dt_bias.astype(jnp.float32))
    o, S = gated_delta_chunked(q, k, v, log_a, beta, S0.astype(jnp.float32), chunk)
    o = rmsnorm(o, norm_w) * jax.nn.silu(z.reshape(B, T, GDN_HEADS, GDN_DV).astype(jnp.float32))
    o = o.reshape(B, T, GDN_HEADS * GDN_DV).astype(x.dtype) @ w_out
    return o, S.astype(S0.dtype), new_buf

def nsa_project(x, w_in):
    B, T, _ = x.shape
    h = x @ w_in
    qd = NSA_HEADS * NSA_DH
    q = h[..., :qd].reshape(B, T, NSA_HEADS, NSA_DH) * NSA_DH ** -0.5
    kv = h[..., qd:qd + 4 * NSA_KV_DIM].reshape(B, T, 4, NSA_KV_GROUPS, NSA_DH)
    win = h[..., qd + 4 * NSA_KV_DIM:qd + 6 * NSA_KV_DIM].reshape(B, T, 2, NSA_KV_GROUPS, NSA_DH)
    gates = jax.nn.sigmoid(h[..., qd + 6 * NSA_KV_DIM:])
    return q, kv, win, gates

def compress_blocks(kv, pe, w1, w2):
    B, L = kv.shape[:2]
    n = (L - CMP_LEN) // CMP_STRIDE + 1
    idx = jnp.arange(n)[:, None] * CMP_STRIDE + jnp.arange(CMP_LEN)[None, :]
    blk = kv[:, idx] + pe[:, None, :]
    blk = jnp.moveaxis(blk, 3, 2).reshape(B, n, NSA_KV_GROUPS, CMP_LEN * NSA_DH)
    return jax.nn.silu(blk @ w1) @ w2

def selection_blocks(k):
    B, L = k.shape[:2]
    n_sel = -(-L // SEL_BLOCK)
    k = jnp.pad(k, ((0, 0), (0, n_sel * SEL_BLOCK - L), (0, 0), (0, 0)))
    return jnp.transpose(k.reshape(B, n_sel, SEL_BLOCK, NSA_KV_GROUPS, NSA_DH), (0, 3, 1, 2, 4))

def cmp_to_sel_overlap(n_cmp, n_sel):
    cs = jnp.arange(n_cmp)[:, None] * CMP_STRIDE
    ss = jnp.arange(n_sel)[None, :] * SEL_BLOCK
    return ((cs < ss + SEL_BLOCK) & (cs + CMP_LEN > ss)).astype(jnp.float32)

def branch_keys(kv_rows, pe_k, pe_v, w1k, w2k, w1v, w2v):
    kc = compress_blocks(kv_rows[:, :, 0], pe_k, w1k, w2k)
    vc = compress_blocks(kv_rows[:, :, 1], pe_v, w1v, w2v)
    k_sel = selection_blocks(kv_rows[:, :, 2])
    v_sel = selection_blocks(kv_rows[:, :, 3])
    overlap = cmp_to_sel_overlap(kc.shape[1], k_sel.shape[2])
    return kc, vc, k_sel, v_sel, overlap

def nsa_attend(q, q_pos, kc, vc, k_sel, v_sel, overlap, k_win, v_win, win_pos, gates):
    B, Tq = q.shape[:2]
    qg = q.reshape(B, Tq, NSA_KV_GROUPS, NSA_HPG, NSA_DH)
    cmp_end = jnp.arange(kc.shape[1]) * CMP_STRIDE + CMP_LEN - 1
    m_c = cmp_end[None, :] <= q_pos[:, None]
    s_c = jnp.einsum('bqghd,bngd->bghqn', qg, kc).astype(jnp.float32)
    p_c = masked_softmax(s_c, m_c)
    o_c = jnp.einsum('bghqn,bngd->bqghd', p_c.astype(vc.dtype), vc)
    n_sel = k_sel.shape[2]
    imp = jnp.einsum('bghqn,nj->bgqj', p_c, overlap)
    cur = q_pos // SEL_BLOCK
    j = jnp.arange(n_sel)[None, :]
    forced = (j == 0) | (j == cur[:, None]) | (j == cur[:, None] - 1)
    score = jnp.where(j > cur[:, None], -jnp.inf, jnp.where(forced, jnp.inf, imp))
    _, idx = lax.top_k(score, min(SEL_TOP, n_sel))
    n_top = idx.shape[-1]
    b_ix = jnp.arange(B)[:, None, None, None]
    g_ix = jnp.arange(NSA_KV_GROUPS)[None, :, None, None]
    ks = k_sel[b_ix, g_ix, idx].reshape(B, NSA_KV_GROUPS, Tq, n_top * SEL_BLOCK, NSA_DH)
    vs = v_sel[b_ix, g_ix, idx].reshape(B, NSA_KV_GROUPS, Tq, n_top * SEL_BLOCK, NSA_DH)
    pos = (idx[..., None] * SEL_BLOCK + jnp.arange(SEL_BLOCK)).reshape(B, NSA_KV_GROUPS, Tq, n_top * SEL_BLOCK)
    m_s = (pos <= q_pos[:, None])[:, :, None]
    s_s = jnp.einsum('bqghd,bgqkd->bghqk', qg, ks).astype(jnp.float32)
    p_s = masked_softmax(s_s, m_s)
    o_s = jnp.einsum('bghqk,bgqkd->bqghd', p_s.astype(vs.dtype), vs)
    m_w = (win_pos[None, :] <= q_pos[:, None]) & (win_pos[None, :] >= q_pos[:, None] - WINDOW) & (win_pos[None, :] >= 0)
    s_w = jnp.einsum('bqghd,bkgd->bghqk', qg, k_win).astype(jnp.float32)
    p_w = masked_softmax(s_w, m_w)
    o_w = jnp.einsum('bghqk,bkgd->bqghd', p_w.astype(v_win.dtype), v_win)
    g = gates.reshape(B, Tq, NSA_KV_GROUPS, NSA_HPG, 3)
    o = g[..., 0:1] * o_c + g[..., 1:2] * o_s + g[..., 2:3] * o_w
    return o.reshape(B, Tq, NSA_HEADS * NSA_DH)

def nsa_prompt(x, win_buf_len, w_in, pe_k, pe_v, w1k, w2k, w1v, w2v, w_out):
    B, T, _ = x.shape
    q, kv_rows, win_rows, gates = nsa_project(x, w_in)
    kc, vc, k_sel, v_sel, overlap = branch_keys(kv_rows, pe_k, pe_v, w1k, w2k, w1v, w2v)
    zpad = jnp.zeros((B, WINDOW, NSA_KV_GROUPS, NSA_DH), x.dtype)
    kw_pad = jnp.concatenate([zpad, win_rows[:, :, 0]], axis=1)
    vw_pad = jnp.concatenate([zpad, win_rows[:, :, 1]], axis=1)
    nb = T // Q_BLOCK
    qb = jnp.moveaxis(q.reshape(B, nb, Q_BLOCK, NSA_HEADS, NSA_DH), 1, 0)
    gb = jnp.moveaxis(gates.reshape(B, nb, Q_BLOCK, 3 * NSA_HEADS), 1, 0)

    def block(inp):
        qi, gi, i = inp
        start = i * Q_BLOCK
        q_pos = start + jnp.arange(Q_BLOCK)
        kw = lax.dynamic_slice_in_dim(kw_pad, start, WINDOW + Q_BLOCK, axis=1)
        vw = lax.dynamic_slice_in_dim(vw_pad, start, WINDOW + Q_BLOCK, axis=1)
        win_pos = start - WINDOW + jnp.arange(WINDOW + Q_BLOCK)
        return nsa_attend(qi, q_pos, kc, vc, k_sel, v_sel, overlap, kw, vw, win_pos, gi)

    o = lax.map(block, (qb, gb, jnp.arange(nb)))
    o = jnp.moveaxis(o, 0, 1).reshape(B, T, NSA_HEADS * NSA_DH) @ w_out
    wbuf = jnp.concatenate([jnp.zeros((B, win_buf_len, 2, NSA_KV_GROUPS, NSA_DH), x.dtype), win_rows], axis=1)[:, T:]
    return o, kv_rows, wbuf

def nsa_sample(x, kv_pool, win_cache, page_table, w_in, pe_k, pe_v, w1k, w2k, w1v, w2v, w_out):
    B, T, _ = x.shape
    q, kv_new, win_new, gates = nsa_project(x, w_in)
    past = kv_pool[page_table]
    past = past.reshape((B, -1) + past.shape[3:])
    past_len = past.shape[1]
    kv_all = jnp.concatenate([past, kv_new], axis=1)
    kc, vc, k_sel, v_sel, overlap = branch_keys(kv_all, pe_k, pe_v, w1k, w2k, w1v, w2v)
    win_all = jnp.concatenate([win_cache, win_new], axis=1)
    win_buf_len = win_cache.shape[1]
    win_pos = past_len - win_buf_len + jnp.arange(win_buf_len + T)
    q_pos = past_len + jnp.arange(T)
    o = nsa_attend(q, q_pos, kc, vc, k_sel, v_sel, overlap, win_all[:, :, 0], win_all[:, :, 1], win_pos, gates)
    return o @ w_out, kv_new, win_all[:, T:]

def setup_inputs(seed: int = 0) -> dict:
    key = jax.random.key(seed)
    ks = jax.random.split(key, 32)
    f32 = jnp.float32
    n_pages = PAST_LEN // PAGE_SIZE
    n_phys = (DEC_BATCH * n_pages * 5) // 4
    win_buf = min(WINDOW, PAST_LEN)

    def nrm(k, shape, scale):
        return jax.random.normal(k, shape, f32) * scale

    dt = jnp.exp(jax.random.uniform(ks[10], (N_GDN, GDN_HEADS), f32, np.log(1e-3), np.log(1e-1)))
    page_table = jax.random.permutation(ks[6], n_phys)[:DEC_BATCH * n_pages].reshape(DEC_BATCH, n_pages).astype(jnp.int32)
    return {
        'x_prompt': nrm(ks[0], (BATCH, SEQ, D_MODEL), 1.0),
        'x_sample': nrm(ks[1], (DEC_BATCH, DEC_SEQ, D_MODEL), 1.0),
        'cache_nsa_kv': nrm(ks[2], (N_NSA, n_phys, PAGE_SIZE, 4, NSA_KV_GROUPS, NSA_DH), 1.0),
        'cache_nsa_win': nrm(ks[3], (N_NSA, DEC_BATCH, win_buf, 2, NSA_KV_GROUPS, NSA_DH), 1.0),
        'state_gdn': nrm(ks[4], (N_GDN, DEC_BATCH, GDN_HEADS, GDN_DK, GDN_DV), 0.1),
        'state_gdn_conv': nrm(ks[5], (N_GDN, DEC_BATCH, GDN_CONV - 1, GDN_QKV), 1.0),
        'page_table': page_table,
        'norm1_w': 1.0 + nrm(ks[7], (DEPTH, D_MODEL), 0.02),
        'norm2_w': 1.0 + nrm(ks[8], (DEPTH, D_MODEL), 0.02),
        'final_norm_w': 1.0 + nrm(ks[9], (D_MODEL,), 0.02),
        'gdn_w_in': nrm(ks[11], (N_GDN, D_MODEL, GDN_IN), D_MODEL ** -0.5),
        'gdn_conv_w': nrm(ks[12], (N_GDN, GDN_CONV, GDN_QKV), GDN_CONV ** -0.5),
        'gdn_A_log': jnp.log(jax.random.uniform(ks[13], (N_GDN, GDN_HEADS), f32, 1.0, 16.0)),
        'gdn_dt_bias': dt + jnp.log(-jnp.expm1(-dt)),
        'gdn_norm_w': 1.0 + nrm(ks[14], (N_GDN, GDN_DV), 0.02),
        'gdn_w_out': nrm(ks[15], (N_GDN, GDN_HEADS * GDN_DV, D_MODEL), (GDN_HEADS * GDN_DV) ** -0.5),
        'nsa_w_in': nrm(ks[16], (N_NSA, D_MODEL, NSA_IN), D_MODEL ** -0.5),
        'nsa_pe_k': nrm(ks[17], (N_NSA, CMP_LEN, NSA_DH), 0.1),
        'nsa_pe_v': nrm(ks[18], (N_NSA, CMP_LEN, NSA_DH), 0.1),
        'nsa_cmp_w1_k': nrm(ks[19], (N_NSA, CMP_LEN * NSA_DH, CMP_HID), (CMP_LEN * NSA_DH) ** -0.5),
        'nsa_cmp_w2_k': nrm(ks[20], (N_NSA, CMP_HID, NSA_DH), CMP_HID ** -0.5),
        'nsa_cmp_w1_v': nrm(ks[21], (N_NSA, CMP_LEN * NSA_DH, CMP_HID), (CMP_LEN * NSA_DH) ** -0.5),
        'nsa_cmp_w2_v': nrm(ks[22], (N_NSA, CMP_HID, NSA_DH), CMP_HID ** -0.5),
        'nsa_w_out': nrm(ks[23], (N_NSA, NSA_HEADS * NSA_DH, D_MODEL), (NSA_HEADS * NSA_DH) ** -0.5),
        'ffn_w_in': nrm(ks[24], (DEPTH, D_MODEL, 2 * D_FF), D_MODEL ** -0.5),
        'ffn_w_out': nrm(ks[25], (DEPTH, D_FF, D_MODEL), D_FF ** -0.5),
    }

def reference(x_prompt, x_sample, cache_nsa_kv, cache_nsa_win, state_gdn, state_gdn_conv, page_table,
              norm1_w, norm2_w, final_norm_w, gdn_w_in, gdn_conv_w, gdn_A_log, gdn_dt_bias, gdn_norm_w, gdn_w_out,
              nsa_w_in, nsa_pe_k, nsa_pe_v, nsa_cmp_w1_k, nsa_cmp_w2_k, nsa_cmp_w1_v, nsa_cmp_w2_v, nsa_w_out,
              ffn_w_in, ffn_w_out):
    xp, xs = x_prompt, x_sample
    bp, tp = xp.shape[:2]
    win_buf_len = cache_nsa_win.shape[2]
    kv_p, kv_s, win_p, win_s = [], [], [], []
    gs_p, gs_s, gc_p, gc_s = [], [], [], []
    for i in range(DEPTH):
        li = i // N_MIXERS
        hp = rmsnorm(xp, norm1_w[i])
        hs = rmsnorm(xs, norm1_w[i])
        if i % N_MIXERS == 0:
            gw = (gdn_w_in[li], gdn_conv_w[li], gdn_A_log[li], gdn_dt_bias[li], gdn_norm_w[li], gdn_w_out[li])
            s0 = jnp.zeros((bp, GDN_HEADS, GDN_DK, GDN_DV), xp.dtype)
            c0 = jnp.zeros((bp, GDN_CONV - 1, GDN_QKV), xp.dtype)
            mp, sp, cp = gdn_mixer(hp, s0, c0, min(GDN_CHUNK, tp), *gw)
            ms, ss, cs = gdn_mixer(hs, state_gdn[li], state_gdn_conv[li], xs.shape[1], *gw)
            gs_p.append(sp)
            gs_s.append(ss)
            gc_p.append(cp)
            gc_s.append(cs)
        else:
            nw = (nsa_w_in[li], nsa_pe_k[li], nsa_pe_v[li], nsa_cmp_w1_k[li], nsa_cmp_w2_k[li],
                  nsa_cmp_w1_v[li], nsa_cmp_w2_v[li], nsa_w_out[li])
            mp, kp, wp = nsa_prompt(hp, win_buf_len, *nw)
            ms, ksm, wsm = nsa_sample(hs, cache_nsa_kv[li], cache_nsa_win[li], page_table, *nw)
            kv_p.append(kp)
            kv_s.append(ksm)
            win_p.append(wp)
            win_s.append(wsm)
        xp = xp + mp
        xs = xs + ms
        xp = xp + swiglu_ffn(rmsnorm(xp, norm2_w[i]), ffn_w_in[i], ffn_w_out[i])
        xs = xs + swiglu_ffn(rmsnorm(xs, norm2_w[i]), ffn_w_in[i], ffn_w_out[i])
    y_prompt = rmsnorm(xp, final_norm_w)
    y_sample = rmsnorm(xs, final_norm_w)
    return (y_prompt, y_sample, jnp.stack(kv_p), jnp.stack(kv_s), jnp.stack(win_p), jnp.stack(win_s),
            jnp.stack(gs_p), jnp.stack(gs_s), jnp.stack(gc_p), jnp.stack(gc_s))


_drawn_inputs = setup_inputs


def setup_inputs(seed=0):
    import zlib

    import numpy as np

    out = dict(_drawn_inputs(seed))
    spreads = {}
    factors = {'norm2_w': 3.071,
     'final_norm_w': 8.115,
     'gdn_norm_w': 4.71,
     'nsa_pe_k': 64.0,
     'cache_nsa_kv': 4.331,
     'nsa_pe_v': 8.0,
     'nsa_cmp_w1_k': 8.0,
     'nsa_cmp_w2_k': 8.0,
     'nsa_cmp_w1_v': 3.099}
    for name, (base, spread) in spreads.items():
        noise = np.random.default_rng([zlib.crc32(name.encode()), seed]).standard_normal(out[name].shape)
        drawn = base * np.exp(spread * noise) if base else spread * noise
        out[name] = __import__('jax').numpy.asarray(drawn.astype(out[name].dtype))
    for name, factor in factors.items():
        out[name] = (out[name] * factor).astype(out[name].dtype)
    return out
```

```python
from contextlib import ExitStack

import numpy as np

import concourse.bass as bass
from concourse import mybir

F32 = mybir.dt.float32
I32 = mybir.dt.int32
ALU = mybir.AluOpType
ACT = mybir.ActivationFunctionType
AX = mybir.AxisListType
ds = bass.ds

P = 128
D = 1024
KD = D // P
TP = 1024
NB, TS = 8, 8
NS = NB * TS
NT = TP + NS
HG = 8
NC = TP // P
QKV = 3 * HG * P
PAST = 512
DFF = 2816
KF = DFF // P
NH = 16
DH = 64
NPG = 4
NPHYS = 40
NCMP = 63
NCMPS = 31
EPS = 1e-6
NEG = -1e30
CH = [(0, 512), (512, 512), (1024, 64)]

CONST = {}


def const_table():
    cols = []

    def add(name, a):
        a = np.asarray(a, np.float32)
        full = np.zeros((P, a.shape[1]), np.float32)
        full[:a.shape[0]] = a
        CONST[name] = (sum(c.shape[1] for c in cols), a.shape[1])
        cols.append(full)

    i = np.arange(P)[:, None]
    j = np.arange(P)[None, :]
    add("ident", i == j)
    add("ones", np.ones((P, P)))
    add("upper", i <= j)
    add("strict", i > j)
    i8, j8 = i[:NS], j[:, :NS]
    same = (i8 // TS) == (j8 // TS)
    add("upper_s", same & (i8 <= j8))
    add("strict_s", same & (i8 > j8))
    add("same_s", same)
    add("batch_s", (i8 // TS) == np.arange(NB)[None, :])
    for s in (1, 2, 4, 8, 16, 32, 64):
        m = (i // (2 * s) == j // (2 * s)) & (i // s % 2 == 1) & (j // s % 2 == 0)
        add(f"mt{s}", m.T)
        if s == 1:
            add("m1", m)
    add("causal_add", np.where(j <= i, 0, NEG))
    add("far_add", np.where(j >= i, 0, NEG))
    n = np.arange(64)[None, :]
    for qt in range(TP // P):
        add(f"cmp_add{qt}", np.where(16 * n + 31 <= qt * P + i, 0, NEG)[:, :NCMP])
    add("row_has_cmp", i >= 31)
    t = i % TS
    k8 = np.arange(TS)[None, :]
    add("s_new_add", np.where(k8 <= t, 0, NEG))
    add("s_far_add", np.where(k8 >= t, 0, NEG))
    add("eps", np.full((P, 1), EPS))
    add("eps_dk", np.full((P, 1), EPS * P))
    add("one", np.ones((P, 1)))
    return np.concatenate(cols, 1)


const_table()
NCONST = sum(w for _, w in CONST.values())


class Core:
    pass


def open_core(nc, ctx, io):
    c = Core()
    c.nc, c.io = nc, io
    c.n = 0
    c.open_sems = []

    def sb(name, cols):
        return ctx.enter_context(nc.sbuf_tensor(name, [P, cols], F32))

    c.ct = sb("consts", NCONST)
    c.xT = sb("xT", KD * NT)[:, :].rearrange("p (k t) -> p k t", k=KD)
    c.xn = sb("xn", KD * NT)[:, :].rearrange("p (k t) -> p k t", k=KD)
    c.xTf = c.xT.rearrange("p k t -> p (k t)")
    c.xnf = c.xn.rearrange("p k t -> p (k t)")
    c.normw = sb("normw", P)[:, :]
    c.convw = sb("convw", 96)[:, :]
    c.W = 32900
    c.work = sb("work", c.W)
    c.tail = c.W - 24 * 24 - 24 * 27 - 54 * HG
    o = c.tail
    c.convT = c.work[:, o:o + 576].rearrange("p (k n) -> p k n", k=24)
    c.newconv = c.work[:, o + 576:o + 576 + 648]
    c.par = c.work[:, o + 1224:o + 1224 + 54 * HG]
    c.ps = ctx.enter_context(nc.psum_tensor("ps", [P, 4096], F32))
    c.pages = ctx.enter_context(nc.sbuf_tensor("pages", [1, NB * NPG], I32))
    c.at = 0
    return c


def const(c, name):
    o, w = CONST[name]
    return c.ct[:, o:o + w]


def take(c, cols):
    a = c.work[:, c.at:c.at + cols]
    c.at += cols
    assert c.at <= c.W, c.at
    return a


def bank(c, b, n=1):
    return c.ps[:, 512 * b:512 * (b + n)]


def proj_main(c, slot):
    return c.ps[:, 1536 * slot:1536 * slot + 1024]


def proj_psum(c, slot):
    o = 1536 * slot
    return [c.ps[:, o:o + 512], c.ps[:, o + 512:o + 1024], c.ps[:, o + 1024:o + 1024 + NS]]


def sems(nc, ctx, c, *names):
    c.n += 1
    new = [nc.alloc_semaphore(f"{n}_{c.n}") for n in names]
    c.open_sems += new
    return new


def recycle_semaphores(c):
    c.nc.all_engine_barrier()
    c.nc.clear_and_free_semaphores(c.open_sems)
    c.nc.all_engine_barrier()
    c.open_sems = []


def load_stage(c):
    nc, io = c.nc, c.io
    c.at = 0
    rows = take(c, 9 * D).rearrange("p (t d) -> p t d", t=9)
    cv = take(c, QKV)
    vec = take(c, 4 * P)
    with ExitStack() as ctx:
        ld, ldc, tr, ev, zero, cpy = sems(nc, ctx, c, "loaded", "consts_loaded", "turned", "evacuated", "zeroed", "zero2")
        with nc.Block() as block:
            @block.sync
            def _(sp):
                sp.dma_start(c.ct[:, :], io["consts"]).then_inc(ldc, 16)
                sp.dma_start(rows[:, 0:8, :], io["x_prompt"][0].rearrange("(t p) d -> p t d", p=P)).then_inc(ld, 16)
                sp.dma_start(rows[0:NS, 8, :], io["x_sample"].rearrange("b t d -> (b t) d")).then_inc(ld, 16)
                sp.dma_start(cv[0:24, :], io["state_gdn_conv"][0].rearrange("b r f -> (b r) f")).then_inc(ld, 16)
                sp.dma_start(c.pages[:, :], io["page_table"].rearrange("b (o n) -> o (b n)", o=1)).then_inc(ld, 16)
                sp.wait_ge(zero, 1)
                sp.dma_start(vec[0:16, 0:128], io["norm1_w"].rearrange("l (k p) -> (l k) p", p=P)).then_inc(ld, 16)
                sp.dma_start(vec[16:32, 0:128], io["norm2_w"].rearrange("l (k p) -> (l k) p", p=P)).then_inc(ld, 16)
                sp.dma_start(vec[32:40, 0:128], io["final_norm_w"].rearrange("(k p) -> k p", p=P)).then_inc(ld, 16)
                sp.dma_start(vec[40:41, 0:128], io["gdn_norm_w"]).then_inc(ld, 16)
                sp.dma_start(vec[0:96, 128:256], io["gdn_conv_w"][0].rearrange("r (k p) -> (r k) p", p=P)).then_inc(ld, 16)

            @block.gpsimd
            def _(pool):
                pool.memset(vec[:, :], 0.0).then_inc(zero, 1)

            jobs = [(rows[0:(P if t < 8 else NS), t, k * P:(k + 1) * P], c.xT[:, k, t * P:t * P + (P if t < 8 else NS)])
                    for t in range(9) for k in range(KD)]
            jobs += [(cv[0:24, k * P:(k + 1) * P], c.convT[:, k, :]) for k in range(24)]
            jobs += [(vec[:, 0:128], c.normw[:, :]), (vec[0:96, 128:256], c.convw[:, :])]

            @block.tensor
            def _(pe):
                pe.wait_ge(ldc, 16)
                pe.wait_ge(ld, 9 * 16)
                for n, (src, dst) in enumerate(jobs):
                    if n >= 8:
                        pe.wait_ge(ev, n - 7)
                    r = src.shape[0]
                    pe.transpose(bank(c, n % 8)[:, 0:r], src, const(c, "ident")[0:r, 0:r]).then_inc(tr, 1)

            @block.vector
            def _(dve):
                for n, (src, dst) in enumerate(jobs):
                    dve.wait_ge(tr, n + 1)
                    w = dst.shape[1]
                    dve.tensor_copy(dst, bank(c, n % 8)[:, 0:w]).then_inc(ev, 1)


def norm_stage(c, which, out, base):
    nc = c.nc
    c.at = base
    sq = take(c, 2 * NT).rearrange("p (s t) -> p s t", s=2)
    rt = take(c, NT)
    with ExitStack() as ctx:
        sqr, ss, root, inv, done = sems(nc, ctx, c, "squared", "summed", "rooted", "inverted", "normed")
        acc = proj_psum(c, 0)
        with nc.Block() as block:
            @block.scalar
            def _(act):
                for k in range(KD):
                    if k >= 2:
                        act.wait_ge(ss, k - 1)
                    act.activation(sq[:, k % 2, :], c.xT[:, k, :], ACT.Square).then_inc(sqr, 1)
                act.wait_ge(ss, KD)
                for (o, w), a in zip(CH, acc):
                    act.activation(rt[:, o:o + w], a, ACT.Sqrt, bias=const(c, "eps"), scale=1.0 / D).then_inc(root, 1)

            @block.tensor
            def _(pe):
                for k in range(KD):
                    pe.wait_ge(sqr, k + 1)
                    for n, ((o, w), a) in enumerate(zip(CH, acc)):
                        mm = pe.matmul(a, const(c, "ones"), sq[:, k % 2, o:o + w], start=(k == 0), stop=(k == KD - 1))
                    mm.then_inc(ss, 1)

            @block.vector
            def _(dve):
                dve.wait_ge(root, 3)
                dve.reciprocal(rt[:, :], rt[:, :]).then_inc(inv, 1)
                dve.wait_ge(inv, 1)
                for k in range(KD):
                    dve.scalar_tensor_tensor(out=out[:, k, :], in0=c.xT[:, k, :], scalar=c.normw[:, which * 8 + k:which * 8 + k + 1],
                                             in1=rt[:, :], op0=ALU.mult, op1=ALU.mult).then_inc(done, 1)


def mm_tile(pe, dst, w, rhs, nk):
    for (o, n), a in zip(CH, dst):
        for k in range(nk):
            mm = pe.matmul(a, w[:, k, :], rhs[:, k, o:o + n], start=(k == 0), stop=(k == nk - 1))
    return mm


def proj_stage(c, nk, tiles, src, rhs, wbuf, evac):
    nc = c.nc
    with ExitStack() as ctx:
        w0, w1, mm0, mm1, free0, free1 = sems(
            nc, ctx, c, "w0_loaded", "w1_loaded", "tile0_done", "tile1_done", "tile0_taken", "tile1_taken")
        wl, mmd, free = (w0, w1), (mm0, mm1), (free0, free1)
        npc = len(src(0, 0))
        with nc.Block() as block:
            @block.sync
            def _(sp):
                for j in range(2):
                    for dst, s in src(j, j):
                        sp.dma_start(dst, s).then_inc(wl[j], 16)
                with sp.Fori(0, tiles // 2 - 1) as i:
                    for j in range(2):
                        sp.wait_ge(mmd[j], i + 1)
                        for dst, s in src(2 * i + 2 + j, j):
                            sp.dma_start(dst, s).then_inc(wl[j], 16)

            @block.tensor
            def _(pe):
                with pe.Fori(0, tiles // 2) as i:
                    for j in range(2):
                        pe.wait_ge(wl[j], (i + 1) * (16 * npc))
                        pe.wait_ge(free[j], i * 2 + 1)
                        mm_tile(pe, proj_psum(c, j), wbuf[j], rhs, nk).then_inc(mmd[j], 1)

            @block.vector
            def _(dve):
                for j in range(2):
                    dve.sem_inc(free[j], 1)
                with dve.Fori(0, tiles // 2) as i:
                    for j in range(2):
                        dve.wait_ge(mmd[j], i + 1)
                        for ins in evac(dve, i * 2 + j, proj_main(c, j), proj_psum(c, j)[2]):
                            ins.then_inc(free[j], 1)


def out_stage(c, nk, src, rhs, wbuf):
    def evac(dve, m, main, last):
        x = c.xTf[:, ds(m * NT, TP)]
        yield dve.tensor_tensor(x, x, main, ALU.add)
        x = c.xTf[:, ds(m * NT + TP, NS)]
        yield dve.tensor_tensor(x, x, last, ALU.add)

    proj_stage(c, nk, KD, src, rhs, wbuf, evac)


def ffn_stages(c, layer):
    nc, io = c.nc, c.io
    c.at = 0
    hid = take(c, KF * NT)
    hid3 = hid.rearrange("p (k t) -> p k t", k=KF)
    hbase = c.at
    norm_stage(c, 2 + layer, c.xn, 0)
    c.at = hbase
    sg = take(c, NT)
    wb = [take(c, KD * P).rearrange("p (k f) -> p k f", k=KD) for _ in range(4)]
    w_in = io["ffn_w_in"][layer].rearrange("(k p) f -> p k f", p=P)
    w_out = io["ffn_w_out"][layer].rearrange("(k p) f -> p k f", p=P)
    with ExitStack() as ctx:
        names = [f"{a}{j}" for a in ("gate_w_loaded", "up_w_loaded") for j in range(2)]
        gw0, gw1, uw0, uw1 = sems(nc, ctx, c, *names)
        gmm, umm, silu, prod = sems(nc, ctx, c, "gate_done", "up_done", "silu_done", "hidden_done")
        gw, uw = (gw0, gw1), (uw0, uw1)
        with nc.Block() as block:
            @block.sync
            def _(sp):
                for j in range(2):
                    sp.dma_start(wb[2 * j], w_in[:, :, j * P:(j + 1) * P]).then_inc(gw[j], 16)
                    sp.dma_start(wb[2 * j + 1], w_in[:, :, DFF + j * P:DFF + (j + 1) * P]).then_inc(uw[j], 16)
                with sp.Fori(0, KF // 2 - 1) as i:
                    for j in range(2):
                        sp.wait_ge(umm, i * 2 + j + 1)
                        o = (i + 1) * (2 * P) + j * P
                        sp.dma_start(wb[2 * j], w_in[:, :, ds(o, P)]).then_inc(gw[j], 16)
                        sp.dma_start(wb[2 * j + 1], w_in[:, :, ds(o + DFF, P)]).then_inc(uw[j], 16)

            @block.tensor
            def _(pe):
                with pe.Fori(0, KF // 2) as i:
                    for j in range(2):
                        pe.wait_ge(gw[j], (i + 1) * 16)
                        pe.wait_ge(silu, i * 4 + 2 * j + 1)
                        mm_tile(pe, proj_psum(c, 0), wb[2 * j], c.xn, KD).then_inc(gmm, 1)
                        pe.wait_ge(uw[j], (i + 1) * 16)
                        pe.wait_ge(prod, i * 4 + 2 * j + 1)
                        mm_tile(pe, proj_psum(c, 1), wb[2 * j + 1], c.xn, KD).then_inc(umm, 1)

            @block.scalar
            def _(act):
                act.sem_inc(silu, 1)
                with act.Fori(0, KF // 2) as i:
                    for j in range(2):
                        act.wait_ge(gmm, i * 2 + j + 1)
                        act.wait_ge(prod, i * 4 + 2 * j + 1)
                        act.activation(sg[:, 0:TP], proj_main(c, 0), ACT.Silu).then_inc(silu, 1)
                        act.activation(sg[:, TP:NT], proj_psum(c, 0)[2], ACT.Silu).then_inc(silu, 1)

            @block.vector
            def _(dve):
                dve.sem_inc(prod, 1)
                with dve.Fori(0, KF // 2) as i:
                    for j in range(2):
                        dve.wait_ge(umm, i * 2 + j + 1)
                        dve.wait_ge(silu, i * 4 + 2 * j + 3)
                        o = (i * 2 + j) * NT
                        dve.tensor_tensor(hid[:, ds(o, TP)], sg[:, 0:TP], proj_main(c, 1), ALU.mult).then_inc(prod, 1)
                        dve.tensor_tensor(hid[:, ds(o + TP, NS)], sg[:, TP:NT], proj_psum(c, 1)[2], ALU.mult).then_inc(prod, 1)
    flat = c.xnf
    wo = [flat[:, j * KF * P:(j + 1) * KF * P].rearrange("p (k f) -> p k f", k=KF) for j in range(2)]
    out_stage(c, KF, lambda m, j: [(wo[j], w_out[:, :, ds(m * P, P)])], hid3, wo)


BETA, NBETA, GCUM, TAIL, ETOT, LOGA = range(6)
NPAR = 6 * 9


def gate_stage(c):
    nc, io = c.nc, c.io
    c.at = 0
    wba = take(c, KD * 16).rearrange("p (k f) -> p k f", k=KD)
    row = take(c, 16)
    ba = take(c, 144)
    t1, t2, t3 = take(c, 72), take(c, 72), take(c, 72)
    rb = take(c, 16)
    gs, tot = take(c, 72), take(c, 72)
    par = c.par.rearrange("p (h q c) -> p q c h", h=HG, q=6)
    ba3 = ba.rearrange("p (c n) -> p c n", c=9)

    def v(a):
        return a.rearrange("p (c h) -> p c h", c=9)

    with ExitStack() as ctx:
        ld, z, pm, step, a1, pg = sems(nc, ctx, c, "gate_inputs", "zeroed", "products", "vector_step", "scalar_step", "sums")
        with nc.Block() as block:
            @block.sync
            def _(sp):
                sp.dma_start(wba, io["gdn_w_in"][0].rearrange("(k p) f -> p k f", p=P)[:, :, 4096:4112]).then_inc(ld, 16)
                sp.dma_start(row[0:1, 0:8], io["gdn_dt_bias"]).then_inc(ld, 16)
                sp.dma_start(row[0:1, 8:16], io["gdn_A_log"]).then_inc(ld, 16)

            @block.gpsimd
            def _(pool):
                pool.memset(ba, 0.0).then_inc(z, 1)
                pool.memset(gs, 0.0).then_inc(z, 1)
                pool.memset(tot, 0.0).then_inc(z, 1)

            @block.tensor
            def _(pe):
                pe.wait_ge(ld, 48)
                for t in range(9):
                    n = P if t < 8 else NS
                    for k in range(KD):
                        pe.matmul(bank(c, 0)[0:n, 16 * t:16 * t + 16], c.xn[:, k, t * P:t * P + n], wba[:, k, :],
                                  start=(k == 0), stop=(k == KD - 1))
                pe.matmul(bank(c, 1)[:, 0:16], const(c, "ones")[0:1, :], row[0:1, :], start=True, stop=True).then_inc(pm, 1)
                pe.wait_ge(step, 8)
                la, las = t3[:, 0:64], t3[0:NS, 64:72]
                pe.matmul(bank(c, 2)[:, 0:64], const(c, "upper"), la, start=True, stop=True)
                pe.matmul(bank(c, 3)[0:NS, 0:8], const(c, "upper_s")[0:NS, :], las, start=True, stop=True)
                pe.matmul(bank(c, 4)[:, 0:64], const(c, "ones"), la, start=True, stop=True)
                pe.matmul(bank(c, 5)[0:NS, 0:8], const(c, "same_s")[0:NS, :], las, start=True, stop=True).then_inc(pg, 1)

            @block.scalar
            def _(act):
                act.wait_ge(step, 4)
                act.activation(par[:, BETA], ba3[:, :, 0:8], ACT.Sigmoid).then_inc(a1, 1)
                act.activation(rb[:, 8:16], rb[:, 8:16], ACT.Exp).then_inc(a1, 1)
                act.activation(t2, t2, ACT.Exp, scale=-1.0).then_inc(a1, 1)
                act.wait_ge(a1, 3)
                act.activation(t2, t2, ACT.Ln, bias=const(c, "one")).then_inc(a1, 1)
                act.wait_ge(step, 11)
                act.activation(par[:, TAIL], v(gs), ACT.Exp).then_inc(a1, 1)
                act.activation(par[:, ETOT], v(tot), ACT.Exp).then_inc(a1, 1)

            @block.vector
            def _(dve):
                dve.wait_ge(z, 3)
                dve.wait_ge(pm, 1)
                dve.tensor_copy(ba[:, 0:128], bank(c, 0)[:, 0:128])
                dve.tensor_copy(ba[0:NS, 128:144], bank(c, 0)[0:NS, 128:144])
                dve.tensor_copy(rb, bank(c, 1)[:, 0:16]).then_inc(step, 1)
                dve.wait_ge(step, 1)
                dve.tensor_tensor(v(t1), ba3[:, :, 8:16], rb[:, 0:8].rearrange("p (o h) -> p o h", o=1).to_broadcast([P, 9, 8]),
                                  ALU.add).then_inc(step, 1)
                dve.wait_ge(step, 2)
                dve.tensor_scalar(t3, t1, -1.0, None, ALU.mult).then_inc(step, 1)
                dve.wait_ge(step, 3)
                dve.tensor_tensor(t2, t1, t3, ALU.max).then_inc(step, 1)
                dve.tensor_scalar(t1, t1, 0.0, None, ALU.max).then_inc(step, 1)
                dve.wait_ge(a1, 4)
                dve.wait_ge(step, 5)
                dve.tensor_scalar(par[:, NBETA], par[:, BETA], -1.0, None, ALU.mult).then_inc(step, 1)
                dve.tensor_tensor(t1, t1, t2, ALU.add).then_inc(step, 1)
                dve.wait_ge(step, 7)
                dve.scalar_tensor_tensor(out=v(t3), in0=v(t1), scalar=-1.0,
                                         in1=rb[:, 8:16].rearrange("p (o h) -> p o h", o=1).to_broadcast([P, 9, 8]),
                                         op0=ALU.mult, op1=ALU.mult).then_inc(step, 1)
                dve.wait_ge(pg, 1)
                dve.wait_ge(step, 8)
                dve.tensor_copy(par[:, LOGA], v(t3))
                dve.tensor_copy(gs[:, 0:64], bank(c, 2)[:, 0:64])
                dve.tensor_copy(gs[0:NS, 64:72], bank(c, 3)[0:NS, 0:8])
                dve.tensor_copy(tot[:, 0:64], bank(c, 4)[:, 0:64])
                dve.tensor_copy(tot[0:NS, 64:72], bank(c, 5)[0:NS, 0:8]).then_inc(step, 1)
                dve.wait_ge(step, 9)
                dve.tensor_copy(par[:, GCUM], v(gs)).then_inc(step, 1)
                dve.wait_ge(step, 10)
                dve.tensor_tensor(gs, tot, gs, ALU.subtract).then_inc(step, 1)
                dve.wait_ge(a1, 6)


def gdn_stage(c):
    nc, io = c.nc, c.io
    c.at = 0
    w = [take(c, KD * P).rearrange("p (k f) -> p k f", k=KD) for _ in range(4)]
    yT = take(c, HG * NT)
    qkvz = [take(c, NT) for _ in range(4)]
    cin = [take(c, 3 + TP + NB * (3 + TS)) for _ in range(2)]
    sq, rt = take(c, NT), take(c, NT)
    s0 = take(c, NB * P)
    sn = take(c, NB * P)
    um = take(c, NB * P)
    parh, st0, st1, us, kst, cw, eb = take(c, NPAR), take(c, P), take(c, P), take(c, P), take(c, NS), take(c, 12), take(c, NB)
    kt, bv = take(c, 9 * P), take(c, 9 * P)
    assert c.at <= c.tail, c.at
    eg, e1, e2, lt, ml, x, xt, pp = [c.xTf[:, n * NT:(n + 1) * NT] for n in range(8)]
    park = nc.dram_tensor("parked_residual", (P, KD * NT), F32).ap()
    kT, qT, vT, zT = qkvz[1], qkvz[0], qkvz[2], qkvz[3]
    st = [st0, st1]
    w_in = io["gdn_w_in"][0].rearrange("(k p) f -> p k f", p=P)
    A, B, C, Dp = 0, 1024, 2048, 3072

    def par(q, n, height):
        return parh[0:height, q * 9 + n:q * 9 + n + 1]

    GROUPS = [dict(n=8, r=P, o=0, c0=0, up="upper", lo="strict", lv=(2, 4, 8, 16, 32, 64)),
              dict(n=1, r=NS, o=TP, c0=8, up="upper_s", lo="strict_s", lv=(2, 4))]
    NLV = 8

    def blk(a, g, k, height=None):
        return a[0:(height or g["r"]), g["o"] + k * g["r"]:g["o"] + (k + 1) * g["r"]]

    def tok(a, g, k):
        return a[0:g["r"], (g["c0"] + k) * P:(g["c0"] + k + 1) * P]

    def ps(base, g, k, height=None, width=None):
        width = width or g["r"]
        return c.ps[0:(height or g["r"]), base + k * width:base + (k + 1) * width]

    def grp(a, g):
        return a[0:g["r"], g["o"]:g["o"] + g["n"] * g["r"]].rearrange("p (n f) -> p n f", n=g["n"])

    def psg(base, g):
        return c.ps[0:g["r"], base:base + g["n"] * g["r"]].rearrange("p (n f) -> p n f", n=g["n"])

    def mask(name, g):
        m = const(c, name)[0:g["r"], 0:g["r"]]
        return m.rearrange("p (o f) -> p o f", o=1).to_broadcast([g["r"], g["n"], g["r"]])

    def norm_acc():
        return [bank(c, 6), bank(c, 7), bank(c, 5)[:, 0:NS]]

    with ExitStack() as ctx:
        names = ["parked", "states_loaded", "states_stored", "state_out"] + [f"w{j}_loaded" for j in range(4)]
        (parked, s0l, sns, sto, *wl) = sems(nc, ctx, c, *names)
        (pj, pfree0, pfree1, hist, raw, conv, conved, sqd, ssd, rooted, normed, nconv) = sems(
            nc, ctx, c, "projected", "slot0_read", "slot1_read", "history_set", "raw_copied", "conv_done", "activated",
            "squared", "summed", "rooted", "normed", "conv_rows_kept")
        (p1, p2, p3, a1, v1, a2, v2, v3, mlr, pr, psr, yr, xr) = sems(
            nc, ctx, c, "turned_products", "query_key", "l_turned", "tail_keys", "differences", "decays", "l_and_scores",
            "x_begun", "l_masked", "p_product", "p_copied", "y_products", "x_updated")
        (ksr, rr, ur, usr, dsr, str_) = sems(nc, ctx, c, "key_state", "rhs_ready", "u_product", "u_copied", "state_product", "state_ready")
        (kss, kstc, kst2, rs, u2, us2, um2, o2, oc2, sn2) = sems(
            nc, ctx, c, "s_key_state", "s_copied", "s_turned", "s_rhs", "s_u", "s_u_copied", "s_u_spread", "s_out", "s_out_copied", "s_states")
        (oc, osq, oss, ort, yd, dc, pc) = sems(
            nc, ctx, c, "o_copied", "o_squared", "o_summed", "o_rooted", "y_done", "vector_chain", "params_copied")
        pfree = [pfree0, pfree1]
        with nc.Block() as block:
            @block.sync
            def _(sp):
                for s in (sto, sns):
                    sp.sem_inc(s, 1)
                sp.dma_start(park, c.xTf).then_inc(parked, 16)
                for j in range(4):
                    sp.dma_start(w[j], w_in[:, :, j * D:j * D + P]).then_inc(wl[j], 16)
                sp.dma_start(s0.rearrange("p (b v) -> p b v", b=NB), io["state_gdn"][0][:, 0].rearrange("b k v -> k b v")).then_inc(s0l, 16)
                sp.wait_ge(parked, 16)

                def head(i, more):
                    if more:
                        for j in range(4):
                            sp.wait_ge(pj, i * 4 + j + 1)
                            sp.dma_start(w[j], w_in[:, :, ds((i + 1) * P + j * D, P)]).then_inc(wl[j], 16)
                    sp.wait_ge(str_, i * 8 + 8)
                    sp.dma_start(io["out6"][0, 0][ds(i, 1)].rearrange("o k v -> k (o v)"), st[1]).then_inc(sto, 16)
                    sp.wait_ge(sn2, i + 1)
                    sp.dma_start(io["out7"][0][:, ds(i, 1)].rearrange("b o k v -> k (b o) v"),
                                 sn.rearrange("p (b v) -> p b v", b=NB)).then_inc(sns, 16)
                    if more:
                        sp.dma_start(s0.rearrange("p (b v) -> p b v", b=NB),
                                     io["state_gdn"][0][:, ds(i + 1, 1)].rearrange("b o k v -> k (b o) v")).then_inc(s0l, 16)

                with sp.Fori(0, HG - 1) as i:
                    head(i, True)
                head(HG - 1, False)
                sp.wait_ge(sto, 16 * HG + 1)
                sp.wait_ge(sns, 16 * HG + 1)

            @block.tensor
            def _(pe):
                pe.wait_ge(parked, 16)

                def alone():
                    pe.nop(nofuse=True)

                with pe.Fori(0, HG) as i:
                    pe.wait_ge(yd, i + 1)
                    for j in range(4):
                        pe.wait_ge(wl[j], (i + 1) * 16)
                        pe.wait_ge(pfree[j % 2], i * 4 + 2 * (j // 2) + 1)
                        mm_tile(pe, proj_psum(c, j % 2), w[j], c.xn, KD).then_inc(pj, 1)
                    for j in range(2):
                        pe.wait_ge(sqd, i * 2 + j + 1)
                        for (o, n), a in zip(CH, norm_acc()):
                            mm = pe.matmul(a, const(c, "ones"), sq[:, o:o + n], start=True, stop=True)
                        mm.then_inc(ssd, 1)
                    pe.wait_ge(normed, i * 2 + 2)
                    pe.wait_ge(conved, i * 3 + 3)
                    pe.wait_ge(pfree[1], i * 4 + 5)
                    pe.wait_ge(pc, i + 1)
                    alone()
                    for gi, g in enumerate(GROUPS):
                        n, r = g["n"], g["r"]
                        for k in range(n):
                            pe.transpose(ps(A, g, k, width=P), blk(kT, g, k, P), const(c, "ident"))
                        for k in range(n):
                            pe.transpose(ps(B, g, k, width=P), blk(vT, g, k, P), const(c, "ident"))
                        for k in range(n):
                            pe.matmul(ps(C, g, k, P), par(LOGA, g["c0"] + k, r).to_broadcast([r, P]), const(c, g["up"])[0:r, 0:r],
                                      start=True, stop=True)
                        for k in range(n):
                            mm = pe.matmul(ps(Dp, g, k), blk(kT, g, k, P), blk(kT, g, k, P), start=True, stop=True)
                        mm.then_inc(p1, 1)
                        pe.wait_ge(a1, i * 2 + gi + 1)
                        alone()
                        for k in range(n):
                            mm = pe.matmul(ps(A, g, k), blk(kT, g, k, P), blk(qT, g, k, P), start=True, stop=True)
                        mm.then_inc(p2, 1)
                        pe.wait_ge(v2, i * 2 + gi + 1)
                        alone()
                        for k in range(n):
                            mm = pe.transpose(ps(B, g, k), blk(e1, g, k), const(c, "ident")[0:r, 0:r])
                        mm.then_inc(p3, 1)
                        pe.wait_ge(v3, i * 2 + gi + 1)
                        for l, s in enumerate(g["lv"]):
                            q = i * NLV + 6 * gi + l
                            pe.wait_ge(mlr, q + 1)
                            if l:
                                pe.wait_ge(xr, q)
                            alone()
                            for k in range(n):
                                mm = pe.matmul(ps(C, g, k), blk(ml, g, k), blk(x, g, k), start=True, stop=True)
                            mm.then_inc(pr, 1)
                            pe.wait_ge(psr, q + 1)
                            alone()
                            for k in range(n):
                                pe.matmul(ps(Dp, g, k), blk(xt, g, k), blk(pp, g, k), start=True, stop=True)
                            for k in range(n):
                                mm = pe.matmul(ps(A, g, k), blk(pp, g, k), blk(xt, g, k), start=True, stop=True)
                            mm.then_inc(yr, 1)
                        pe.wait_ge(xr, i * NLV + 6 * gi + len(g["lv"]))
                        if gi == 0:
                            for k in range(n):
                                if k:
                                    pe.wait_ge(str_, i * 8 + k)
                                    pe.matmul(c.ps[:, A:A + P], blk(kT, g, k), st[(k - 1) % 2], start=True, stop=True).then_inc(ksr, 1)
                                    pe.matmul(ps(C, g, k), st[(k - 1) % 2], blk(qT, g, k), start=True, stop=False)
                                    pe.wait_ge(rr, i * 7 + k)
                                pe.matmul(c.ps[:, B:B + P], blk(xt, g, k), tok(bv, g, k), start=True, stop=True,
                                          skip_group_check=True).then_inc(ur, 1)
                                pe.wait_ge(usr, i * 8 + k + 1)
                                pe.matmul(ps(C, g, k), us, blk(e2, g, k), start=(k == 0), stop=True)
                                pe.matmul(c.ps[:, Dp:Dp + P], tok(kt, g, k), us, start=True, stop=True,
                                          skip_group_check=True).then_inc(dsr, 1)
                            pe.wait_ge(str_, i * 8 + 8)
                            pe.wait_ge(oc, i + 1)
                            alone()
                    g = GROUPS[1]
                    pe.wait_ge(s0l, (i + 1) * 16)
                    for b in range(NB):
                        mm = pe.matmul(c.ps[:, A + TS * b:A + TS * b + TS], s0[:, b * P:(b + 1) * P], kT[:, TP + TS * b:TP + TS * b + TS],
                                       start=True, stop=True)
                    mm.then_inc(kss, 1)
                    pe.wait_ge(kstc, i + 1)
                    alone()
                    pe.transpose(c.ps[0:NS, B:B + P], kst, const(c, "ident")).then_inc(kst2, 1)
                    pe.wait_ge(rs, i + 1)
                    alone()
                    pe.matmul(c.ps[0:NS, C:C + P], blk(xt, g, 0), tok(bv, g, 0), start=True, stop=True).then_inc(u2, 1)
                    pe.wait_ge(us2, i + 1)
                    alone()
                    pe.matmul(c.ps[:, Dp:Dp + NS], us[0:NS, :], blk(e2, g, 0), start=True, stop=False, skip_group_check=True)
                    for b in range(NB):
                        pe.matmul(c.ps[:, Dp + TS * b:Dp + TS * b + TS], s0[:, b * P:(b + 1) * P],
                                  qT[:, TP + TS * b:TP + TS * b + TS], start=False, stop=(b == NB - 1), skip_group_check=True)
                    pe.matmul(c.ps[:, Dp + 512:Dp + 512 + NB], par(LOGA, 8, NS).to_broadcast([NS, P]), const(c, "batch_s")[0:NS, :],
                              start=True, stop=True)
                    pe.wait_ge(um2, i + 1)
                    for hf in range(2):
                        mm = pe.matmul(c.ps[:, A + 512 * hf:A + 512 * hf + 512], tok(kt, g, 0), um[0:NS, 512 * hf:512 * hf + 512],
                                       start=True, stop=True)
                    mm.then_inc(o2, 1)
                    pe.wait_ge(osq, i + 1)
                    for (o, n), a in zip(CH, (bank(c, 2), bank(c, 3), bank(c, 4)[:, 0:NS])):
                        mm = pe.matmul(a, const(c, "ones"), sq[:, o:o + n], start=True, stop=True)
                    mm.then_inc(oss, 1)

            def sview(a, lo, n):
                return a[:, 3 + TP:].rearrange("p (b t) -> p b t", b=NB)[:, :, lo:lo + n]

            @block.scalar
            def _(act):
                act.wait_ge(parked, 16)
                for s in pfree:
                    act.sem_inc(s, 1)
                with act.Fori(0, HG) as i:
                    for j in range(3):
                        act.wait_ge(pj, i * 4 + j + 1)
                        if j == 2:
                            act.wait_ge(conv, i * 3 + 2)
                            act.wait_ge(nconv, i * 3 + 1)
                        a = proj_psum(c, j % 2)
                        act.activation(cin[j % 2][:, 3:3 + TP], proj_main(c, j % 2), ACT.Copy).then_inc(pfree[j % 2], 1)
                        act.activation(sview(cin[j % 2], 3, TS), a[2].rearrange("p (b t) -> p b t", b=NB), ACT.Copy).then_inc(pfree[j % 2], 1)
                    act.wait_ge(pj, i * 4 + 4)
                    act.activation(zT[:, 0:TP], proj_main(c, 1), ACT.Silu).then_inc(pfree[1], 1)
                    act.activation(zT[:, TP:NT], proj_psum(c, 1)[2], ACT.Silu).then_inc(pfree[1], 1)
                    for j in range(3):
                        act.wait_ge(conv, i * 3 + j + 2)
                        act.activation(qkvz[j], qkvz[j], ACT.Silu).then_inc(conved, 1)
                    for j in range(2):
                        act.wait_ge(conved, i * 3 + j + 1)
                        if j:
                            act.wait_ge(ssd, i * 2 + j)
                        act.activation(sq, qkvz[j], ACT.Square).then_inc(sqd, 1)
                        act.wait_ge(ssd, i * 2 + j + 1)
                        if j:
                            act.wait_ge(normed, i * 2 + j)
                        for (o, n), a in zip(CH, norm_acc()):
                            act.activation(rt[:, o:o + n], a, ACT.Sqrt, bias=const(c, "eps_dk" if j == 0 else "eps"),
                                           scale=float(P) if j == 0 else 1.0).then_inc(rooted, 1)
                    for gi, g in enumerate(GROUPS):
                        act.wait_ge(p1, i * 2 + gi + 1)
                        act.wait_ge(pc, i + 1)
                        for k in range(g["n"]):
                            act.activation(tok(kt, g, k), ps(A, g, k, width=P), ACT.Copy, scale=par(TAIL, g["c0"] + k, g["r"]))
                        act.activation(eg[:, g["o"]:g["o"] + g["n"] * g["r"]], c.ps[:, C:C + g["n"] * g["r"]], ACT.Exp).then_inc(a1, 1)
                        act.wait_ge(v1, i * 2 + gi + 1)
                        act.activation(grp(e1, g), grp(e1, g), ACT.Exp, scale=-1.0)
                        act.activation(grp(e2, g), grp(e2, g), ACT.Exp).then_inc(a2, 1)
                        for l, s in enumerate(g["lv"]):
                            act.wait_ge(pr, i * NLV + 6 * gi + l + 1)
                            act.activation(grp(pp, g), psg(C, g), ACT.Copy).then_inc(psr, 1)
                        if gi == 0:
                            for k in range(g["n"]):
                                act.wait_ge(ur, i * 8 + k + 1)
                                act.activation(us, c.ps[:, B:B + P], ACT.Copy).then_inc(usr, 1)
                            act.wait_ge(dsr, i * 8 + 8)
                            act.activation(sq[:, 0:TP], c.ps[:, C:C + TP], ACT.Square)
                            act.activation(rt[:, 0:TP], c.ps[:, C:C + TP], ACT.Copy).then_inc(oc, 1)
                    act.wait_ge(kss, i + 1)
                    act.activation(kst, c.ps[:, A:A + NS], ACT.Copy).then_inc(kstc, 1)
                    act.wait_ge(u2, i + 1)
                    act.activation(us[0:NS, :], c.ps[0:NS, C:C + P], ACT.Copy).then_inc(us2, 1)
                    act.wait_ge(o2, i + 1)
                    act.activation(eb, c.ps[:, Dp + 512:Dp + 512 + NB], ACT.Exp)
                    act.activation(rt[:, TP:NT], c.ps[:, Dp:Dp + NS], ACT.Copy).then_inc(oc2, 1)
                    act.activation(sq[:, TP:NT], c.ps[:, Dp:Dp + NS], ACT.Square).then_inc(osq, 1)
                    act.wait_ge(oss, i + 1)
                    for (o, n), a in zip(CH, (bank(c, 2), bank(c, 3), bank(c, 4)[:, 0:NS])):
                        act.activation(pp[:, o:o + n], a, ACT.Sqrt, bias=const(c, "eps"), scale=1.0 / P).then_inc(ort, 1)

            @block.vector
            def _(dve):
                dve.wait_ge(parked, 16)
                for s in (yd, conv):
                    dve.sem_inc(s, 1)
                CHAIN = 20
                with dve.Fori(0, HG) as i:
                    n_chain = [0]

                    def settle(ins):
                        n_chain[0] += 1
                        ins.then_inc(dc, 1)
                        dve.wait_ge(dc, i * CHAIN + n_chain[0])

                    settle(dve.tensor_copy(cw, c.convw[:, ds(i, 89)][:, 0:89:8]))
                    dve.tensor_copy(parh, c.par[:, ds(i * NPAR, NPAR)]).then_inc(pc, 1)
                    dve.wait_ge(pc, i + 1)
                    for j in range(3):
                        s = cin[j % 2]
                        dve.wait_ge(hist, i * 3 + j + 1)
                        dve.wait_ge(pfree[j % 2], i * 4 + 2 * (j // 2) + 3)
                        y = qkvz[j][:, 0:TP]
                        ys = qkvz[j][:, TP:NT].rearrange("p (b t) -> p b t", b=NB)
                        dve.tensor_scalar(y, s[:, 0:TP], cw[:, j:j + 1], None, ALU.mult)
                        settle(dve.tensor_scalar(ys, sview(s, 0, TS), cw[:, j:j + 1], None, ALU.mult))
                        for t in range(1, 4):
                            tap = cw[:, 3 * t + j:3 * t + j + 1]
                            dve.scalar_tensor_tensor(out=y, in0=s[:, t:t + TP], scalar=tap, in1=y, op0=ALU.mult, op1=ALU.add)
                            ins = dve.scalar_tensor_tensor(out=ys, in0=sview(s, t, TS), scalar=tap, in1=ys, op0=ALU.mult, op1=ALU.add)
                            if t < 3:
                                settle(ins)
                            else:
                                ins.then_inc(conv, 1)
                    for j in range(2):
                        dve.wait_ge(rooted, i * 6 + 3 * j + 3)
                        settle(dve.reciprocal(rt, rt))
                        dve.tensor_tensor(qkvz[j], qkvz[j], rt, ALU.mult).then_inc(normed, 1)
                    for gi, g in enumerate(GROUPS):
                        dve.wait_ge(p1, i * 2 + gi + 1)
                        for k in range(g["n"]):
                            q, r = g["c0"] + k, g["r"]
                            dve.tensor_scalar(tok(bv, g, k), ps(B, g, k, width=P), par(BETA, q, r), None, ALU.mult)
                        dve.wait_ge(a1, i * 2 + gi + 1)
                        for k in range(g["n"]):
                            q, r = g["c0"] + k, g["r"]
                            dve.tensor_scalar(blk(e1, g, k), ps(C, g, k), par(GCUM, q, r), 0.0, ALU.subtract, ALU.max)
                            ins = dve.tensor_scalar(blk(e2, g, k), ps(C, g, k), par(GCUM, q, r), 0.0, ALU.subtract, ALU.min)
                        ins.then_inc(v1, 1)
                        dve.wait_ge(a2, i * 2 + gi + 1)
                        dve.wait_ge(v1, i * 2 + gi + 1)
                        dve.tensor_tensor(grp(e1, g), grp(e1, g), mask(g["lo"], g), ALU.mult)
                        settle(dve.tensor_tensor(grp(e2, g), grp(e2, g), mask(g["up"], g), ALU.mult))
                        for k in range(g["n"]):
                            dve.scalar_tensor_tensor(out=blk(e1, g, k), in0=ps(Dp, g, k), scalar=par(BETA, g["c0"] + k, g["r"]),
                                                     in1=blk(e1, g, k), op0=ALU.mult, op1=ALU.mult)
                        dve.wait_ge(p2, i * 2 + gi + 1)
                        dve.tensor_tensor(grp(e2, g), psg(A, g), grp(e2, g), ALU.mult)
                        cols = slice(g["o"], g["o"] + g["n"] * g["r"])
                        dve.tensor_tensor(kT[:, cols], kT[:, cols], eg[:, cols], ALU.mult)
                        dve.tensor_tensor(qT[:, cols], qT[:, cols], eg[:, cols], ALU.mult).then_inc(v2, 1)
                        dve.wait_ge(v2, i * 2 + gi + 1)
                        dve.tensor_tensor(grp(x, g), grp(e1, g), mask("m1", g), ALU.mult)
                        dve.wait_ge(p3, i * 2 + gi + 1)
                        settle(dve.tensor_copy(grp(lt, g), psg(B, g)))
                        dve.tensor_tensor(grp(x, g), mask("ident", g), grp(x, g), ALU.subtract)
                        settle(dve.tensor_tensor(grp(xt, g), grp(lt, g), mask("mt1", g), ALU.mult))
                        dve.tensor_tensor(grp(xt, g), mask("ident", g), grp(xt, g), ALU.subtract).then_inc(v3, 1)
                        dve.wait_ge(v3, i * 2 + gi + 1)
                        for l, s in enumerate(g["lv"]):
                            dve.wait_ge(yr, i * NLV + 6 * gi + l + 1)
                            dve.tensor_tensor(grp(x, g), grp(x, g), psg(Dp, g), ALU.subtract)
                            dve.tensor_tensor(grp(xt, g), grp(xt, g), psg(A, g), ALU.subtract).then_inc(xr, 1)
                            dve.wait_ge(xr, i * NLV + 6 * gi + l + 1)
                        if gi == 0:
                            for k in range(8):
                                if k:
                                    dve.wait_ge(ksr, i * 7 + k)
                                    dve.scalar_tensor_tensor(out=tok(bv, g, k), in0=c.ps[:, A:A + P], scalar=par(NBETA, k, P),
                                                             in1=tok(bv, g, k), op0=ALU.mult, op1=ALU.add).then_inc(rr, 1)
                                dve.wait_ge(dsr, i * 8 + k + 1)
                                if k == 0:
                                    dve.wait_ge(sto, i * 16 + 1)
                                    dve.tensor_copy(st[0], c.ps[:, Dp:Dp + P]).then_inc(str_, 1)
                                else:
                                    dve.wait_ge(str_, i * 8 + k)
                                    dve.scalar_tensor_tensor(out=st[k % 2], in0=st[(k - 1) % 2], scalar=par(ETOT, k, P),
                                                             in1=c.ps[:, Dp:Dp + P], op0=ALU.mult, op1=ALU.add).then_inc(str_, 1)
                    g = GROUPS[1]
                    dve.wait_ge(kst2, i + 1)
                    dve.scalar_tensor_tensor(out=tok(bv, g, 0), in0=c.ps[0:NS, B:B + P], scalar=par(NBETA, 8, NS),
                                             in1=tok(bv, g, 0), op0=ALU.mult, op1=ALU.add).then_inc(rs, 1)
                    dve.wait_ge(us2, i + 1)
                    dve.tensor_tensor(um[0:NS, :].rearrange("p (b v) -> p b v", b=NB),
                                      us[0:NS, :].rearrange("p (o v) -> p o v", o=1).to_broadcast([NS, NB, P]),
                                      const(c, "batch_s")[0:NS, :].rearrange("p (b o) -> p b o", o=1).to_broadcast([NS, NB, P]),
                                      ALU.mult).then_inc(um2, 1)
                    dve.wait_ge(oc2, i + 1)
                    dve.wait_ge(sns, i * 16 + 1)
                    for b in range(NB):
                        ins = dve.scalar_tensor_tensor(out=sn[:, b * P:(b + 1) * P], in0=s0[:, b * P:(b + 1) * P], scalar=eb[:, b:b + 1],
                                                       in1=c.ps[:, A + P * b:A + P * b + P], op0=ALU.mult, op1=ALU.add)
                    ins.then_inc(sn2, 1)
                    dve.wait_ge(ort, i * 3 + 3)
                    dve.wait_ge(oc, i + 1)
                    settle(dve.reciprocal(pp, pp))
                    settle(dve.tensor_tensor(rt, rt, pp, ALU.mult))
                    dve.scalar_tensor_tensor(out=yT[:, ds(i * NT, NT)], in0=rt, scalar=c.normw[:, 40:41], in1=zT,
                                             op0=ALU.mult, op1=ALU.mult).then_inc(yd, 1)
                    assert n_chain[0] == CHAIN, n_chain

            @block.gpsimd
            def _(pool):
                pool.wait_ge(parked, 16)
                for s in cin:
                    ins = pool.memset(s[:, 0:3], 0.0)
                with pool.Fori(0, HG) as i:
                    for j in range(3):
                        s = cin[j % 2]
                        tile = i + j * 8
                        if j == 2:
                            pool.wait_ge(conv, i * 3 + 2)
                        else:
                            pool.wait_ge(conv, i * 3 + 1)
                        pool.tensor_copy(sview(s, 0, 3),
                                         c.convT.rearrange("p k n -> p (k n)")[:, ds(tile * 24, 24)].rearrange("p (b r) -> p b r", b=NB)
                                         ).then_inc(hist, 1)
                        pool.wait_ge(pfree[j % 2], i * 4 + 2 * (j // 2) + 3)
                        pool.tensor_copy(c.newconv[:, ds(tile * 27, 3)], s[:, TP:TP + 3])
                        pool.tensor_copy(c.newconv[:, ds(tile * 27 + 3, 24)].rearrange("p (b r) -> p b r", b=NB),
                                         sview(s, TS, 3)).then_inc(nconv, 1)
                    for gi, g in enumerate(GROUPS):
                        pool.wait_ge(v3, i * 2 + gi + 1)
                        for l, s in enumerate(g["lv"]):
                            if l:
                                pool.wait_ge(pr, i * NLV + 6 * gi + l)
                            pool.tensor_tensor(grp(ml, g), grp(lt, g), mask(f"mt{s}", g), ALU.mult).then_inc(mlr, 1)

    conv_rows = take(c, QKV)
    with ExitStack() as ctx:
        back, tr, ev, st_ = sems(nc, ctx, c, "residual_back", "turned", "evacuated", "conv_stored")
        with nc.Block() as block:
            @block.sync
            def _(sp):
                sp.dma_start(c.xTf, park).then_inc(back, 16)
                sp.wait_ge(ev, 24)
                sp.dma_start(io["out8"][0, 0], conv_rows[0:3, :]).then_inc(st_, 16)
                sp.dma_start(io["out9"][0].rearrange("b r f -> (b r) f"), conv_rows[3:27, :]).then_inc(st_, 16)
                sp.wait_ge(st_, 32)
                sp.wait_ge(back, 16)

            @block.tensor
            def _(pe):
                for n in range(24):
                    if n >= 8:
                        pe.wait_ge(ev, n - 7)
                    pe.transpose(bank(c, n % 8)[0:27, 0:P], c.newconv[:, n * 27:(n + 1) * 27], const(c, "ident")).then_inc(tr, 1)

            @block.vector
            def _(dve):
                for n in range(24):
                    dve.wait_ge(tr, n + 1)
                    dve.tensor_copy(conv_rows[0:27, n * P:(n + 1) * P], bank(c, n % 8)[0:27, 0:P]).then_inc(ev, 1)

    wo = [conv_rows[:, j * 1024:(j + 1) * 1024].rearrange("p (k f) -> p k f", k=KD) for j in range(2)]
    w_out = io["gdn_w_out"][0].rearrange("(k p) f -> p k f", p=P)
    out_stage(c, KD, lambda m, j: [(wo[j], w_out[:, :, ds(m * P, P)])], yT.rearrange("p (k t) -> p k t", k=HG), wo)


def final_stage(c):
    nc, io = c.nc, c.io
    norm_stage(c, 4, c.xn, 0)
    c.at = 0
    rows = take(c, 9 * D).rearrange("p (t d) -> p t d", t=9)
    jobs = [(t, k) for t in range(9) for k in range(KD)]
    with ExitStack() as ctx:
        tr, ev, st_ = sems(nc, ctx, c, "turned", "evacuated", "rows_stored")
        with nc.Block() as block:
            @block.tensor
            def _(pe):
                for n, (t, k) in enumerate(jobs):
                    if n >= 8:
                        pe.wait_ge(ev, n - 7)
                    r = P if t < 8 else NS
                    pe.transpose(bank(c, n % 8)[0:r, 0:P], c.xn[:, k, t * P:t * P + r], const(c, "ident")).then_inc(tr, 1)

            @block.vector
            def _(dve):
                for n, (t, k) in enumerate(jobs):
                    dve.wait_ge(tr, n + 1)
                    r = P if t < 8 else NS
                    dve.tensor_copy(rows[0:r, t, k * P:(k + 1) * P], bank(c, n % 8)[0:r, 0:P]).then_inc(ev, 1)

            @block.sync
            def _(sp):
                for t in range(9):
                    sp.wait_ge(ev, 8 * t + 8)
                    if t < 8:
                        sp.dma_start(io["out0"][0, t * P:(t + 1) * P, :], rows[:, t, :]).then_inc(st_, 16)
                    else:
                        sp.dma_start(io["out1"].rearrange("b t d -> (b t) d"), rows[0:NS, t, :]).then_inc(st_, 16)
                sp.wait_ge(st_, 9 * 16)


class Nsa:
    pass


def nsa_buffers(c):
    c.at = 0
    a = Nsa()
    a.qTf = take(c, HG * NT)
    a.qT = a.qTf.rearrange("p (k t) -> p k t", k=HG)
    a.kvT = take(c, 6 * NT).rearrange("p (k t) -> p k t", k=6)
    a.rows = take(c, 9 * 6 * P).rearrange("p (t f) -> p t f", t=9)
    a.gates = take(c, 9 * 48).rearrange("p (t f) -> p t f", t=9)
    a.kc = take(c, 320)
    a.vcp = take(c, P)
    a.vcs = take(c, NB * P)
    a.vnew = take(c, NB * 2 * P)
    a.sgates = take(c, NB * 3)
    a.free = c.at
    return a


def nsa_project(c, a):
    nc, io = c.nc, c.io
    c.at = a.free
    w_in = io["nsa_w_in"][0].rearrange("(k p) f -> p k f", p=P)
    wb = [take(c, KD * P).rearrange("p (k f) -> p k f", k=KD) for _ in range(2)]
    wg = take(c, KD * 48).rearrange("p (k f) -> p k f", k=KD)

    def q_src(m, j):
        return [(wb[j][:, :, g * DH:(g + 1) * DH], w_in[:, :, ds(m * DH + g * HG * DH, DH)]) for g in range(2)]

    def q_evac(dve, m, main, last):
        yield dve.tensor_scalar(a.qTf[:, ds(m * NT, TP)], main, DH ** -0.5, None, ALU.mult)
        yield dve.tensor_scalar(a.qTf[:, ds(m * NT + TP, NS)], last, DH ** -0.5, None, ALU.mult)

    proj_stage(c, KD, HG, q_src, c.xn, wb, q_evac)
    kvf = a.kvT.rearrange("p k t -> p (k t)")

    def kv_evac(dve, m, main, last):
        yield dve.tensor_copy(kvf[:, ds(m * NT, TP)], main)
        yield dve.tensor_copy(kvf[:, ds(m * NT + TP, NS)], last)

    proj_stage(c, KD, 6, lambda m, j: [(wb[j], w_in[:, :, ds(m * P + D, P)])], c.xn, wb, kv_evac)

    park = nc.dram_tensor("decode_gates", (NS, 48), F32).ap()
    jobs = [(t, k) for t in range(9) for k in range(6)]
    with ExitStack() as ctx:
        wl, gm, gd, tr, ev, gst, vn, st = sems(nc, ctx, c, "gate_w_loaded", "gates_multiplied", "gates_done", "turned", "evacuated",
                                               "gates_parked", "new_rows_placed", "rows_stored")
        with nc.Block() as block:
            @block.sync
            def _(sp):
                sp.dma_start(wg, w_in[:, :, 1792:1840]).then_inc(wl, 16)
                sp.dma_start(io["out5"][0].rearrange("b r k g d -> b r (k g d)")[:, 0:PAST - TS],
                             io["cache_nsa_win"][0].rearrange("b r k g d -> b r (k g d)")[:, TS:PAST]).then_inc(st, 16)
                sp.wait_ge(gd, 2)
                sp.dma_start(park, a.gates[0:NS, 8, :]).then_inc(gst, 16)
                sp.wait_ge(gst, 16)
                for gh in range(NH):
                    sp.dma_start(a.sgates[gh * TS:(gh + 1) * TS, :].rearrange("t (b r) -> t b r", b=NB),
                                 park[:, gh * 3:gh * 3 + 3].rearrange("(b t) r -> t b r", b=NB)).then_inc(vn, 16)
                sp.wait_ge(ev, len(jobs))
                for b in range(NB):
                    for n, k in enumerate((3, 5)):
                        o = (b * 2 + n) * P
                        sp.dma_start(a.vnew[0:TS, o:o + P], a.rows[b * TS:(b + 1) * TS, 8, k * P:(k + 1) * P]).then_inc(vn, 16)
                sp.dma_start(io["out2"][0, 0].rearrange("(t p) k g d -> p t (k g d)", p=P), a.rows[:, 0:8, 0:512]).then_inc(st, 16)
                sp.dma_start(io["out3"][0].rearrange("b t k g d -> (b t) (k g d)"), a.rows[0:NS, 8, 0:512]).then_inc(st, 16)
                sp.dma_start(io["out4"][0, 0].rearrange("(t p) k g d -> p t (k g d)", p=P), a.rows[:, 4:8, 512:768]).then_inc(st, 16)
                for b in range(NB):
                    sp.dma_start(io["out5"][0, b].rearrange("r k g d -> r (k g d)")[PAST - TS:PAST],
                                 a.rows[b * TS:(b + 1) * TS, 8, 512:768]).then_inc(st, 16)
                sp.wait_ge(st, 16 * (4 + NB))
                sp.wait_ge(vn, 16 * (NH + 2 * NB))

            @block.tensor
            def _(pe):
                pe.wait_ge(wl, 16)
                for t in range(9):
                    n = P if t < 8 else NS
                    for k in range(KD):
                        mm = pe.matmul(bank(c, 0)[0:n, 48 * t:48 * t + 48], c.xn[:, k, t * P:t * P + n], wg[:, k, :],
                                       start=(k == 0), stop=(k == KD - 1))
                mm.then_inc(gm, 1)
                for n, (t, k) in enumerate(jobs):
                    if n >= 7:
                        pe.wait_ge(ev, n - 6)
                    r = P if t < 8 else NS
                    pe.transpose(bank(c, 1 + n % 7)[0:r, 0:P], a.kvT[:, k, t * P:t * P + r], const(c, "ident")).then_inc(tr, 1)

            @block.scalar
            def _(act):
                act.wait_ge(gm, 1)
                act.activation(a.gates[:, 0:8, :], bank(c, 0)[:, 0:384].rearrange("p (t f) -> p t f", t=8), ACT.Sigmoid).then_inc(gd, 1)
                act.activation(a.gates[0:NS, 8, :], bank(c, 0)[0:NS, 384:432], ACT.Sigmoid).then_inc(gd, 1)

            @block.vector
            def _(dve):
                for n, (t, k) in enumerate(jobs):
                    dve.wait_ge(tr, n + 1)
                    r = P if t < 8 else NS
                    dve.tensor_copy(a.rows[0:r, t, k * P:(k + 1) * P], bank(c, 1 + n % 7)[0:r, 0:P]).then_inc(ev, 1)


def compress_stage(c, a, kind):
    nc, io = c.nc, c.io
    c.at = a.free
    pastT = take(c, NB * PAST + 32)
    hid = take(c, 4 * 320).rearrange("p (n m) -> p n m", n=4)
    w2 = take(c, 2 * DH).rearrange("p (n f) -> p n f", n=2)
    ring = take(c, 8 * P).rearrange("p (s f) -> p s f", s=8)
    pe_rows, bias = take(c, P), take(c, 4)
    w1 = c.xnf[:, 0:8192].rearrange("p (l f) -> p l f", l=32)
    name = "kv"[kind]
    w1_d = io[f"nsa_cmp_w1_{name}"][0].rearrange("(l d) f -> d l f", d=DH)
    w2_d = io[f"nsa_cmp_w2_{name}"][0].rearrange("(n p) f -> p n f", p=P)
    pool_d = io["cache_nsa_kv"][0].rearrange("n p k g d -> n p k (g d)")
    PIECES = 4
    LP = 32 // PIECES
    with ExitStack() as ctx:
        wl = sems(nc, ctx, c, *[f"w1_piece{q}_loaded" for q in range(PIECES)])
        pgl = sems(nc, ctx, c, *[f"page{q}_loaded" for q in range(8)])
        w2l, pel, tr, ev, pt, hm, bc, hd, om, od, z = sems(
            nc, ctx, c, "w2_loaded", "positions_loaded", "pages_turned", "pages_kept", "positions_turned", "hidden_product", "bias_copied",
            "hidden_done", "out_product", "out_copied", "pad_zeroed")
        with nc.Block() as block:
            @block.sync
            def _(sp):
                sp.dma_start(w2, w2_d).then_inc(w2l, 16)
                for g in range(2):
                    sp.dma_start(pe_rows[0:32, g * DH:(g + 1) * DH], io[f"nsa_pe_{name}"][0]).then_inc(pel, 16)
                for q in range(PIECES):
                    for g in range(2):
                        sp.dma_start(w1[g * DH:(g + 1) * DH, q * LP:(q + 1) * LP, :], w1_d[:, q * LP:(q + 1) * LP, :]).then_inc(wl[q], 16)

            @block.gpsimd
            def _(pool):
                pool.memset(hid[:, :, 63:64], 0.0).then_inc(z, 1)
                pool.sem_inc(ev, 1)
                with pool.Fori(0, 4) as i:
                    for s in range(8):
                        page = pool.value_load(c.pages[0:1, ds(i * 8 + s, 1)], min_val=0, max_val=NPHYS - 1)
                        pool.wait_ge(ev, i * 8 + 1)
                        pool.dma_start(ring[:, s, :], pool_d[ds(page, 1), :, kind, :].rearrange("o p f -> p (o f)")).then_inc(pgl[s], 16)

            @block.tensor
            def _(pe):
                pe.wait_ge(pel, 32)
                pe.transpose(bank(c, 7)[:, 0:32], pe_rows[0:32, :], const(c, "ident")[0:32, 0:32]).then_inc(pt, 1)
                with pe.Fori(0, 4) as i:
                    for s in range(8):
                        pe.wait_ge(pgl[s], i * 16 + 16)
                        if s % 4 == 0:
                            pe.wait_ge(ev, i * 8 + 1)
                        pe.transpose(bank(c, s // 4)[:, (s % 4) * P:(s % 4 + 1) * P], ring[:, s, :], const(c, "ident")).then_inc(tr, 1)
                pe.wait_ge(ev, 34)
                for l in range(32):
                    if l % LP == 0:
                        pe.wait_ge(wl[l // LP], 32)
                    for g in range(2):
                        rows = slice(g * DH, (g + 1) * DH)
                        for hf in range(2):
                            b = (g * 2 + hf) * 2
                            wt = w1[rows, l, hf * P:(hf + 1) * P]
                            pe.matmul(bank(c, b)[:, 0:NCMP], wt, a.kvT[rows, kind, l:l + 16 * (NCMP - 1) + 1:16], start=(l == 0), stop=(l == 31))
                            mm = pe.matmul(bank(c, b + 1)[:, 0:257], wt, pastT[rows, l:l + 16 * 256 + 1:16], start=(l == 0), stop=(l == 31))
                mm.then_inc(hm, 1)
                pe.wait_ge(hd, 1)
                pe.wait_ge(w2l, 16)
                pe.wait_ge(z, 1)
                if kind == 0:
                    for g in range(2):
                        for hf in range(2):
                            mm = pe.matmul(bank(c, 0)[g * DH:(g + 1) * DH, 0:320], w2[:, hf, :], hid[:, g * 2 + hf, :],
                                           start=(hf == 0), stop=(hf == 1))
                    mm.then_inc(om, 1)
                else:
                    for n in range(9):
                        m, o = (NCMP, 0) if n == 0 else (NCMPS, 64 + 32 * (n - 1))
                        for g in range(2):
                            for hf in range(2):
                                mm = pe.matmul(c.ps[0:m, 512 * (n // 4) + (n % 4) * P + g * DH:512 * (n // 4) + (n % 4) * P + (g + 1) * DH],
                                               hid[:, g * 2 + hf, o:o + m], w2[:, hf, :], start=(hf == 0), stop=(hf == 1))
                    mm.then_inc(om, 1)

            @block.vector
            def _(dve):
                with dve.Fori(0, 4) as i:
                    for s in range(8):
                        dve.wait_ge(tr, i * 8 + (s // 4 * 4 + 4))
                        dve.tensor_copy(pastT[:, ds(i * 1024 + s * P, P)], bank(c, s // 4)[:, (s % 4) * P:(s % 4 + 1) * P]).then_inc(ev, 1)
                dve.wait_ge(pt, 1)
                dve.tensor_copy(pastT[:, NB * PAST:], bank(c, 7)[:, 0:32]).then_inc(ev, 1)
                dve.wait_ge(hm, 1)
                for n in range(4):
                    ins = dve.tensor_copy(bias[:, n:n + 1], bank(c, 2 * n + 1)[:, 256:257])
                ins.then_inc(bc, 1)
                dve.wait_ge(om, 1)
                if kind == 0:
                    dve.tensor_copy(a.kc, bank(c, 0)[:, 0:320]).then_inc(od, 1)
                else:
                    dve.tensor_copy(a.vcp[0:NCMP, :], c.ps[0:NCMP, 0:P])
                    dve.tensor_copy(a.vcs[0:NCMPS, 0:3 * P], c.ps[0:NCMPS, P:4 * P])
                    dve.tensor_copy(a.vcs[0:NCMPS, 3 * P:], c.ps[0:NCMPS, 4 * P:9 * P]).then_inc(od, 1)

            @block.scalar
            def _(act):
                act.wait_ge(bc, 1)
                for n in range(4):
                    act.activation(hid[:, n, 0:NCMP], bank(c, 2 * n)[:, 0:NCMP], ACT.Silu, bias=bias[:, n:n + 1])
                    ins = act.activation(hid[:, n, 64:320], bank(c, 2 * n + 1)[:, 0:256], ACT.Silu, bias=bias[:, n:n + 1])
                ins.then_inc(hd, 1)


def prompt_attention(c, a):
    nc = c.nc
    c.at = a.free
    qs = take(c, TP)
    PW = 1024 + 640 + 64
    pr = [take(c, PW) for _ in range(2)]
    pts = [take(c, 512) for _ in range(2)]
    ot = [take(c, P) for _ in range(2)]
    nmax, rsum, rc, coef = take(c, 6), take(c, 6), take(c, 6), take(c, 6)
    QT = TP // P
    UNITS = [(i, g) for i in range(QT) for g in range(2)]
    NU = len(UNITS)

    def blocks(u):
        i, g = UNITS[u]
        w0 = max(0, i - 4)
        bl = [("s", k, 128 * k, P) for k in range(i + 1)]
        bl += [("w", k, 1024 + 128 * (k - w0), P) for k in range(w0, i + 1)]
        return bl + [("c", 0, 1664, NCMP)]

    def groups(u):
        bl = blocks(u)
        gr = [bl[n:n + 4] for n in range(0, len(bl), 4)]
        if UNITS[u][1]:
            gr.append("out")
        return gr

    FLOW = [(u, n, gr) for u in range(NU) for n, gr in enumerate(groups(u))]
    first = [next(x for x, (uu, n, _) in enumerate(FLOW) if uu == u) for u in range(NU)] + [len(FLOW)]
    NF = len(FLOW)

    def by_act(x):
        return x % 2 == 0

    def n_act(x):
        return sum(by_act(y) for y in range(x + 1))

    N_ACT = n_act(NF - 1)
    N_DVE = NF - N_ACT
    S, W = 0, 1024

    with ExitStack() as ctx:
        qc, sc, mx, ex, tr, eva, evd, pv, cf, cb, dc, mc = sems(
            nc, ctx, c, "queries_copied", "scores_done", "maxima_ready", "probs_ready", "probs_turned", "turned_by_act", "turned_by_dve",
            "outputs_done", "coefficients", "combined", "vector_chain", "masked")

        def kept(eng, t, x):
            if by_act(x):
                eng.wait_ge(eva, t * N_ACT + n_act(x))
            else:
                eng.wait_ge(evd, t * N_DVE + (x + 1 - n_act(x)))

        with nc.Block() as block:
            @block.tensor
            def _(pe):
                def scores(t, u):
                    i, g = UNITS[u]
                    rows = slice(g * DH, (g + 1) * DH)
                    q = qs[rows, i * P:(i + 1) * P]
                    w0, n = max(0, i - 4), i + 1
                    for o in range(0, n * P, 512):
                        m = min(512, n * P - o)
                        pe.matmul(c.ps[:, S + o:S + o + m], q, a.kvT[rows, 2, o:o + m], start=True, stop=True)
                    nw = (n - w0) * P
                    for o in range(0, nw, 512):
                        m = min(512, nw - o)
                        pe.matmul(c.ps[:, W + o:W + o + m], q, a.kvT[rows, 4, w0 * P + o:w0 * P + o + m], start=True, stop=True)
                    pe.matmul(c.ps[:, W + 640:W + 640 + NCMP], q, a.kc[rows, 0:NCMP], start=True, stop=True).then_inc(sc, 1)

                with pe.Fori(0, HG) as t:
                    pe.wait_ge(qc, t + 1)
                    scores(t, 0)
                    for u, (i, g) in enumerate(UNITS):
                        pe.wait_ge(ex, t * NU + u + 1)
                        if u + 1 < NU:
                            scores(t, u + 1)
                        o = c.ps[:, 3072 + 512 * (u % 2):3072 + 512 * (u % 2) + 192]
                        grs = groups(u)
                        kinds = [b[0] for b in blocks(u)]
                        done = []

                        def products(n):
                            kept(pe, t, first[u] + n)
                            x = (first[u] + n) % 2
                            for m, (kind, kb, col, w) in enumerate(grs[n]):
                                br = "csw".index(kind)
                                v = {"s": a.rows[:, kb, 384 + g * DH:384 + (g + 1) * DH], "w": a.rows[:, kb, 640 + g * DH:640 + (g + 1) * DH],
                                     "c": a.vcp[0:NCMP, g * DH:(g + 1) * DH]}[kind]
                                done.append(kind)
                                mm = pe.matmul(o[:, br * DH:(br + 1) * DH], pts[x][0:w, m * P:(m + 1) * P], v,
                                               start=(done.count(kind) == 1), stop=(done.count(kind) == kinds.count(kind)))
                            return mm

                        for n, gr in enumerate(grs):
                            x = first[u] + n
                            if gr == "out":
                                products(n - 1).then_inc(pv, 1)
                                pe.wait_ge(cb, t * NU + u + 1)
                                if x >= 2:
                                    kept(pe, t, x - 2)
                                pe.transpose(c.ps[:, 2048 + 512 * (x % 2):2048 + 512 * (x % 2) + P], ot[i % 2], const(c, "ident")).then_inc(tr, 1)
                                continue
                            if x >= 2:
                                kept(pe, t, x - 2)
                            if gr[0][0] == "c":
                                pe.nop(nofuse=True)
                            for m, (kind, kb, col, w) in enumerate(gr):
                                mm = pe.transpose(c.ps[0:w, 2048 + 512 * (x % 2) + m * P:2048 + 512 * (x % 2) + (m + 1) * P],
                                                  pr[u % 2][:, col:col + w], const(c, "ident"))
                            mm.then_inc(tr, 1)
                            if n == 0 and u >= 2:
                                pe.wait_ge(cb, t * NU + u - 1)
                            if n:
                                products(n - 1)
                        if grs[-1] != "out":
                            products(len(grs) - 1).then_inc(pv, 1)

            def take_group(eng, t, x, copy, sem):
                u, n, gr = FLOW[x]
                eng.wait_ge(tr, t * NF + x + 1)
                src = c.ps[:, 2048 + 512 * (x % 2):2048 + 512 * (x % 2) + 512]
                if gr == "out":
                    i = UNITS[u][0]
                    copy(c.xnf[:, ds(t * NT + i * P, P)], src[:, 0:P]).then_inc(sem, 1)
                    return
                last = gr[-1]
                if last[0] == "c":
                    if len(gr) > 1:
                        copy(pts[x % 2][:, 0:(len(gr) - 1) * P], src[:, 0:(len(gr) - 1) * P])
                    copy(pts[x % 2][0:NCMP, (len(gr) - 1) * P:len(gr) * P], src[0:NCMP, (len(gr) - 1) * P:len(gr) * P]).then_inc(sem, 1)
                else:
                    copy(pts[x % 2][:, 0:len(gr) * P], src[:, 0:len(gr) * P]).then_inc(sem, 1)

            @block.scalar
            def _(act):
                def exps(t, u):
                    i, g = UNITS[u]
                    w0, n = max(0, i - 4), i + 1
                    p = pr[u % 2]
                    o = 3 * (u % 2)
                    if u >= 2:
                        act.wait_ge(cb, t * NU + u - 1)
                    act.wait_ge(mx, t * NU + u + 1)
                    act.activation(p[:, 1664:1664 + NCMP], c.ps[:, W + 640:W + 640 + NCMP], ACT.Exp, bias=nmax[:, o:o + 1], accum_out=rsum[:, o:o + 1])
                    act.activation(p[:, 0:n * P], c.ps[:, S:S + n * P], ACT.Exp, bias=nmax[:, o + 1:o + 2], accum_out=rsum[:, o + 1:o + 2])
                    act.activation(p[:, 1024:1024 + (n - w0) * P], c.ps[:, W:W + (n - w0) * P], ACT.Exp, bias=nmax[:, o + 2:o + 3],
                                   accum_out=rsum[:, o + 2:o + 3]).then_inc(ex, 1)

                with act.Fori(0, HG) as t:
                    exps(t, 0)
                    for u in range(NU):
                        if u + 1 < NU:
                            exps(t, u + 1)
                        for x in range(first[u], first[u + 1]):
                            if by_act(x):
                                take_group(act, t, x, lambda d, s: act.activation(d, s, ACT.Copy), eva)

            @block.vector
            def _(dve):
                def maxima(t, u):
                    i, g = UNITS[u]
                    w0, n = max(0, i - 4), i + 1
                    o = 3 * (u % 2)
                    dve.wait_ge(sc, t * NU + u + 1)
                    d = c.ps[:, S + i * P:S + n * P]
                    dve.tensor_tensor(d, d, const(c, "causal_add"), ALU.add)
                    d = c.ps[:, W + (i - w0) * P:W + (n - w0) * P]
                    dve.tensor_tensor(d, d, const(c, "causal_add"), ALU.add)
                    if i >= 4:
                        d = c.ps[:, W:W + P]
                        dve.tensor_tensor(d, d, const(c, "far_add"), ALU.add)
                    d = c.ps[:, W + 640:W + 640 + NCMP]
                    dve.tensor_tensor(d, d, const(c, f"cmp_add{i}"), ALU.add).then_inc(mc, 1)
                    dve.wait_ge(mc, t * NU + u + 1)
                    dve.tensor_reduce(nmax[:, o:o + 1], d, AX.X, ALU.max, negate=True)
                    dve.tensor_reduce(nmax[:, o + 1:o + 2], c.ps[:, S:S + n * P], AX.X, ALU.max, negate=True)
                    dve.tensor_reduce(nmax[:, o + 2:o + 3], c.ps[:, W:W + (n - w0) * P], AX.X, ALU.max, negate=True).then_inc(mx, 1)

                CHAIN = 4 * NU + 2
                with dve.Fori(0, HG) as t:
                    n_chain = [0]

                    def settle(ins):
                        n_chain[0] += 1
                        ins.then_inc(dc, 1)
                        dve.wait_ge(dc, t * CHAIN + n_chain[0])

                    dve.tensor_copy(qs, a.qTf[:, ds(t * NT, TP)]).then_inc(qc, 1)
                    maxima(t, 0)
                    for u, (i, g) in enumerate(UNITS):
                        if u + 1 < NU:
                            maxima(t, u + 1)
                        o = 3 * (u % 2)
                        dve.wait_ge(ex, t * NU + u + 1)
                        settle(dve.reciprocal(rc[:, o:o + 3], rsum[:, o:o + 3]))
                        settle(dve.tensor_tensor(coef[:, o:o + 3], rc[:, o:o + 3],
                                                 a.gates.rearrange("p t f -> p (t f)")[:, ds(t * 3 + (i * 48 + g * 24), 3)], ALU.mult))
                        if i == 0:
                            settle(dve.tensor_tensor(coef[:, o:o + 1], coef[:, o:o + 1], const(c, "row_has_cmp"), ALU.mult))
                        for x in range(first[u], first[u + 1]):
                            if FLOW[x][2] == "out":
                                continue
                            if not by_act(x):
                                take_group(dve, t, x, dve.tensor_copy, evd)
                        dve.wait_ge(pv, t * NU + u + 1)
                        out = ot[i % 2][:, g * DH:(g + 1) * DH]
                        acc = c.ps[:, 3072 + 512 * (u % 2):3072 + 512 * (u % 2) + 192]
                        settle(dve.tensor_scalar(out, acc[:, 0:DH], coef[:, o:o + 1], None, ALU.mult))
                        settle(dve.scalar_tensor_tensor(out=out, in0=acc[:, DH:2 * DH], scalar=coef[:, o + 1:o + 2], in1=out, op0=ALU.mult, op1=ALU.add))
                        dve.scalar_tensor_tensor(out=out, in0=acc[:, 2 * DH:], scalar=coef[:, o + 2:o + 3], in1=out,
                                                 op0=ALU.mult, op1=ALU.add).then_inc(cb, 1)
                        x = first[u + 1] - 1
                        if FLOW[x][2] == "out" and not by_act(x):
                            take_group(dve, t, x, dve.tensor_copy, evd)
                    assert n_chain[0] == CHAIN, n_chain


def sample_attention(c, a):
    nc, io = c.nc, c.io
    c.at = a.free
    SK = PAST + TS
    kv = [take(c, NPG * 2 * P).rearrange("p (n f) -> p n f", n=NPG) for _ in range(2)]
    wn = take(c, NPG * 2 * P).rearrange("p (n f) -> p n f", n=NPG)
    kT = take(c, 2 * PAST)
    qb, knew, kcb, vcb, vnb = take(c, NS), take(c, 2 * TS), take(c, NCMPS), take(c, P), take(c, 2 * P)
    pts = [take(c, 512) for _ in range(2)]
    small = take(c, 12)
    nmax, rsum, rc, coef = [small[:, 3 * n:3 * n + 3] for n in range(4)]
    ob = take(c, P)
    dead = a.kvT[:, 0:2, :].rearrange("p k t -> p (k t)")
    sb = dead[:, 0:2 * SK + NCMPS]
    pb = dead[:, 2 * SK + NCMPS:2 * (2 * SK + NCMPS)] if 2 * (2 * SK + NCMPS) <= 2 * NT else take(c, 2 * SK + NCMPS)
    pool_d = io["cache_nsa_kv"][0].rearrange("n p k g d -> n p (k g d)")
    win_d = io["cache_nsa_win"][0].rearrange("b (n p) k g d -> b p n (k g d)", p=P)
    BL = [("s", n, 128 * n, P) for n in range(4)] + [("s", 4, PAST, TS)]
    BL += [("w", n, SK + 128 * n, P) for n in range(4)] + [("w", 4, SK + PAST, TS)] + [("c", 0, 2 * SK, NCMPS)]
    GR = [BL[0:4], BL[4:8], BL[8:11]]
    RANGE = [(2 * SK, NCMPS), (0, SK), (SK, SK)]

    with ExitStack() as ctx:
        kl0, kl1, wnl, kt_, ktc, qc, sc, scp, mx, ex, cf, tr, ev, pv, cb, ot, od, vc, used = sems(
            nc, ctx, c, "pages0_loaded", "pages1_loaded", "window_loaded", "keys_turned", "keys_copied", "inputs_copied", "scores_done",
            "scores_copied", "maxima_ready", "probs_ready", "coefficients", "probs_turned", "turned_kept", "outputs_done", "combined",
            "out_turned", "out_kept", "vector_chain", "rows_used")
        kl = [kl0, kl1]
        with nc.Block() as block:
            @block.gpsimd
            def _(pool):
                pool.sem_inc(pv, 1)
                with pool.Fori(0, NB // 2) as i:
                    for j in range(2):
                        pool.wait_ge(pv, i * 2 + 1)
                        for n in range(NPG):
                            page = pool.value_load(c.pages[0:1, ds(i * 8 + j * 4 + n, 1)], min_val=0, max_val=NPHYS - 1)
                            pool.dma_start(kv[j][:, n, :], pool_d[ds(page, 1), :, 256:512].rearrange("o p f -> p (o f)")).then_inc(kl[j], 16)

            @block.sync
            def _(sp):
                sp.dma_start(wn, win_d[0]).then_inc(wnl, 16)
                with sp.Fori(0, NB - 1) as b:
                    sp.wait_ge(pv, b + 2)
                    sp.dma_start(wn, win_d[ds(b + 1, 1)].rearrange("o p n f -> p (o n) f")).then_inc(wnl, 16)

            def product(pe, j, b, x):
                pe.wait_ge(ev, b * 3 + x + 1)
                pe.nop(nofuse=True)
                for m, (kind, n, col, w) in enumerate(GR[x]):
                    br = "csw".index(kind)
                    for g in range(2):
                        f = slice(g * DH, (g + 1) * DH)
                        if kind == "c":
                            v = vcb[0:NCMPS, f]
                        elif n == 4:
                            v = vnb[0:TS, "sw".index(kind) * P + g * DH:"sw".index(kind) * P + (g + 1) * DH]
                        else:
                            v = (kv[j] if kind == "s" else wn)[:, n, P + g * DH:P + (g + 1) * DH]
                        mm = pe.matmul(bank(c, 7)[f, br * DH:(br + 1) * DH], pts[x % 2][0:w, m * P + g * DH:m * P + (g + 1) * DH], v,
                                       start=(n == 0), stop=(n == 4 or kind == "c"), skip_group_check=True)
                return mm

            @block.tensor
            def _(pe):
                with pe.Fori(0, NB // 2) as i:
                    for j in range(2):
                        b = i * 2 + j
                        pe.wait_ge(kl[j], i * 64 + 64)
                        for n in range(NPG):
                            pe.transpose(bank(c, 0)[:, n * P:(n + 1) * P], kv[j][:, n, 0:P], const(c, "ident"))
                        pe.wait_ge(wnl, b * 16 + 16)
                        for n in range(NPG):
                            mm = pe.transpose(bank(c, 1)[:, n * P:(n + 1) * P], wn[:, n, 0:P], const(c, "ident"))
                        mm.then_inc(kt_, 1)
                        pe.wait_ge(ktc, b + 1)
                        pe.wait_ge(qc, b + 1)
                        pe.nop(nofuse=True)
                        for g in range(2):
                            rows = slice(g * DH, (g + 1) * DH)
                            for n in range(2):
                                pe.matmul(bank(c, 2 + n)[rows, :], qb[rows, :], kT[rows, n * PAST:(n + 1) * PAST], start=True, stop=True)
                            pe.matmul(bank(c, 4)[rows, 0:2 * TS], qb[rows, :], knew[rows, :], start=True, stop=True)
                            mm = pe.matmul(bank(c, 4)[rows, 2 * TS:2 * TS + NCMPS], qb[rows, :], kcb[rows, :], start=True, stop=True)
                        mm.then_inc(sc, 1)
                        pe.wait_ge(ex, b + 1)
                        pe.nop(nofuse=True)
                        for x, gr in enumerate(GR):
                            if x == 2:
                                pe.wait_ge(ev, b * 3 + 1)
                                pe.nop(nofuse=True)
                            for m, (kind, n, col, w) in enumerate(gr):
                                mm = pe.transpose(bank(c, 5 + x % 2)[0:w, m * P:(m + 1) * P], pb[:, col:col + w], const(c, "ident"))
                            mm.then_inc(tr, 1)
                            if x:
                                product(pe, j, b, x - 1)
                        product(pe, j, b, 2).then_inc(pv, 1)
                        pe.wait_ge(cb, b + 1)
                        pe.transpose(bank(c, 0)[:, 0:P], ob, const(c, "ident")).then_inc(ot, 1)
                        pe.wait_ge(od, b + 1)

            @block.vector
            def _(dve):
                CHAIN = 6
                with dve.Fori(0, NB) as b:
                    n_chain = [0]

                    def settle(ins):
                        n_chain[0] += 1
                        ins.then_inc(vc, 1)
                        dve.wait_ge(vc, b * CHAIN + n_chain[0])

                    dve.tensor_copy(qb.rearrange("p (h t) -> p h t", h=HG), a.qT[:, :, ds(b * TS + TP, TS)])
                    dve.tensor_copy(knew.rearrange("p (n t) -> p n t", n=2), a.kvT[:, 2:6:2, ds(b * TS + TP, TS)])
                    dve.tensor_copy(kcb, a.kc[:, ds(b * 32 + 64, NCMPS)])
                    dve.tensor_copy(vcb[0:NCMPS, :], a.vcs[0:NCMPS, ds(b * P, P)])
                    dve.tensor_copy(vnb[0:TS, :], a.vnew[0:TS, ds(b * (2 * P), 2 * P)]).then_inc(qc, 1)
                    dve.wait_ge(kt_, b + 1)
                    dve.tensor_copy(kT, c.ps[:, 0:1024]).then_inc(ktc, 1)
                    dve.wait_ge(sc, b + 1)
                    dve.tensor_copy(sb[:, 0:PAST], bank(c, 2))
                    dve.tensor_tensor(sb[:, PAST:SK], bank(c, 4)[:, 0:TS], const(c, "s_new_add"), ALU.add)
                    dve.tensor_tensor(sb[:, SK:SK + TS], bank(c, 3)[:, 0:TS], const(c, "s_far_add"), ALU.add)
                    dve.tensor_copy(sb[:, SK + TS:SK + PAST], bank(c, 3)[:, TS:PAST])
                    dve.tensor_tensor(sb[:, SK + PAST:2 * SK], bank(c, 4)[:, TS:2 * TS], const(c, "s_new_add"), ALU.add)
                    settle(dve.tensor_copy(sb[:, 2 * SK:], bank(c, 4)[:, 2 * TS:2 * TS + NCMPS]))
                    for br, (o, n) in enumerate(RANGE):
                        ins = dve.tensor_reduce(nmax[:, br:br + 1], sb[:, o:o + n], AX.X, ALU.max, negate=True)
                    ins.then_inc(mx, 1)
                    dve.wait_ge(ex, b + 1)
                    settle(dve.reciprocal(rc, rsum))
                    settle(dve.tensor_tensor(coef, rc, a.sgates[:, ds(b * 3, 3)], ALU.mult))
                    for x in range(3):
                        dve.wait_ge(tr, b * 3 + x + 1)
                        ws = [w for *_, w in GR[x]]
                        lo = 0
                        while lo < len(ws):
                            hi = lo
                            while hi < len(ws) and ws[hi] == ws[lo]:
                                hi += 1
                            ins = dve.tensor_copy(pts[x % 2][0:ws[lo], lo * P:hi * P], bank(c, 5 + x % 2)[0:ws[lo], lo * P:hi * P])
                            lo = hi
                        ins.then_inc(ev, 1)
                    dve.wait_ge(pv, b + 2)
                    acc = bank(c, 7)
                    settle(dve.tensor_scalar(ob[:, 0:DH], acc[:, 0:DH], coef[:, 0:1], None, ALU.mult))
                    for br in (1, 2):
                        settle(dve.scalar_tensor_tensor(out=ob[:, 0:DH], in0=acc[:, br * DH:(br + 1) * DH], scalar=coef[:, br:br + 1],
                                                        in1=ob[:, 0:DH], op0=ALU.mult, op1=ALU.add))
                    dve.tensor_copy(ob[:, DH:P], ob[:, 0:DH]).then_inc(cb, 1)
                    dve.wait_ge(ot, b + 1)
                    xo = c.xn[:, :, ds(b * TS + TP, TS)]
                    dve.tensor_copy(xo[0:DH], bank(c, 0)[0:DH, 0:NS].rearrange("p (h t) -> p h t", h=HG))
                    dve.tensor_copy(xo[DH:P], bank(c, 0)[DH:P, NS:P].rearrange("p (h t) -> p h t", h=HG)).then_inc(od, 1)
                    assert n_chain[0] == CHAIN, n_chain

            @block.scalar
            def _(act):
                with act.Fori(0, NB) as b:
                    act.wait_ge(mx, b + 1)
                    for br, (o, n) in enumerate(RANGE):
                        ins = act.activation(pb[:, o:o + n], sb[:, o:o + n], ACT.Exp, bias=nmax[:, br:br + 1], accum_out=rsum[:, br:br + 1])
                    ins.then_inc(ex, 1)


def nsa_layer(c):
    norm_stage(c, 1, c.xn, 0)
    a = nsa_buffers(c)
    nsa_project(c, a)
    compress_stage(c, a, 0)
    compress_stage(c, a, 1)
    prompt_attention(c, a)
    sample_attention(c, a)
    c.at = a.free
    wb = [take(c, KD * P).rearrange("p (k f) -> p k f", k=KD) for _ in range(2)]
    w_out = c.io["nsa_w_out"][0]

    def src(m, j):
        return [(wb[j][g * DH:(g + 1) * DH, :, :],
                 w_out[g * 512:(g + 1) * 512, ds(m * P, P)].rearrange("(h d) f -> d h f", d=DH)) for g in range(2)]

    out_stage(c, KD, src, c.xn, wb)


def hybrid_decoder_kernel(nc, io):
    with ExitStack() as ctx:
        c = open_core(nc, ctx, io)
        load_stage(c)
        norm_stage(c, 0, c.xn, 0)
        gate_stage(c)
        gdn_stage(c)
        ffn_stages(c, 0)
        recycle_semaphores(c)
        nsa_layer(c)
        recycle_semaphores(c)
        ffn_stages(c, 1)
        final_stage(c)


_INS = ['x_prompt', 'x_sample', 'cache_nsa_kv', 'cache_nsa_win', 'state_gdn', 'state_gdn_conv', 'page_table',
        'norm1_w', 'norm2_w', 'final_norm_w', 'gdn_w_in', 'gdn_conv_w', 'gdn_A_log', 'gdn_dt_bias', 'gdn_norm_w', 'gdn_w_out',
        'nsa_w_in', 'nsa_pe_k', 'nsa_pe_v', 'nsa_cmp_w1_k', 'nsa_cmp_w2_k', 'nsa_cmp_w1_v', 'nsa_cmp_w2_v', 'nsa_w_out',
        'ffn_w_in', 'ffn_w_out']
_OUTS = [(1, 1024, 1024), (8, 8, 1024), (1, 1, 1024, 4, 2, 64), (1, 8, 8, 4, 2, 64), (1, 1, 512, 2, 2, 64),
         (1, 8, 512, 2, 2, 64), (1, 1, 8, 128, 128), (1, 8, 8, 128, 128), (1, 1, 3, 3072), (1, 8, 3, 3072)]


def kernel(**inputs):
    import concourse.bacc as _bacc
    from concourse.bass_utils import run_bass_kernel_spmd as _run

    nc = _bacc.Bacc("TRN2", target_bir_lowering=False, num_devices=1)
    arrays, io = {}, {}
    for name in _INS:
        a = np.ascontiguousarray(inputs[name])
        arrays[f"in_{name}_dram"] = a
        io[name] = nc.dram_tensor(f"in_{name}_dram", a.shape, mybir.dt.from_np(a.dtype), kind="ExternalInput").ap()
    table = const_table()
    arrays["in_consts_dram"] = table
    io["consts"] = nc.dram_tensor("in_consts_dram", table.shape, F32, kind="ExternalInput").ap()
    for i, shape in enumerate(_OUTS):
        io[f"out{i}"] = nc.dram_tensor(f"out_{i}_dram", shape, F32, kind="ExternalOutput").ap()
    hybrid_decoder_kernel(nc, io)
    r = _run(nc, [arrays], core_ids=[0])
    return tuple(r.results[0][f"out_{i}_dram"] for i in range(len(_OUTS)))
```

```python
from contextlib import ExitStack

import numpy as np

import concourse.bass as bass
from concourse import mybir

F32 = mybir.dt.float32
I32 = mybir.dt.int32
ALU = mybir.AluOpType
ACT = mybir.ActivationFunctionType
AX = mybir.AxisListType
ds = bass.ds

P = 128
D = 1024
KD = D // P
TP = 1024
NB, TS = 8, 8
NS = NB * TS
NT = TP + NS
HG = 8
NC = TP // P
QKV = 3 * HG * P
PAST = 512
DFF = 2816
KF = DFF // P
NH = 16
DH = 64
NPG = 4
NPHYS = 40
NCMP = 63
NCMPS = 31
EPS = 1e-6
NEG = -1e30
CH = [(0, 363), (363, 363), (726, 362)]

CONST = {}


def const_table():
    cols = []

    def add(name, a):
        a = np.asarray(a, np.float32)
        full = np.zeros((P, a.shape[1]), np.float32)
        full[:a.shape[0]] = a
        CONST[name] = (sum(c.shape[1] for c in cols), a.shape[1])
        cols.append(full)

    i = np.arange(P)[:, None]
    j = np.arange(P)[None, :]
    add("ident", i == j)
    add("ones", np.ones((P, P)))
    add("upper", i <= j)
    add("strict", i > j)
    i8, j8 = i[:NS], j[:, :NS]
    same = (i8 // TS) == (j8 // TS)
    add("upper_s", same & (i8 <= j8))
    add("strict_s", same & (i8 > j8))
    add("same_s", same)
    add("batch_s", (i8 // TS) == np.arange(NB)[None, :])
    for s in (1, 2, 4, 8, 16, 32, 64):
        m = (i // (2 * s) == j // (2 * s)) & (i // s % 2 == 1) & (j // s % 2 == 0)
        add(f"mt{s}", m.T)
        if s == 1:
            add("m1", m)
    add("causal_add", np.where(j <= i, 0, NEG))
    add("far_add", np.where(j >= i, 0, NEG))
    n = np.arange(64)[None, :]
    for qt in range(TP // P):
        add(f"cmp_add{qt}", np.where(16 * n + 31 <= qt * P + i, 0, NEG)[:, :NCMP])
    add("row_has_cmp", i >= 31)
    t = i % TS
    k8 = np.arange(TS)[None, :]
    add("s_new_add", np.where(k8 <= t, 0, NEG))
    add("s_far_add", np.where(k8 >= t, 0, NEG))
    add("eps", np.full((P, 1), EPS))
    add("eps_dk", np.full((P, 1), EPS * P))
    add("one", np.ones((P, 1)))
    return np.concatenate(cols, 1)


const_table()
NCONST = sum(w for _, w in CONST.values())


class Core:
    pass


def open_core(nc, ctx, io):
    c = Core()
    c.nc, c.io = nc, io
    c.n = 0
    c.open_sems = []

    def sb(name, cols):
        return ctx.enter_context(nc.sbuf_tensor(name, [P, cols], F32))

    c.ct = sb("consts", NCONST)
    c.xT = sb("xT", KD * NT)[:, :].rearrange("p (k t) -> p k t", k=KD)
    c.xn = sb("xn", KD * NT)[:, :].rearrange("p (k t) -> p k t", k=KD)
    c.xTf = c.xT.rearrange("p k t -> p (k t)")
    c.xnf = c.xn.rearrange("p k t -> p (k t)")
    c.normw = sb("normw", P)[:, :]
    c.convw = sb("convw", 96)[:, :]
    c.W = 32900
    c.work = sb("work", c.W)
    c.tail = c.W - 24 * 24 - 24 * 27 - 54 * HG
    o = c.tail
    c.convT = c.work[:, o:o + 576].rearrange("p (k n) -> p k n", k=24)
    c.newconv = c.work[:, o + 576:o + 576 + 648]
    c.par = c.work[:, o + 1224:o + 1224 + 54 * HG]
    c.ps = ctx.enter_context(nc.psum_tensor("ps", [P, 4096], F32))
    c.pages = ctx.enter_context(nc.sbuf_tensor("pages", [1, NB * NPG], I32))
    c.at = 0
    return c


def const(c, name):
    o, w = CONST[name]
    return c.ct[:, o:o + w]


def take(c, cols):
    a = c.work[:, c.at:c.at + cols]
    c.at += cols
    assert c.at <= c.W, c.at
    return a


def bank(c, b, n=1):
    return c.ps[:, 512 * b:512 * (b + n)]


def proj_acc(c, first):
    return [bank(c, first + b)[:, 0:n] for b, (_, n) in enumerate(CH)]


def proj_psum(c, slot):
    o = 1536 * slot
    return [c.ps[:, o + 512 * b:o + 512 * b + n] for b, (_, n) in enumerate(CH)]


def proj_parts(c, slot):
    o = 1536 * slot
    two = c.ps[:, o:o + 1024].rearrange("p (b n) -> p b n", b=2)[:, :, 0:CH[1][1]]
    return [(0, CH[2][0], two), (CH[2][0], CH[2][1], c.ps[:, o + 1024:o + 1024 + CH[2][1]])]


def like(a, acc):
    return a if len(acc.shape) == 2 else a.rearrange("p (b n) -> p b n", b=2)


def sems(nc, ctx, c, *names):
    c.n += 1
    new = [nc.alloc_semaphore(f"{n}_{c.n}") for n in names]
    c.open_sems += new
    return new


def recycle_semaphores(c):
    c.nc.all_engine_barrier()
    c.nc.clear_and_free_semaphores(c.open_sems)
    c.nc.all_engine_barrier()
    c.open_sems = []


def load_stage(c):
    nc, io = c.nc, c.io
    c.at = 0
    rows = take(c, 9 * D).rearrange("p (t d) -> p t d", t=9)
    cv = take(c, QKV)
    vec = take(c, 4 * P)
    with ExitStack() as ctx:
        ld, ldc, tr, ev, zero, cpy = sems(nc, ctx, c, "loaded", "consts_loaded", "turned", "evacuated", "zeroed", "zero2")
        with nc.Block() as block:
            @block.sync
            def _(sp):
                sp.dma_start(c.ct[:, :], io["consts"]).then_inc(ldc, 16)
                sp.dma_start(rows[:, 0:8, :], io["x_prompt"][0].rearrange("(t p) d -> p t d", p=P)).then_inc(ld, 16)
                sp.dma_start(rows[0:NS, 8, :], io["x_sample"].rearrange("b t d -> (b t) d")).then_inc(ld, 16)
                sp.dma_start(cv[0:24, :], io["state_gdn_conv"][0].rearrange("b r f -> (b r) f")).then_inc(ld, 16)
                sp.dma_start(c.pages[:, :], io["page_table"].rearrange("b (o n) -> o (b n)", o=1)).then_inc(ld, 16)
                sp.wait_ge(zero, 1)
                sp.dma_start(vec[0:16, 0:128], io["norm1_w"].rearrange("l (k p) -> (l k) p", p=P)).then_inc(ld, 16)
                sp.dma_start(vec[16:32, 0:128], io["norm2_w"].rearrange("l (k p) -> (l k) p", p=P)).then_inc(ld, 16)
                sp.dma_start(vec[32:40, 0:128], io["final_norm_w"].rearrange("(k p) -> k p", p=P)).then_inc(ld, 16)
                sp.dma_start(vec[40:41, 0:128], io["gdn_norm_w"]).then_inc(ld, 16)
                sp.dma_start(vec[0:96, 128:256], io["gdn_conv_w"][0].rearrange("r (k p) -> (r k) p", p=P)).then_inc(ld, 16)

            @block.gpsimd
            def _(pool):
                pool.memset(vec[:, :], 0.0).then_inc(zero, 1)

            jobs = [(rows[0:(P if t < 8 else NS), t, k * P:(k + 1) * P], c.xT[:, k, t * P:t * P + (P if t < 8 else NS)])
                    for t in range(9) for k in range(KD)]
            jobs += [(cv[0:24, k * P:(k + 1) * P], c.convT[:, k, :]) for k in range(24)]
            jobs += [(vec[:, 0:128], c.normw[:, :]), (vec[0:96, 128:256], c.convw[:, :])]

            @block.tensor
            def _(pe):
                pe.wait_ge(ldc, 16)
                pe.wait_ge(ld, 9 * 16)
                for n, (src, dst) in enumerate(jobs):
                    if n >= 8:
                        pe.wait_ge(ev, n - 7)
                    r = src.shape[0]
                    pe.transpose(bank(c, n % 8)[:, 0:r], src, const(c, "ident")[0:r, 0:r]).then_inc(tr, 1)

            @block.vector
            def _(dve):
                for n, (src, dst) in enumerate(jobs):
                    dve.wait_ge(tr, n + 1)
                    w = dst.shape[1]
                    dve.tensor_copy(dst, bank(c, n % 8)[:, 0:w]).then_inc(ev, 1)


def norm_stage(c, which, out, base):
    nc = c.nc
    c.at = base
    sq = take(c, 2 * NT).rearrange("p (s t) -> p s t", s=2)
    rt = take(c, NT)
    with ExitStack() as ctx:
        sqr, ss, root, inv, done = sems(nc, ctx, c, "squared", "summed", "rooted", "inverted", "normed")
        acc = proj_psum(c, 0)
        with nc.Block() as block:
            @block.scalar
            def _(act):
                for k in range(KD):
                    if k >= 2:
                        act.wait_ge(ss, k - 1)
                    act.activation(sq[:, k % 2, :], c.xT[:, k, :], ACT.Square).then_inc(sqr, 1)
                act.wait_ge(ss, KD)
                for (o, w), a in zip(CH, acc):
                    act.activation(rt[:, o:o + w], a, ACT.Sqrt, bias=const(c, "eps"), scale=1.0 / D).then_inc(root, 1)

            @block.tensor
            def _(pe):
                for k in range(KD):
                    pe.wait_ge(sqr, k + 1)
                    for n, ((o, w), a) in enumerate(zip(CH, acc)):
                        mm = pe.matmul(a, const(c, "ones"), sq[:, k % 2, o:o + w], start=(k == 0), stop=(k == KD - 1))
                    mm.then_inc(ss, 1)

            @block.vector
            def _(dve):
                dve.wait_ge(root, 3)
                dve.reciprocal(rt[:, :], rt[:, :]).then_inc(inv, 1)
                dve.wait_ge(inv, 1)
                for k in range(KD):
                    dve.scalar_tensor_tensor(out=out[:, k, :], in0=c.xT[:, k, :], scalar=c.normw[:, which * 8 + k:which * 8 + k + 1],
                                             in1=rt[:, :], op0=ALU.mult, op1=ALU.mult).then_inc(done, 1)


def mm_tile(pe, dst, w, rhs, nk):
    for (o, n), a in zip(CH, dst):
        for k in range(nk):
            mm = pe.matmul(a, w[:, k, :], rhs[:, k, o:o + n], start=(k == 0), stop=(k == nk - 1))
    return mm


def proj_stage(c, nk, tiles, src, rhs, wbuf, evac):
    nc = c.nc
    with ExitStack() as ctx:
        w0, w1, mm0, mm1, free0, free1 = sems(
            nc, ctx, c, "w0_loaded", "w1_loaded", "tile0_done", "tile1_done", "tile0_taken", "tile1_taken")
        wl, mmd, free = (w0, w1), (mm0, mm1), (free0, free1)
        npc = len(src(0, 0))
        with nc.Block() as block:
            @block.sync
            def _(sp):
                for j in range(2):
                    for dst, s in src(j, j):
                        sp.dma_start(dst, s).then_inc(wl[j], 16)
                with sp.Fori(0, tiles // 2 - 1) as i:
                    for j in range(2):
                        sp.wait_ge(mmd[j], i + 1)
                        for dst, s in src(2 * i + 2 + j, j):
                            sp.dma_start(dst, s).then_inc(wl[j], 16)

            @block.tensor
            def _(pe):
                with pe.Fori(0, tiles // 2) as i:
                    for j in range(2):
                        pe.wait_ge(wl[j], (i + 1) * (16 * npc))
                        pe.wait_ge(free[j], i * 2 + 1)
                        mm_tile(pe, proj_psum(c, j), wbuf[j], rhs, nk).then_inc(mmd[j], 1)

            @block.vector
            def _(dve):
                for j in range(2):
                    dve.sem_inc(free[j], 1)
                with dve.Fori(0, tiles // 2) as i:
                    for j in range(2):
                        dve.wait_ge(mmd[j], i + 1)
                        for ins in evac(dve, i * 2 + j, proj_parts(c, j)):
                            ins.then_inc(free[j], 1)


def out_stage(c, nk, src, rhs, wbuf):
    def evac(dve, m, parts):
        for o, n, acc in parts:
            x = like(c.xTf[:, ds(m * NT + o, n)], acc)
            yield dve.tensor_tensor(x, x, acc, ALU.add)

    proj_stage(c, nk, KD, src, rhs, wbuf, evac)


def ffn_stages(c, layer):
    nc, io = c.nc, c.io
    c.at = 0
    hid = take(c, KF * NT)
    hid3 = hid.rearrange("p (k t) -> p k t", k=KF)
    hbase = c.at
    norm_stage(c, 2 + layer, c.xn, 0)
    c.at = hbase
    sg = take(c, NT)
    wb = [take(c, KD * P).rearrange("p (k f) -> p k f", k=KD) for _ in range(4)]
    w_in = io["ffn_w_in"][layer].rearrange("(k p) f -> p k f", p=P)
    w_out = io["ffn_w_out"][layer].rearrange("(k p) f -> p k f", p=P)
    with ExitStack() as ctx:
        names = [f"{a}{j}" for a in ("gate_w_loaded", "up_w_loaded") for j in range(2)]
        gw0, gw1, uw0, uw1 = sems(nc, ctx, c, *names)
        gmm, umm, silu, prod = sems(nc, ctx, c, "gate_done", "up_done", "silu_done", "hidden_done")
        gw, uw = (gw0, gw1), (uw0, uw1)
        with nc.Block() as block:
            @block.sync
            def _(sp):
                for j in range(2):
                    sp.dma_start(wb[2 * j], w_in[:, :, j * P:(j + 1) * P]).then_inc(gw[j], 16)
                    sp.dma_start(wb[2 * j + 1], w_in[:, :, DFF + j * P:DFF + (j + 1) * P]).then_inc(uw[j], 16)
                with sp.Fori(0, KF // 2 - 1) as i:
                    for j in range(2):
                        sp.wait_ge(umm, i * 2 + j + 1)
                        o = (i + 1) * (2 * P) + j * P
                        sp.dma_start(wb[2 * j], w_in[:, :, ds(o, P)]).then_inc(gw[j], 16)
                        sp.dma_start(wb[2 * j + 1], w_in[:, :, ds(o + DFF, P)]).then_inc(uw[j], 16)

            @block.tensor
            def _(pe):
                with pe.Fori(0, KF // 2) as i:
                    for j in range(2):
                        pe.wait_ge(gw[j], (i + 1) * 16)
                        pe.wait_ge(silu, i * 4 + 2 * j + 1)
                        mm_tile(pe, proj_psum(c, 0), wb[2 * j], c.xn, KD).then_inc(gmm, 1)
                        pe.wait_ge(uw[j], (i + 1) * 16)
                        pe.wait_ge(prod, i * 4 + 2 * j + 1)
                        mm_tile(pe, proj_psum(c, 1), wb[2 * j + 1], c.xn, KD).then_inc(umm, 1)

            @block.scalar
            def _(act):
                act.sem_inc(silu, 1)
                with act.Fori(0, KF // 2) as i:
                    for j in range(2):
                        act.wait_ge(gmm, i * 2 + j + 1)
                        act.wait_ge(prod, i * 4 + 2 * j + 1)
                        for o, n, acc in proj_parts(c, 0):
                            act.activation(like(sg[:, o:o + n], acc), acc, ACT.Silu).then_inc(silu, 1)

            @block.vector
            def _(dve):
                dve.sem_inc(prod, 1)
                with dve.Fori(0, KF // 2) as i:
                    for j in range(2):
                        dve.wait_ge(umm, i * 2 + j + 1)
                        dve.wait_ge(silu, i * 4 + 2 * j + 3)
                        for o, n, acc in proj_parts(c, 1):
                            dve.tensor_tensor(like(hid[:, ds((i * 2 + j) * NT + o, n)], acc), like(sg[:, o:o + n], acc), acc,
                                              ALU.mult).then_inc(prod, 1)
    flat = c.xnf
    wo = [flat[:, j * KF * P:(j + 1) * KF * P].rearrange("p (k f) -> p k f", k=KF) for j in range(2)]
    out_stage(c, KF, lambda m, j: [(wo[j], w_out[:, :, ds(m * P, P)])], hid3, wo)


BETA, NBETA, GCUM, TAIL, ETOT, LOGA = range(6)
NPAR = 6 * 9


def gate_stage(c):
    nc, io = c.nc, c.io
    c.at = 0
    wba = take(c, KD * 16).rearrange("p (k f) -> p k f", k=KD)
    row = take(c, 16)
    ba = take(c, 144)
    t1, t2, t3 = take(c, 72), take(c, 72), take(c, 72)
    rb = take(c, 16)
    gs, tot = take(c, 72), take(c, 72)
    par = c.par.rearrange("p (h q c) -> p q c h", h=HG, q=6)
    ba3 = ba.rearrange("p (c n) -> p c n", c=9)

    def v(a):
        return a.rearrange("p (c h) -> p c h", c=9)

    with ExitStack() as ctx:
        ld, z, pm, step, a1, pg = sems(nc, ctx, c, "gate_inputs", "zeroed", "products", "vector_step", "scalar_step", "sums")
        with nc.Block() as block:
            @block.sync
            def _(sp):
                sp.dma_start(wba, io["gdn_w_in"][0].rearrange("(k p) f -> p k f", p=P)[:, :, 4096:4112]).then_inc(ld, 16)
                sp.dma_start(row[0:1, 0:8], io["gdn_dt_bias"]).then_inc(ld, 16)
                sp.dma_start(row[0:1, 8:16], io["gdn_A_log"]).then_inc(ld, 16)

            @block.gpsimd
            def _(pool):
                pool.memset(ba, 0.0).then_inc(z, 1)
                pool.memset(gs, 0.0).then_inc(z, 1)
                pool.memset(tot, 0.0).then_inc(z, 1)

            @block.tensor
            def _(pe):
                pe.wait_ge(ld, 48)
                for t in range(9):
                    n = P if t < 8 else NS
                    for k in range(KD):
                        pe.matmul(bank(c, 0)[0:n, 16 * t:16 * t + 16], c.xn[:, k, t * P:t * P + n], wba[:, k, :],
                                  start=(k == 0), stop=(k == KD - 1))
                pe.matmul(bank(c, 1)[:, 0:16], const(c, "ones")[0:1, :], row[0:1, :], start=True, stop=True).then_inc(pm, 1)
                pe.wait_ge(step, 8)
                la, las = t3[:, 0:64], t3[0:NS, 64:72]
                pe.matmul(bank(c, 2)[:, 0:64], const(c, "upper"), la, start=True, stop=True)
                pe.matmul(bank(c, 3)[0:NS, 0:8], const(c, "upper_s")[0:NS, :], las, start=True, stop=True)
                pe.matmul(bank(c, 4)[:, 0:64], const(c, "ones"), la, start=True, stop=True)
                pe.matmul(bank(c, 5)[0:NS, 0:8], const(c, "same_s")[0:NS, :], las, start=True, stop=True).then_inc(pg, 1)

            @block.scalar
            def _(act):
                act.wait_ge(step, 4)
                act.activation(par[:, BETA], ba3[:, :, 0:8], ACT.Sigmoid).then_inc(a1, 1)
                act.activation(rb[:, 8:16], rb[:, 8:16], ACT.Exp).then_inc(a1, 1)
                act.activation(t2, t2, ACT.Exp, scale=-1.0).then_inc(a1, 1)
                act.wait_ge(a1, 3)
                act.activation(t2, t2, ACT.Ln, bias=const(c, "one")).then_inc(a1, 1)
                act.wait_ge(step, 11)
                act.activation(par[:, TAIL], v(gs), ACT.Exp).then_inc(a1, 1)
                act.activation(par[:, ETOT], v(tot), ACT.Exp).then_inc(a1, 1)

            @block.vector
            def _(dve):
                dve.wait_ge(z, 3)
                dve.wait_ge(pm, 1)
                dve.tensor_copy(ba[:, 0:128], bank(c, 0)[:, 0:128])
                dve.tensor_copy(ba[0:NS, 128:144], bank(c, 0)[0:NS, 128:144])
                dve.tensor_copy(rb, bank(c, 1)[:, 0:16]).then_inc(step, 1)
                dve.wait_ge(step, 1)
                dve.tensor_tensor(v(t1), ba3[:, :, 8:16], rb[:, 0:8].rearrange("p (o h) -> p o h", o=1).to_broadcast([P, 9, 8]),
                                  ALU.add).then_inc(step, 1)
                dve.wait_ge(step, 2)
                dve.tensor_scalar(t3, t1, -1.0, None, ALU.mult).then_inc(step, 1)
                dve.wait_ge(step, 3)
                dve.tensor_tensor(t2, t1, t3, ALU.max).then_inc(step, 1)
                dve.tensor_scalar(t1, t1, 0.0, None, ALU.max).then_inc(step, 1)
                dve.wait_ge(a1, 4)
                dve.wait_ge(step, 5)
                dve.tensor_scalar(par[:, NBETA], par[:, BETA], -1.0, None, ALU.mult).then_inc(step, 1)
                dve.tensor_tensor(t1, t1, t2, ALU.add).then_inc(step, 1)
                dve.wait_ge(step, 7)
                dve.scalar_tensor_tensor(out=v(t3), in0=v(t1), scalar=-1.0,
                                         in1=rb[:, 8:16].rearrange("p (o h) -> p o h", o=1).to_broadcast([P, 9, 8]),
                                         op0=ALU.mult, op1=ALU.mult).then_inc(step, 1)
                dve.wait_ge(pg, 1)
                dve.wait_ge(step, 8)
                dve.tensor_copy(par[:, LOGA], v(t3))
                dve.tensor_copy(gs[:, 0:64], bank(c, 2)[:, 0:64])
                dve.tensor_copy(gs[0:NS, 64:72], bank(c, 3)[0:NS, 0:8])
                dve.tensor_copy(tot[:, 0:64], bank(c, 4)[:, 0:64])
                dve.tensor_copy(tot[0:NS, 64:72], bank(c, 5)[0:NS, 0:8]).then_inc(step, 1)
                dve.wait_ge(step, 9)
                dve.tensor_copy(par[:, GCUM], v(gs)).then_inc(step, 1)
                dve.wait_ge(step, 10)
                dve.tensor_tensor(gs, tot, gs, ALU.subtract).then_inc(step, 1)
                dve.wait_ge(a1, 6)


def gdn_stage(c):
    nc, io = c.nc, c.io
    c.at = 0
    w = [take(c, KD * P).rearrange("p (k f) -> p k f", k=KD) for _ in range(4)]
    yT = take(c, HG * NT)
    qkvz = [take(c, NT) for _ in range(4)]
    cin = [take(c, 3 + TP + NB * (3 + TS)) for _ in range(2)]
    sq, rt = take(c, NT), take(c, NT)
    s0 = take(c, NB * P)
    sn = take(c, NB * P)
    um = take(c, NB * P)
    parh, st0, st1, us, kst, cw, eb = take(c, NPAR), take(c, P), take(c, P), take(c, P), take(c, NS), take(c, 12), take(c, NB)
    kt, bv = take(c, 9 * P), take(c, 9 * P)
    assert c.at <= c.tail, c.at
    eg, e1, e2, lt, ml, x, xt, pp = [c.xTf[:, n * NT:(n + 1) * NT] for n in range(8)]
    park = nc.dram_tensor("parked_residual", (P, KD * NT), F32).ap()
    kT, qT, vT, zT = qkvz[1], qkvz[0], qkvz[2], qkvz[3]
    st = [st0, st1]
    w_in = io["gdn_w_in"][0].rearrange("(k p) f -> p k f", p=P)
    A, B, C, Dp = 0, 1024, 2048, 3072

    def par(q, n, height):
        return parh[0:height, q * 9 + n:q * 9 + n + 1]

    GROUPS = [dict(n=8, r=P, o=0, c0=0, up="upper", lo="strict", lv=(2, 4, 8, 16, 32, 64)),
              dict(n=1, r=NS, o=TP, c0=8, up="upper_s", lo="strict_s", lv=(2, 4))]
    NLV = 8

    def blk(a, g, k, height=None):
        return a[0:(height or g["r"]), g["o"] + k * g["r"]:g["o"] + (k + 1) * g["r"]]

    def tok(a, g, k):
        return a[0:g["r"], (g["c0"] + k) * P:(g["c0"] + k + 1) * P]

    def ps(base, g, k, height=None, width=None):
        width = width or g["r"]
        return c.ps[0:(height or g["r"]), base + k * width:base + (k + 1) * width]

    def grp(a, g):
        return a[0:g["r"], g["o"]:g["o"] + g["n"] * g["r"]].rearrange("p (n f) -> p n f", n=g["n"])

    def psg(base, g):
        return c.ps[0:g["r"], base:base + g["n"] * g["r"]].rearrange("p (n f) -> p n f", n=g["n"])

    def mask(name, g):
        m = const(c, name)[0:g["r"], 0:g["r"]]
        return m.rearrange("p (o f) -> p o f", o=1).to_broadcast([g["r"], g["n"], g["r"]])

    def norm_acc():
        return [bank(c, b)[:, 0:n] for b, (_, n) in zip((6, 7, 5), CH)]

    with ExitStack() as ctx:
        names = ["parked", "states_loaded", "states_stored", "state_out"] + [f"w{j}_loaded" for j in range(4)]
        (parked, s0l, sns, sto, *wl) = sems(nc, ctx, c, *names)
        (pj, pfree0, pfree1, hist, raw, conv, conved, sqd, ssd, rooted, normed, nconv) = sems(
            nc, ctx, c, "projected", "slot0_read", "slot1_read", "history_set", "raw_copied", "conv_done", "activated",
            "squared", "summed", "rooted", "normed", "conv_rows_kept")
        (p1, p2, p3, a1, v1, a2, v2, v3, mlr, pr, psr, yr, xr) = sems(
            nc, ctx, c, "turned_products", "query_key", "l_turned", "tail_keys", "differences", "decays", "l_and_scores",
            "x_begun", "l_masked", "p_product", "p_copied", "y_products", "x_updated")
        (ksr, rr, ur, usr, dsr, str_) = sems(nc, ctx, c, "key_state", "rhs_ready", "u_product", "u_copied", "state_product", "state_ready")
        (kss, kstc, kst2, rs, u2, us2, um2, o2, oc2, sn2) = sems(
            nc, ctx, c, "s_key_state", "s_copied", "s_turned", "s_rhs", "s_u", "s_u_copied", "s_u_spread", "s_out", "s_out_copied", "s_states")
        (oc, osq, oss, ort, yd, dc, pc) = sems(
            nc, ctx, c, "o_copied", "o_squared", "o_summed", "o_rooted", "y_done", "vector_chain", "params_copied")
        pfree = [pfree0, pfree1]
        with nc.Block() as block:
            @block.sync
            def _(sp):
                for s in (sto, sns):
                    sp.sem_inc(s, 1)
                sp.dma_start(park, c.xTf).then_inc(parked, 16)
                for j in range(4):
                    sp.dma_start(w[j], w_in[:, :, j * D:j * D + P]).then_inc(wl[j], 16)
                sp.dma_start(s0.rearrange("p (b v) -> p b v", b=NB), io["state_gdn"][0][:, 0].rearrange("b k v -> k b v")).then_inc(s0l, 16)
                sp.wait_ge(parked, 16)

                def head(i, more):
                    if more:
                        for j in range(4):
                            sp.wait_ge(pj, i * 4 + j + 1)
                            sp.dma_start(w[j], w_in[:, :, ds((i + 1) * P + j * D, P)]).then_inc(wl[j], 16)
                    sp.wait_ge(str_, i * 8 + 8)
                    sp.dma_start(io["out6"][0, 0][ds(i, 1)].rearrange("o k v -> k (o v)"), st[1]).then_inc(sto, 16)
                    sp.wait_ge(sn2, i + 1)
                    sp.dma_start(io["out7"][0][:, ds(i, 1)].rearrange("b o k v -> k (b o) v"),
                                 sn.rearrange("p (b v) -> p b v", b=NB)).then_inc(sns, 16)
                    if more:
                        sp.dma_start(s0.rearrange("p (b v) -> p b v", b=NB),
                                     io["state_gdn"][0][:, ds(i + 1, 1)].rearrange("b o k v -> k (b o) v")).then_inc(s0l, 16)

                with sp.Fori(0, HG - 1) as i:
                    head(i, True)
                head(HG - 1, False)
                sp.wait_ge(sto, 16 * HG + 1)
                sp.wait_ge(sns, 16 * HG + 1)

            @block.tensor
            def _(pe):
                pe.wait_ge(parked, 16)

                def alone():
                    pe.nop(nofuse=True)

                with pe.Fori(0, HG) as i:
                    pe.wait_ge(yd, i + 1)
                    for j in range(4):
                        pe.wait_ge(wl[j], (i + 1) * 16)
                        pe.wait_ge(pfree[j % 2], i * 4 + 2 * (j // 2) + 1)
                        mm_tile(pe, proj_psum(c, j % 2), w[j], c.xn, KD).then_inc(pj, 1)
                    for j in range(2):
                        pe.wait_ge(sqd, i * 2 + j + 1)
                        for (o, n), a in zip(CH, norm_acc()):
                            mm = pe.matmul(a, const(c, "ones"), sq[:, o:o + n], start=True, stop=True)
                        mm.then_inc(ssd, 1)
                    pe.wait_ge(normed, i * 2 + 2)
                    pe.wait_ge(conved, i * 3 + 3)
                    pe.wait_ge(pfree[1], i * 4 + 5)
                    pe.wait_ge(pc, i + 1)
                    alone()
                    for gi, g in enumerate(GROUPS):
                        n, r = g["n"], g["r"]
                        for k in range(n):
                            pe.transpose(ps(A, g, k, width=P), blk(kT, g, k, P), const(c, "ident"))
                        for k in range(n):
                            pe.transpose(ps(B, g, k, width=P), blk(vT, g, k, P), const(c, "ident"))
                        for k in range(n):
                            pe.matmul(ps(C, g, k, P), par(LOGA, g["c0"] + k, r).to_broadcast([r, P]), const(c, g["up"])[0:r, 0:r],
                                      start=True, stop=True)
                        for k in range(n):
                            mm = pe.matmul(ps(Dp, g, k), blk(kT, g, k, P), blk(kT, g, k, P), start=True, stop=True)
                        mm.then_inc(p1, 1)
                        pe.wait_ge(a1, i * 2 + gi + 1)
                        alone()
                        for k in range(n):
                            mm = pe.matmul(ps(A, g, k), blk(kT, g, k, P), blk(qT, g, k, P), start=True, stop=True)
                        mm.then_inc(p2, 1)
                        pe.wait_ge(v2, i * 2 + gi + 1)
                        alone()
                        for k in range(n):
                            mm = pe.transpose(ps(B, g, k), blk(e1, g, k), const(c, "ident")[0:r, 0:r])
                        mm.then_inc(p3, 1)
                        pe.wait_ge(v3, i * 2 + gi + 1)
                        for l, s in enumerate(g["lv"]):
                            q = i * NLV + 6 * gi + l
                            pe.wait_ge(mlr, q + 1)
                            if l:
                                pe.wait_ge(xr, q)
                            alone()
                            for k in range(n):
                                mm = pe.matmul(ps(C, g, k), blk(ml, g, k), blk(x, g, k), start=True, stop=True)
                            mm.then_inc(pr, 1)
                            pe.wait_ge(psr, q + 1)
                            alone()
                            for k in range(n):
                                pe.matmul(ps(Dp, g, k), blk(xt, g, k), blk(pp, g, k), start=True, stop=True)
                            for k in range(n):
                                mm = pe.matmul(ps(A, g, k), blk(pp, g, k), blk(xt, g, k), start=True, stop=True)
                            mm.then_inc(yr, 1)
                        pe.wait_ge(xr, i * NLV + 6 * gi + len(g["lv"]))
                        if gi == 0:
                            for k in range(n):
                                if k:
                                    pe.wait_ge(str_, i * 8 + k)
                                    pe.matmul(c.ps[:, A:A + P], blk(kT, g, k), st[(k - 1) % 2], start=True, stop=True).then_inc(ksr, 1)
                                    pe.matmul(ps(C, g, k), st[(k - 1) % 2], blk(qT, g, k), start=True, stop=False)
                                    pe.wait_ge(rr, i * 7 + k)
                                pe.matmul(c.ps[:, B:B + P], blk(xt, g, k), tok(bv, g, k), start=True, stop=True,
                                          skip_group_check=True).then_inc(ur, 1)
                                pe.wait_ge(usr, i * 8 + k + 1)
                                pe.matmul(ps(C, g, k), us, blk(e2, g, k), start=(k == 0), stop=True)
                                pe.matmul(c.ps[:, Dp:Dp + P], tok(kt, g, k), us, start=True, stop=True,
                                          skip_group_check=True).then_inc(dsr, 1)
                            pe.wait_ge(str_, i * 8 + 8)
                            pe.wait_ge(oc, i + 1)
                            alone()
                    g = GROUPS[1]
                    pe.wait_ge(s0l, (i + 1) * 16)
                    for b in range(NB):
                        mm = pe.matmul(c.ps[:, A + TS * b:A + TS * b + TS], s0[:, b * P:(b + 1) * P], kT[:, TP + TS * b:TP + TS * b + TS],
                                       start=True, stop=True)
                    mm.then_inc(kss, 1)
                    pe.wait_ge(kstc, i + 1)
                    alone()
                    pe.transpose(c.ps[0:NS, B:B + P], kst, const(c, "ident")).then_inc(kst2, 1)
                    pe.wait_ge(rs, i + 1)
                    alone()
                    pe.matmul(c.ps[0:NS, C:C + P], blk(xt, g, 0), tok(bv, g, 0), start=True, stop=True).then_inc(u2, 1)
                    pe.wait_ge(us2, i + 1)
                    alone()
                    pe.matmul(c.ps[:, Dp:Dp + NS], us[0:NS, :], blk(e2, g, 0), start=True, stop=False, skip_group_check=True)
                    for b in range(NB):
                        pe.matmul(c.ps[:, Dp + TS * b:Dp + TS * b + TS], s0[:, b * P:(b + 1) * P],
                                  qT[:, TP + TS * b:TP + TS * b + TS], start=False, stop=(b == NB - 1), skip_group_check=True)
                    pe.matmul(c.ps[:, Dp + 512:Dp + 512 + NB], par(LOGA, 8, NS).to_broadcast([NS, P]), const(c, "batch_s")[0:NS, :],
                              start=True, stop=True)
                    pe.wait_ge(um2, i + 1)
                    for hf in range(2):
                        mm = pe.matmul(c.ps[:, A + 512 * hf:A + 512 * hf + 512], tok(kt, g, 0), um[0:NS, 512 * hf:512 * hf + 512],
                                       start=True, stop=True)
                    mm.then_inc(o2, 1)
                    pe.wait_ge(osq, i + 1)
                    for (o, n), a in zip(CH, proj_acc(c, 2)):
                        mm = pe.matmul(a, const(c, "ones"), sq[:, o:o + n], start=True, stop=True)
                    mm.then_inc(oss, 1)

            def sview(a, lo, n):
                return a[:, 3 + TP:].rearrange("p (b t) -> p b t", b=NB)[:, :, lo:lo + n]

            @block.scalar
            def _(act):
                act.wait_ge(parked, 16)
                for s in pfree:
                    act.sem_inc(s, 1)
                with act.Fori(0, HG) as i:
                    for j in range(3):
                        act.wait_ge(pj, i * 4 + j + 1)
                        if j == 2:
                            act.wait_ge(conv, i * 3 + 2)
                            act.wait_ge(nconv, i * 3 + 1)
                        (_, n, acc), (o, _, acc2) = proj_parts(c, j % 2)
                        act.activation(like(cin[j % 2][:, 3:3 + n], acc), acc, ACT.Copy).then_inc(pfree[j % 2], 1)
                        act.activation(cin[j % 2][:, 3 + o:3 + TP], acc2[:, 0:TP - o], ACT.Copy)
                        act.activation(sview(cin[j % 2], 3, TS), acc2[:, TP - o:].rearrange("p (b t) -> p b t", b=NB), ACT.Copy).then_inc(pfree[j % 2], 1)
                    act.wait_ge(pj, i * 4 + 4)
                    for o, n, acc in proj_parts(c, 1):
                        act.activation(like(zT[:, o:o + n], acc), acc, ACT.Silu).then_inc(pfree[1], 1)
                    for j in range(3):
                        act.wait_ge(conv, i * 3 + j + 2)
                        act.activation(qkvz[j], qkvz[j], ACT.Silu).then_inc(conved, 1)
                    for j in range(2):
                        act.wait_ge(conved, i * 3 + j + 1)
                        if j:
                            act.wait_ge(ssd, i * 2 + j)
                        act.activation(sq, qkvz[j], ACT.Square).then_inc(sqd, 1)
                        act.wait_ge(ssd, i * 2 + j + 1)
                        if j:
                            act.wait_ge(normed, i * 2 + j)
                        for (o, n), a in zip(CH, norm_acc()):
                            act.activation(rt[:, o:o + n], a, ACT.Sqrt, bias=const(c, "eps_dk" if j == 0 else "eps"),
                                           scale=float(P) if j == 0 else 1.0).then_inc(rooted, 1)
                    for gi, g in enumerate(GROUPS):
                        act.wait_ge(p1, i * 2 + gi + 1)
                        act.wait_ge(pc, i + 1)
                        for k in range(g["n"]):
                            act.activation(tok(kt, g, k), ps(A, g, k, width=P), ACT.Copy, scale=par(TAIL, g["c0"] + k, g["r"]))
                        act.activation(eg[:, g["o"]:g["o"] + g["n"] * g["r"]], c.ps[:, C:C + g["n"] * g["r"]], ACT.Exp).then_inc(a1, 1)
                        act.wait_ge(v1, i * 2 + gi + 1)
                        act.activation(grp(e1, g), grp(e1, g), ACT.Exp, scale=-1.0)
                        act.activation(grp(e2, g), grp(e2, g), ACT.Exp).then_inc(a2, 1)
                        for l, s in enumerate(g["lv"]):
                            act.wait_ge(pr, i * NLV + 6 * gi + l + 1)
                            act.activation(grp(pp, g), psg(C, g), ACT.Copy).then_inc(psr, 1)
                        if gi == 0:
                            for k in range(g["n"]):
                                act.wait_ge(ur, i * 8 + k + 1)
                                act.activation(us, c.ps[:, B:B + P], ACT.Copy).then_inc(usr, 1)
                            act.wait_ge(dsr, i * 8 + 8)
                            act.activation(sq[:, 0:TP], c.ps[:, C:C + TP], ACT.Square)
                            act.activation(rt[:, 0:TP], c.ps[:, C:C + TP], ACT.Copy).then_inc(oc, 1)
                    act.wait_ge(kss, i + 1)
                    act.activation(kst, c.ps[:, A:A + NS], ACT.Copy).then_inc(kstc, 1)
                    act.wait_ge(u2, i + 1)
                    act.activation(us[0:NS, :], c.ps[0:NS, C:C + P], ACT.Copy).then_inc(us2, 1)
                    act.wait_ge(o2, i + 1)
                    act.activation(eb, c.ps[:, Dp + 512:Dp + 512 + NB], ACT.Exp)
                    act.activation(rt[:, TP:NT], c.ps[:, Dp:Dp + NS], ACT.Copy).then_inc(oc2, 1)
                    act.activation(sq[:, TP:NT], c.ps[:, Dp:Dp + NS], ACT.Square).then_inc(osq, 1)
                    act.wait_ge(oss, i + 1)
                    for (o, n), a in zip(CH, proj_acc(c, 2)):
                        act.activation(pp[:, o:o + n], a, ACT.Sqrt, bias=const(c, "eps"), scale=1.0 / P).then_inc(ort, 1)

            @block.vector
            def _(dve):
                dve.wait_ge(parked, 16)
                for s in (yd, conv):
                    dve.sem_inc(s, 1)
                CHAIN = 20
                with dve.Fori(0, HG) as i:
                    n_chain = [0]

                    def settle(ins):
                        n_chain[0] += 1
                        ins.then_inc(dc, 1)
                        dve.wait_ge(dc, i * CHAIN + n_chain[0])

                    settle(dve.tensor_copy(cw, c.convw[:, ds(i, 89)][:, 0:89:8]))
                    dve.tensor_copy(parh, c.par[:, ds(i * NPAR, NPAR)]).then_inc(pc, 1)
                    dve.wait_ge(pc, i + 1)
                    for j in range(3):
                        s = cin[j % 2]
                        dve.wait_ge(hist, i * 3 + j + 1)
                        dve.wait_ge(pfree[j % 2], i * 4 + 2 * (j // 2) + 3)
                        y = qkvz[j][:, 0:TP]
                        ys = qkvz[j][:, TP:NT].rearrange("p (b t) -> p b t", b=NB)
                        dve.tensor_scalar(y, s[:, 0:TP], cw[:, j:j + 1], None, ALU.mult)
                        settle(dve.tensor_scalar(ys, sview(s, 0, TS), cw[:, j:j + 1], None, ALU.mult))
                        for t in range(1, 4):
                            tap = cw[:, 3 * t + j:3 * t + j + 1]
                            dve.scalar_tensor_tensor(out=y, in0=s[:, t:t + TP], scalar=tap, in1=y, op0=ALU.mult, op1=ALU.add)
                            ins = dve.scalar_tensor_tensor(out=ys, in0=sview(s, t, TS), scalar=tap, in1=ys, op0=ALU.mult, op1=ALU.add)
                            if t < 3:
                                settle(ins)
                            else:
                                ins.then_inc(conv, 1)
                    for j in range(2):
                        dve.wait_ge(rooted, i * 6 + 3 * j + 3)
                        settle(dve.reciprocal(rt, rt))
                        dve.tensor_tensor(qkvz[j], qkvz[j], rt, ALU.mult).then_inc(normed, 1)
                    for gi, g in enumerate(GROUPS):
                        dve.wait_ge(p1, i * 2 + gi + 1)
                        for k in range(g["n"]):
                            q, r = g["c0"] + k, g["r"]
                            dve.tensor_scalar(tok(bv, g, k), ps(B, g, k, width=P), par(BETA, q, r), None, ALU.mult)
                        dve.wait_ge(a1, i * 2 + gi + 1)
                        for k in range(g["n"]):
                            q, r = g["c0"] + k, g["r"]
                            dve.tensor_scalar(blk(e1, g, k), ps(C, g, k), par(GCUM, q, r), 0.0, ALU.subtract, ALU.max)
                            ins = dve.tensor_scalar(blk(e2, g, k), ps(C, g, k), par(GCUM, q, r), 0.0, ALU.subtract, ALU.min)
                        ins.then_inc(v1, 1)
                        dve.wait_ge(a2, i * 2 + gi + 1)
                        dve.wait_ge(v1, i * 2 + gi + 1)
                        dve.tensor_tensor(grp(e1, g), grp(e1, g), mask(g["lo"], g), ALU.mult)
                        settle(dve.tensor_tensor(grp(e2, g), grp(e2, g), mask(g["up"], g), ALU.mult))
                        for k in range(g["n"]):
                            dve.scalar_tensor_tensor(out=blk(e1, g, k), in0=ps(Dp, g, k), scalar=par(BETA, g["c0"] + k, g["r"]),
                                                     in1=blk(e1, g, k), op0=ALU.mult, op1=ALU.mult)
                        dve.wait_ge(p2, i * 2 + gi + 1)
                        dve.tensor_tensor(grp(e2, g), psg(A, g), grp(e2, g), ALU.mult)
                        cols = slice(g["o"], g["o"] + g["n"] * g["r"])
                        dve.tensor_tensor(kT[:, cols], kT[:, cols], eg[:, cols], ALU.mult)
                        dve.tensor_tensor(qT[:, cols], qT[:, cols], eg[:, cols], ALU.mult).then_inc(v2, 1)
                        dve.wait_ge(v2, i * 2 + gi + 1)
                        dve.tensor_tensor(grp(x, g), grp(e1, g), mask("m1", g), ALU.mult)
                        dve.wait_ge(p3, i * 2 + gi + 1)
                        settle(dve.tensor_copy(grp(lt, g), psg(B, g)))
                        dve.tensor_tensor(grp(x, g), mask("ident", g), grp(x, g), ALU.subtract)
                        settle(dve.tensor_tensor(grp(xt, g), grp(lt, g), mask("mt1", g), ALU.mult))
                        dve.tensor_tensor(grp(xt, g), mask("ident", g), grp(xt, g), ALU.subtract).then_inc(v3, 1)
                        dve.wait_ge(v3, i * 2 + gi + 1)
                        for l, s in enumerate(g["lv"]):
                            dve.wait_ge(yr, i * NLV + 6 * gi + l + 1)
                            dve.tensor_tensor(grp(x, g), grp(x, g), psg(Dp, g), ALU.subtract)
                            dve.tensor_tensor(grp(xt, g), grp(xt, g), psg(A, g), ALU.subtract).then_inc(xr, 1)
                            dve.wait_ge(xr, i * NLV + 6 * gi + l + 1)
                        if gi == 0:
                            for k in range(8):
                                if k:
                                    dve.wait_ge(ksr, i * 7 + k)
                                    dve.scalar_tensor_tensor(out=tok(bv, g, k), in0=c.ps[:, A:A + P], scalar=par(NBETA, k, P),
                                                             in1=tok(bv, g, k), op0=ALU.mult, op1=ALU.add).then_inc(rr, 1)
                                dve.wait_ge(dsr, i * 8 + k + 1)
                                if k == 0:
                                    dve.wait_ge(sto, i * 16 + 1)
                                    dve.tensor_copy(st[0], c.ps[:, Dp:Dp + P]).then_inc(str_, 1)
                                else:
                                    dve.wait_ge(str_, i * 8 + k)
                                    dve.scalar_tensor_tensor(out=st[k % 2], in0=st[(k - 1) % 2], scalar=par(ETOT, k, P),
                                                             in1=c.ps[:, Dp:Dp + P], op0=ALU.mult, op1=ALU.add).then_inc(str_, 1)
                    g = GROUPS[1]
                    dve.wait_ge(kst2, i + 1)
                    dve.scalar_tensor_tensor(out=tok(bv, g, 0), in0=c.ps[0:NS, B:B + P], scalar=par(NBETA, 8, NS),
                                             in1=tok(bv, g, 0), op0=ALU.mult, op1=ALU.add).then_inc(rs, 1)
                    dve.wait_ge(us2, i + 1)
                    dve.tensor_tensor(um[0:NS, :].rearrange("p (b v) -> p b v", b=NB),
                                      us[0:NS, :].rearrange("p (o v) -> p o v", o=1).to_broadcast([NS, NB, P]),
                                      const(c, "batch_s")[0:NS, :].rearrange("p (b o) -> p b o", o=1).to_broadcast([NS, NB, P]),
                                      ALU.mult).then_inc(um2, 1)
                    dve.wait_ge(oc2, i + 1)
                    dve.wait_ge(sns, i * 16 + 1)
                    for b in range(NB):
                        ins = dve.scalar_tensor_tensor(out=sn[:, b * P:(b + 1) * P], in0=s0[:, b * P:(b + 1) * P], scalar=eb[:, b:b + 1],
                                                       in1=c.ps[:, A + P * b:A + P * b + P], op0=ALU.mult, op1=ALU.add)
                    ins.then_inc(sn2, 1)
                    dve.wait_ge(ort, i * 3 + 3)
                    dve.wait_ge(oc, i + 1)
                    settle(dve.reciprocal(pp, pp))
                    settle(dve.tensor_tensor(rt, rt, pp, ALU.mult))
                    dve.scalar_tensor_tensor(out=yT[:, ds(i * NT, NT)], in0=rt, scalar=c.normw[:, 40:41], in1=zT,
                                             op0=ALU.mult, op1=ALU.mult).then_inc(yd, 1)
                    assert n_chain[0] == CHAIN, n_chain

            @block.gpsimd
            def _(pool):
                pool.wait_ge(parked, 16)
                for s in cin:
                    ins = pool.memset(s[:, 0:3], 0.0)
                with pool.Fori(0, HG) as i:
                    for j in range(3):
                        s = cin[j % 2]
                        tile = i + j * 8
                        if j == 2:
                            pool.wait_ge(conv, i * 3 + 2)
                        else:
                            pool.wait_ge(conv, i * 3 + 1)
                        pool.tensor_copy(sview(s, 0, 3),
                                         c.convT.rearrange("p k n -> p (k n)")[:, ds(tile * 24, 24)].rearrange("p (b r) -> p b r", b=NB)
                                         ).then_inc(hist, 1)
                        pool.wait_ge(pfree[j % 2], i * 4 + 2 * (j // 2) + 3)
                        pool.tensor_copy(c.newconv[:, ds(tile * 27, 3)], s[:, TP:TP + 3])
                        pool.tensor_copy(c.newconv[:, ds(tile * 27 + 3, 24)].rearrange("p (b r) -> p b r", b=NB),
                                         sview(s, TS, 3)).then_inc(nconv, 1)
                    for gi, g in enumerate(GROUPS):
                        pool.wait_ge(v3, i * 2 + gi + 1)
                        for l, s in enumerate(g["lv"]):
                            if l:
                                pool.wait_ge(pr, i * NLV + 6 * gi + l)
                            pool.tensor_tensor(grp(ml, g), grp(lt, g), mask(f"mt{s}", g), ALU.mult).then_inc(mlr, 1)

    conv_rows = take(c, QKV)
    with ExitStack() as ctx:
        back, tr, ev, st_ = sems(nc, ctx, c, "residual_back", "turned", "evacuated", "conv_stored")
        with nc.Block() as block:
            @block.sync
            def _(sp):
                sp.dma_start(c.xTf, park).then_inc(back, 16)
                sp.wait_ge(ev, 24)
                sp.dma_start(io["out8"][0, 0], conv_rows[0:3, :]).then_inc(st_, 16)
                sp.dma_start(io["out9"][0].rearrange("b r f -> (b r) f"), conv_rows[3:27, :]).then_inc(st_, 16)
                sp.wait_ge(st_, 32)
                sp.wait_ge(back, 16)

            @block.tensor
            def _(pe):
                for n in range(24):
                    if n >= 8:
                        pe.wait_ge(ev, n - 7)
                    pe.transpose(bank(c, n % 8)[0:27, 0:P], c.newconv[:, n * 27:(n + 1) * 27], const(c, "ident")).then_inc(tr, 1)

            @block.vector
            def _(dve):
                for n in range(24):
                    dve.wait_ge(tr, n + 1)
                    dve.tensor_copy(conv_rows[0:27, n * P:(n + 1) * P], bank(c, n % 8)[0:27, 0:P]).then_inc(ev, 1)

    wo = [conv_rows[:, j * 1024:(j + 1) * 1024].rearrange("p (k f) -> p k f", k=KD) for j in range(2)]
    w_out = io["gdn_w_out"][0].rearrange("(k p) f -> p k f", p=P)
    out_stage(c, KD, lambda m, j: [(wo[j], w_out[:, :, ds(m * P, P)])], yT.rearrange("p (k t) -> p k t", k=HG), wo)


def final_stage(c):
    nc, io = c.nc, c.io
    norm_stage(c, 4, c.xn, 0)
    c.at = 0
    rows = take(c, 9 * D).rearrange("p (t d) -> p t d", t=9)
    jobs = [(t, k) for t in range(9) for k in range(KD)]
    with ExitStack() as ctx:
        tr, ev, st_ = sems(nc, ctx, c, "turned", "evacuated", "rows_stored")
        with nc.Block() as block:
            @block.tensor
            def _(pe):
                for n, (t, k) in enumerate(jobs):
                    if n >= 8:
                        pe.wait_ge(ev, n - 7)
                    r = P if t < 8 else NS
                    pe.transpose(bank(c, n % 8)[0:r, 0:P], c.xn[:, k, t * P:t * P + r], const(c, "ident")).then_inc(tr, 1)

            @block.vector
            def _(dve):
                for n, (t, k) in enumerate(jobs):
                    dve.wait_ge(tr, n + 1)
                    r = P if t < 8 else NS
                    dve.tensor_copy(rows[0:r, t, k * P:(k + 1) * P], bank(c, n % 8)[0:r, 0:P]).then_inc(ev, 1)

            @block.sync
            def _(sp):
                for t in range(9):
                    sp.wait_ge(ev, 8 * t + 8)
                    if t < 8:
                        sp.dma_start(io["out0"][0, t * P:(t + 1) * P, :], rows[:, t, :]).then_inc(st_, 16)
                    else:
                        sp.dma_start(io["out1"].rearrange("b t d -> (b t) d"), rows[0:NS, t, :]).then_inc(st_, 16)
                sp.wait_ge(st_, 9 * 16)


class Nsa:
    pass


def nsa_buffers(c):
    c.at = 0
    a = Nsa()
    a.qTf = take(c, HG * NT)
    a.qT = a.qTf.rearrange("p (k t) -> p k t", k=HG)
    a.kvT = take(c, 6 * NT).rearrange("p (k t) -> p k t", k=6)
    a.rows = take(c, 9 * 6 * P).rearrange("p (t f) -> p t f", t=9)
    a.gates = take(c, 9 * 48).rearrange("p (t f) -> p t f", t=9)
    a.kc = take(c, 320)
    a.vcp = take(c, P)
    a.vcs = take(c, NB * P)
    a.vnew = take(c, NB * 2 * P)
    a.sgates = take(c, NB * 3)
    a.free = c.at
    return a


def nsa_project(c, a):
    nc, io = c.nc, c.io
    c.at = a.free
    w_in = io["nsa_w_in"][0].rearrange("(k p) f -> p k f", p=P)
    wb = [take(c, KD * P).rearrange("p (k f) -> p k f", k=KD) for _ in range(2)]
    wg = take(c, KD * 48).rearrange("p (k f) -> p k f", k=KD)

    def q_src(m, j):
        return [(wb[j][:, :, g * DH:(g + 1) * DH], w_in[:, :, ds(m * DH + g * HG * DH, DH)]) for g in range(2)]

    def q_evac(dve, m, parts):
        for o, n, acc in parts:
            yield dve.tensor_scalar(like(a.qTf[:, ds(m * NT + o, n)], acc), acc, DH ** -0.5, None, ALU.mult)

    proj_stage(c, KD, HG, q_src, c.xn, wb, q_evac)
    kvf = a.kvT.rearrange("p k t -> p (k t)")

    def kv_evac(dve, m, parts):
        for o, n, acc in parts:
            yield dve.tensor_copy(like(kvf[:, ds(m * NT + o, n)], acc), acc)

    proj_stage(c, KD, 6, lambda m, j: [(wb[j], w_in[:, :, ds(m * P + D, P)])], c.xn, wb, kv_evac)

    park = nc.dram_tensor("decode_gates", (NS, 48), F32).ap()
    jobs = [(t, k) for t in range(9) for k in range(6)]
    with ExitStack() as ctx:
        wl, gm, gd, tr, ev, gst, vn, st = sems(nc, ctx, c, "gate_w_loaded", "gates_multiplied", "gates_done", "turned", "evacuated",
                                               "gates_parked", "new_rows_placed", "rows_stored")
        with nc.Block() as block:
            @block.sync
            def _(sp):
                sp.dma_start(wg, w_in[:, :, 1792:1840]).then_inc(wl, 16)
                sp.dma_start(io["out5"][0].rearrange("b r k g d -> b r (k g d)")[:, 0:PAST - TS],
                             io["cache_nsa_win"][0].rearrange("b r k g d -> b r (k g d)")[:, TS:PAST]).then_inc(st, 16)
                sp.wait_ge(gd, 2)
                sp.dma_start(park, a.gates[0:NS, 8, :]).then_inc(gst, 16)
                sp.wait_ge(gst, 16)
                for gh in range(NH):
                    sp.dma_start(a.sgates[gh * TS:(gh + 1) * TS, :].rearrange("t (b r) -> t b r", b=NB),
                                 park[:, gh * 3:gh * 3 + 3].rearrange("(b t) r -> t b r", b=NB)).then_inc(vn, 16)
                sp.wait_ge(ev, len(jobs))
                for b in range(NB):
                    for n, k in enumerate((3, 5)):
                        o = (b * 2 + n) * P
                        sp.dma_start(a.vnew[0:TS, o:o + P], a.rows[b * TS:(b + 1) * TS, 8, k * P:(k + 1) * P]).then_inc(vn, 16)
                sp.dma_start(io["out2"][0, 0].rearrange("(t p) k g d -> p t (k g d)", p=P), a.rows[:, 0:8, 0:512]).then_inc(st, 16)
                sp.dma_start(io["out3"][0].rearrange("b t k g d -> (b t) (k g d)"), a.rows[0:NS, 8, 0:512]).then_inc(st, 16)
                sp.dma_start(io["out4"][0, 0].rearrange("(t p) k g d -> p t (k g d)", p=P), a.rows[:, 4:8, 512:768]).then_inc(st, 16)
                for b in range(NB):
                    sp.dma_start(io["out5"][0, b].rearrange("r k g d -> r (k g d)")[PAST - TS:PAST],
                                 a.rows[b * TS:(b + 1) * TS, 8, 512:768]).then_inc(st, 16)
                sp.wait_ge(st, 16 * (4 + NB))
                sp.wait_ge(vn, 16 * (NH + 2 * NB))

            @block.tensor
            def _(pe):
                pe.wait_ge(wl, 16)
                for t in range(9):
                    n = P if t < 8 else NS
                    for k in range(KD):
                        mm = pe.matmul(bank(c, 0)[0:n, 48 * t:48 * t + 48], c.xn[:, k, t * P:t * P + n], wg[:, k, :],
                                       start=(k == 0), stop=(k == KD - 1))
                mm.then_inc(gm, 1)
                for n, (t, k) in enumerate(jobs):
                    if n >= 7:
                        pe.wait_ge(ev, n - 6)
                    r = P if t < 8 else NS
                    pe.transpose(bank(c, 1 + n % 7)[0:r, 0:P], a.kvT[:, k, t * P:t * P + r], const(c, "ident")).then_inc(tr, 1)

            @block.scalar
            def _(act):
                act.wait_ge(gm, 1)
                act.activation(a.gates[:, 0:8, :], bank(c, 0)[:, 0:384].rearrange("p (t f) -> p t f", t=8), ACT.Sigmoid).then_inc(gd, 1)
                act.activation(a.gates[0:NS, 8, :], bank(c, 0)[0:NS, 384:432], ACT.Sigmoid).then_inc(gd, 1)

            @block.vector
            def _(dve):
                for n, (t, k) in enumerate(jobs):
                    dve.wait_ge(tr, n + 1)
                    r = P if t < 8 else NS
                    dve.tensor_copy(a.rows[0:r, t, k * P:(k + 1) * P], bank(c, 1 + n % 7)[0:r, 0:P]).then_inc(ev, 1)


def compress_stage(c, a, kind):
    nc, io = c.nc, c.io
    c.at = a.free
    pastT = take(c, NB * PAST + 32)
    hid = take(c, 4 * 320).rearrange("p (n m) -> p n m", n=4)
    w2 = take(c, 2 * DH).rearrange("p (n f) -> p n f", n=2)
    ring = take(c, 8 * P).rearrange("p (s f) -> p s f", s=8)
    pe_rows, bias = take(c, P), take(c, 4)
    w1 = c.xnf[:, 0:8192].rearrange("p (l f) -> p l f", l=32)
    name = "kv"[kind]
    w1_d = io[f"nsa_cmp_w1_{name}"][0].rearrange("(l d) f -> d l f", d=DH)
    w2_d = io[f"nsa_cmp_w2_{name}"][0].rearrange("(n p) f -> p n f", p=P)
    pool_d = io["cache_nsa_kv"][0].rearrange("n p k g d -> n p k (g d)")
    PIECES = 4
    LP = 32 // PIECES
    with ExitStack() as ctx:
        wl = sems(nc, ctx, c, *[f"w1_piece{q}_loaded" for q in range(PIECES)])
        pgl = sems(nc, ctx, c, *[f"page{q}_loaded" for q in range(8)])
        w2l, pel, tr, ev, pt, hm, bc, hd, om, od, z = sems(
            nc, ctx, c, "w2_loaded", "positions_loaded", "pages_turned", "pages_kept", "positions_turned", "hidden_product", "bias_copied",
            "hidden_done", "out_product", "out_copied", "pad_zeroed")
        with nc.Block() as block:
            @block.sync
            def _(sp):
                sp.dma_start(w2, w2_d).then_inc(w2l, 16)
                for g in range(2):
                    sp.dma_start(pe_rows[0:32, g * DH:(g + 1) * DH], io[f"nsa_pe_{name}"][0]).then_inc(pel, 16)
                for q in range(PIECES):
                    for g in range(2):
                        sp.dma_start(w1[g * DH:(g + 1) * DH, q * LP:(q + 1) * LP, :], w1_d[:, q * LP:(q + 1) * LP, :]).then_inc(wl[q], 16)

            @block.gpsimd
            def _(pool):
                pool.memset(hid[:, :, 63:64], 0.0).then_inc(z, 1)
                pool.sem_inc(ev, 1)
                with pool.Fori(0, 4) as i:
                    for s in range(8):
                        page = pool.value_load(c.pages[0:1, ds(i * 8 + s, 1)], min_val=0, max_val=NPHYS - 1)
                        pool.wait_ge(ev, i * 8 + 1)
                        pool.dma_start(ring[:, s, :], pool_d[ds(page, 1), :, kind, :].rearrange("o p f -> p (o f)")).then_inc(pgl[s], 16)

            @block.tensor
            def _(pe):
                pe.wait_ge(pel, 32)
                pe.transpose(bank(c, 7)[:, 0:32], pe_rows[0:32, :], const(c, "ident")[0:32, 0:32]).then_inc(pt, 1)
                with pe.Fori(0, 4) as i:
                    for s in range(8):
                        pe.wait_ge(pgl[s], i * 16 + 16)
                        if s % 4 == 0:
                            pe.wait_ge(ev, i * 8 + 1)
                        pe.transpose(bank(c, s // 4)[:, (s % 4) * P:(s % 4 + 1) * P], ring[:, s, :], const(c, "ident")).then_inc(tr, 1)
                pe.wait_ge(ev, 34)
                for l in range(32):
                    if l % LP == 0:
                        pe.wait_ge(wl[l // LP], 32)
                    for g in range(2):
                        rows = slice(g * DH, (g + 1) * DH)
                        for hf in range(2):
                            b = (g * 2 + hf) * 2
                            wt = w1[rows, l, hf * P:(hf + 1) * P]
                            pe.matmul(bank(c, b)[:, 0:NCMP], wt, a.kvT[rows, kind, l:l + 16 * (NCMP - 1) + 1:16], start=(l == 0), stop=(l == 31))
                            mm = pe.matmul(bank(c, b + 1)[:, 0:257], wt, pastT[rows, l:l + 16 * 256 + 1:16], start=(l == 0), stop=(l == 31))
                mm.then_inc(hm, 1)
                pe.wait_ge(hd, 1)
                pe.wait_ge(w2l, 16)
                pe.wait_ge(z, 1)
                if kind == 0:
                    for g in range(2):
                        for hf in range(2):
                            mm = pe.matmul(bank(c, 0)[g * DH:(g + 1) * DH, 0:320], w2[:, hf, :], hid[:, g * 2 + hf, :],
                                           start=(hf == 0), stop=(hf == 1))
                    mm.then_inc(om, 1)
                else:
                    for n in range(9):
                        m, o = (NCMP, 0) if n == 0 else (NCMPS, 64 + 32 * (n - 1))
                        for g in range(2):
                            for hf in range(2):
                                mm = pe.matmul(c.ps[0:m, 512 * (n // 4) + (n % 4) * P + g * DH:512 * (n // 4) + (n % 4) * P + (g + 1) * DH],
                                               hid[:, g * 2 + hf, o:o + m], w2[:, hf, :], start=(hf == 0), stop=(hf == 1))
                    mm.then_inc(om, 1)

            @block.vector
            def _(dve):
                with dve.Fori(0, 4) as i:
                    for s in range(8):
                        dve.wait_ge(tr, i * 8 + (s // 4 * 4 + 4))
                        dve.tensor_copy(pastT[:, ds(i * 1024 + s * P, P)], bank(c, s // 4)[:, (s % 4) * P:(s % 4 + 1) * P]).then_inc(ev, 1)
                dve.wait_ge(pt, 1)
                dve.tensor_copy(pastT[:, NB * PAST:], bank(c, 7)[:, 0:32]).then_inc(ev, 1)
                dve.wait_ge(hm, 1)
                for n in range(4):
                    ins = dve.tensor_copy(bias[:, n:n + 1], bank(c, 2 * n + 1)[:, 256:257])
                ins.then_inc(bc, 1)
                dve.wait_ge(om, 1)
                if kind == 0:
                    dve.tensor_copy(a.kc, bank(c, 0)[:, 0:320]).then_inc(od, 1)
                else:
                    dve.tensor_copy(a.vcp[0:NCMP, :], c.ps[0:NCMP, 0:P])
                    dve.tensor_copy(a.vcs[0:NCMPS, 0:3 * P], c.ps[0:NCMPS, P:4 * P])
                    dve.tensor_copy(a.vcs[0:NCMPS, 3 * P:], c.ps[0:NCMPS, 4 * P:9 * P]).then_inc(od, 1)

            @block.scalar
            def _(act):
                act.wait_ge(bc, 1)
                for n in range(4):
                    act.activation(hid[:, n, 0:NCMP], bank(c, 2 * n)[:, 0:NCMP], ACT.Silu, bias=bias[:, n:n + 1])
                    ins = act.activation(hid[:, n, 64:320], bank(c, 2 * n + 1)[:, 0:256], ACT.Silu, bias=bias[:, n:n + 1])
                ins.then_inc(hd, 1)


def prompt_attention(c, a):
    nc = c.nc
    c.at = a.free
    qs = [a.kvT[:, n, 0:TP] for n in range(2)]
    pr = [take(c, 1024 + 640 + 64) for _ in range(2)]
    pts = [take(c, 512) for _ in range(2)]
    ot = [take(c, P) for _ in range(2)]
    nmax, rsum, rc, coef = take(c, 6), take(c, 6), take(c, 6), take(c, 6)
    QT = TP // P
    UNITS = [(i, g) for i in range(QT) for g in range(2)]
    NU = len(UNITS)
    NHALF = 2 * NU

    def blocks(k):
        i, g = UNITS[k // 2]
        w0 = max(0, i - 4)
        if k % 2 == 0:
            return [("s", n, 128 * n, P) for n in range(i + 1)]
        return [("w", n, 1024 + 128 * (n - w0), P) for n in range(w0, i + 1)] + [("c", 0, 1664, NCMP)]

    FLOW = []
    for k in range(NHALF):
        bl = blocks(k)
        FLOW += [(k, bl[n:n + 4]) for n in range(0, len(bl), 4)]
        if k % 4 == 1 and k > 4:
            FLOW.append(((k - 5) // 4, None))
    FLOW.append((QT - 1, None))
    NF = len(FLOW)
    taken = [x for x in range(NF) if FLOW[x][1]]
    outs = [x for x in range(NF) if not FLOW[x][1]]
    NT_, NO = len(taken), len(outs)
    S, W = 0, 1024

    with ExitStack() as ctx:
        qc, sc, mx, ex, tr, kept, okept, pv, cb, dc, mc = sems(
            nc, ctx, c, "queries_copied", "scores_done", "maxima_ready", "probs_ready", "group_turned", "group_kept", "output_kept",
            "unit_multiplied", "combined", "vector_chain", "masked")

        with nc.Block() as block:
            @block.tensor
            def _(pe):
                def scores(t, k):
                    i, g = UNITS[k // 2]
                    q = qs[g][:, i * P:(i + 1) * P]
                    w0, n = (max(0, i - 4), i + 1) if k % 2 else (0, i + 1)
                    base, tile = (W, 4) if k % 2 else (S, 2)
                    cols = (n - w0) * P
                    for o in range(0, cols, 512):
                        m = min(512, cols - o)
                        mm = pe.matmul(c.ps[:, base + o:base + o + m], q, a.kvT[:, tile, w0 * P + o:w0 * P + o + m], start=True, stop=True)
                    if k % 2:
                        mm = pe.matmul(c.ps[:, W + 640:W + 640 + NCMP], q, a.kc[:, 0:NCMP], start=True, stop=True)
                    mm.then_inc(sc, 1)

                def products(t, x):
                    k, gr = FLOW[x]
                    if gr is None:
                        return
                    u, g = k // 2, UNITS[k // 2][1]
                    o = c.ps[:, 3072 + 512 * (u % 2):3072 + 512 * (u % 2) + 384]
                    pe.wait_ge(kept, t * NT_ + taken.index(x) + 1)
                    for m, b in enumerate(gr):
                        kind, kb, col, w = b
                        same = [y for y in blocks(k) if y[0] == kind]
                        br = "csw".index(kind)
                        v = a.vcp[0:NCMP, :] if kind == "c" else a.rows[:, kb, 384:512] if kind == "s" else a.rows[:, kb, 640:768]
                        mm = pe.matmul(o[:, br * P:(br + 1) * P], pts[x % 2][0:w, m * P:(m + 1) * P], v, start=(b == same[0]), stop=(b == same[-1]))
                    if k % 2 and gr[-1][0] == "c":
                        mm.then_inc(pv, 1)

                with pe.Fori(0, HG) as t:
                    pe.wait_ge(qc, t + 1)
                    scores(t, 0)
                    scores(t, 1)
                    for x, (k, gr) in enumerate(FLOW):
                        turned = c.ps[:, 2048 + 512 * (x % 2):2048 + 512 * (x % 2) + 512]
                        if gr is None:
                            if x == NF - 1:
                                products(t, x - 1)
                            pe.wait_ge(cb, t * NU + 2 * k + 2)
                            pe.transpose(turned[:, 0:P], ot[k % 2], const(c, "ident")).then_inc(tr, 1)
                            if x < NF - 1:
                                products(t, x - 1)
                            continue
                        if gr[0] == blocks(k)[0]:
                            pe.wait_ge(ex, t * NHALF + k + 1)
                            if k + 2 < NHALF:
                                scores(t, k + 2)
                        if x >= 2 and FLOW[x - 2][1] is None:
                            pe.wait_ge(okept, t * NO + outs.index(x - 2) + 1)
                        if gr[0][0] == "c":
                            pe.nop(nofuse=True)
                        for m, (kind, kb, col, w) in enumerate(gr):
                            mm = pe.transpose(turned[0:w, m * P:(m + 1) * P], pr[(k // 2) % 2][:, col:col + w], const(c, "ident"))
                        mm.then_inc(tr, 1)
                        if gr[0] == blocks(k)[0] and k % 2 == 0 and k >= 4:
                            pe.wait_ge(cb, t * NU + k // 2 - 1)
                        if x:
                            products(t, x - 1)

            @block.scalar
            def _(act):
                def exps(t, k):
                    i, g = UNITS[k // 2]
                    p = pr[(k // 2) % 2]
                    o = 3 * ((k // 2) % 2)
                    act.wait_ge(mx, t * NHALF + k + 1)
                    if k % 2:
                        n = i + 1 - max(0, i - 4)
                        act.activation(p[:, 1664:1664 + NCMP], c.ps[:, W + 640:W + 640 + NCMP], ACT.Exp, bias=nmax[:, o:o + 1], accum_out=rsum[:, o:o + 1])
                        act.activation(p[:, 1024:1024 + n * P], c.ps[:, W:W + n * P], ACT.Exp, bias=nmax[:, o + 2:o + 3],
                                       accum_out=rsum[:, o + 2:o + 3]).then_inc(ex, 1)
                    else:
                        n = i + 1
                        act.activation(p[:, 0:n * P], c.ps[:, S:S + n * P], ACT.Exp, bias=nmax[:, o + 1:o + 2], accum_out=rsum[:, o + 1:o + 2]).then_inc(ex, 1)

                with act.Fori(0, HG) as t:
                    exps(t, 0)
                    exps(t, 1)
                    for k in range(NHALF):
                        for x in range(NF):
                            if FLOW[x][1] is None or FLOW[x][0] != k:
                                continue
                            gr = FLOW[x][1]
                            act.wait_ge(tr, t * NF + x + 1)
                            src = c.ps[:, 2048 + 512 * (x % 2):2048 + 512 * (x % 2) + 512]
                            full = len(gr) - (gr[-1][0] == "c")
                            if full:
                                ins = act.activation(pts[x % 2][:, 0:full * P], src[:, 0:full * P], ACT.Copy)
                            if full < len(gr):
                                cols = slice(full * P, (full + 1) * P)
                                ins = act.activation(pts[x % 2][0:NCMP, cols], src[0:NCMP, cols], ACT.Copy)
                            ins.then_inc(kept, 1)
                        if k + 2 < NHALF:
                            exps(t, k + 2)

            @block.vector
            def _(dve):
                def maxima(t, k):
                    i, g = UNITS[k // 2]
                    o = 3 * ((k // 2) % 2)
                    dve.wait_ge(sc, t * NHALF + k + 1)
                    if k % 2:
                        n = i + 1 - max(0, i - 4)
                        d = c.ps[:, W + (n - 1) * P:W + n * P]
                        dve.tensor_tensor(d, d, const(c, "causal_add"), ALU.add)
                        if i >= 4:
                            d = c.ps[:, W:W + P]
                            dve.tensor_tensor(d, d, const(c, "far_add"), ALU.add)
                        d = c.ps[:, W + 640:W + 640 + NCMP]
                        dve.tensor_tensor(d, d, const(c, f"cmp_add{i}"), ALU.add).then_inc(mc, 1)
                        dve.wait_ge(mc, t * NHALF + k + 1)
                        dve.tensor_reduce(nmax[:, o:o + 1], d, AX.X, ALU.max, negate=True)
                        dve.tensor_reduce(nmax[:, o + 2:o + 3], c.ps[:, W:W + n * P], AX.X, ALU.max, negate=True).then_inc(mx, 1)
                    else:
                        n = i + 1
                        d = c.ps[:, S + i * P:S + n * P]
                        dve.tensor_tensor(d, d, const(c, "causal_add"), ALU.add).then_inc(mc, 1)
                        dve.wait_ge(mc, t * NHALF + k + 1)
                        dve.tensor_reduce(nmax[:, o + 1:o + 2], c.ps[:, S:S + n * P], AX.X, ALU.max, negate=True).then_inc(mx, 1)

                CHAIN = 4 * NU + 2
                dve.memset(qs[0][DH:P, :], 0.0)
                dve.memset(qs[1][0:DH, :], 0.0)
                with dve.Fori(0, HG) as t:
                    n_chain = [0]

                    def settle(ins):
                        n_chain[0] += 1
                        ins.then_inc(dc, 1)
                        dve.wait_ge(dc, t * CHAIN + n_chain[0])

                    def coefficients(u):
                        i, g = UNITS[u]
                        o = 3 * (u % 2)
                        dve.wait_ge(ex, t * NHALF + 2 * u + 2)
                        settle(dve.reciprocal(rc[:, o:o + 3], rsum[:, o:o + 3]))
                        ins = dve.tensor_tensor(coef[:, o:o + 3], rc[:, o:o + 3],
                                                a.gates.rearrange("p t f -> p (t f)")[:, ds(t * 3 + (i * 48 + g * 24), 3)], ALU.mult)
                        if u == 0 or u == 1:
                            settle(ins)
                            ins = dve.tensor_tensor(coef[:, o:o + 1], coef[:, o:o + 1], const(c, "row_has_cmp"), ALU.mult)
                        settle(ins)

                    def combine(u):
                        i, g = UNITS[u]
                        o = 3 * (u % 2)
                        dve.wait_ge(pv, t * NU + u + 1)
                        out = ot[i % 2][:, g * DH:(g + 1) * DH]
                        acc = [c.ps[:, 3072 + 512 * (u % 2) + br * P + g * DH:3072 + 512 * (u % 2) + br * P + (g + 1) * DH] for br in range(3)]
                        settle(dve.tensor_scalar(out, acc[0], coef[:, o:o + 1], None, ALU.mult))
                        settle(dve.scalar_tensor_tensor(out=out, in0=acc[1], scalar=coef[:, o + 1:o + 2], in1=out, op0=ALU.mult, op1=ALU.add))
                        dve.scalar_tensor_tensor(out=out, in0=acc[2], scalar=coef[:, o + 2:o + 3], in1=out,
                                                 op0=ALU.mult, op1=ALU.add).then_inc(cb, 1)

                    def keep_output(x):
                        i = FLOW[x][0]
                        dve.wait_ge(tr, t * NF + x + 1)
                        dve.tensor_copy(c.xnf[:, ds(t * NT + i * P, P)], c.ps[:, 2048 + 512 * (x % 2):2048 + 512 * (x % 2) + P]).then_inc(okept, 1)

                    dve.tensor_copy(qs[0][0:DH, :], a.qTf[0:DH, ds(t * NT, TP)])
                    dve.tensor_copy(qs[1][DH:P, :], a.qTf[DH:P, ds(t * NT, TP)]).then_inc(qc, 1)
                    maxima(t, 0)
                    maxima(t, 1)
                    for k in range(NHALF):
                        if k + 2 < NHALF:
                            maxima(t, k + 2)
                        if k % 2:
                            coefficients(k // 2)
                        elif k >= 2:
                            combine(k // 2 - 1)
                        if k % 4 == 1 and k > 4:
                            keep_output(outs[(k - 5) // 4])
                    combine(NU - 1)
                    keep_output(outs[-1])
                    assert n_chain[0] == 4 * NU + 2, n_chain


def sample_attention(c, a):
    nc, io = c.nc, c.io
    c.at = a.free
    SK = PAST + TS
    kv = [take(c, NPG * 2 * P).rearrange("p (n f) -> p n f", n=NPG) for _ in range(2)]
    wn = take(c, NPG * 2 * P).rearrange("p (n f) -> p n f", n=NPG)
    kT = take(c, 2 * PAST)
    qb, knew, kcb, vcb, vnb = take(c, NS), take(c, 2 * TS), take(c, NCMPS), take(c, P), take(c, 2 * P)
    pts = [take(c, 512) for _ in range(2)]
    small = take(c, 12)
    nmax, rsum, rc, coef = [small[:, 3 * n:3 * n + 3] for n in range(4)]
    ob = take(c, P)
    dead = a.kvT[:, 0:2, :].rearrange("p k t -> p (k t)")
    sb = dead[:, 0:2 * SK + NCMPS]
    pb = dead[:, 2 * SK + NCMPS:2 * (2 * SK + NCMPS)] if 2 * (2 * SK + NCMPS) <= 2 * NT else take(c, 2 * SK + NCMPS)
    pool_d = io["cache_nsa_kv"][0].rearrange("n p k g d -> n p (k g d)")
    win_d = io["cache_nsa_win"][0].rearrange("b (n p) k g d -> b p n (k g d)", p=P)
    BL = [("s", n, 128 * n, P) for n in range(4)] + [("s", 4, PAST, TS)]
    BL += [("w", n, SK + 128 * n, P) for n in range(4)] + [("w", 4, SK + PAST, TS)] + [("c", 0, 2 * SK, NCMPS)]
    GR = [BL[0:4], BL[4:8], BL[8:11]]
    RANGE = [(2 * SK, NCMPS), (0, SK), (SK, SK)]

    with ExitStack() as ctx:
        kl0, kl1, wnl, kt_, ktc, qc, sc, scp, mx, ex, cf, tr, ev, pv, cb, ot, od, vc, used = sems(
            nc, ctx, c, "pages0_loaded", "pages1_loaded", "window_loaded", "keys_turned", "keys_copied", "inputs_copied", "scores_done",
            "scores_copied", "maxima_ready", "probs_ready", "coefficients", "probs_turned", "turned_kept", "outputs_done", "combined",
            "out_turned", "out_kept", "vector_chain", "rows_used")
        kl = [kl0, kl1]
        with nc.Block() as block:
            @block.gpsimd
            def _(pool):
                pool.sem_inc(pv, 1)
                with pool.Fori(0, NB // 2) as i:
                    for j in range(2):
                        pool.wait_ge(pv, i * 2 + 1)
                        for n in range(NPG):
                            page = pool.value_load(c.pages[0:1, ds(i * 8 + j * 4 + n, 1)], min_val=0, max_val=NPHYS - 1)
                            pool.dma_start(kv[j][:, n, :], pool_d[ds(page, 1), :, 256:512].rearrange("o p f -> p (o f)")).then_inc(kl[j], 16)

            @block.sync
            def _(sp):
                sp.dma_start(wn, win_d[0]).then_inc(wnl, 16)
                with sp.Fori(0, NB - 1) as b:
                    sp.wait_ge(pv, b + 2)
                    sp.dma_start(wn, win_d[ds(b + 1, 1)].rearrange("o p n f -> p (o n) f")).then_inc(wnl, 16)

            def product(pe, j, b, x):
                pe.wait_ge(ev, b * 3 + x + 1)
                pe.nop(nofuse=True)
                for m, (kind, n, col, w) in enumerate(GR[x]):
                    br = "csw".index(kind)
                    for g in range(2):
                        f = slice(g * DH, (g + 1) * DH)
                        if kind == "c":
                            v = vcb[0:NCMPS, f]
                        elif n == 4:
                            v = vnb[0:TS, "sw".index(kind) * P + g * DH:"sw".index(kind) * P + (g + 1) * DH]
                        else:
                            v = (kv[j] if kind == "s" else wn)[:, n, P + g * DH:P + (g + 1) * DH]
                        mm = pe.matmul(bank(c, 7)[f, br * DH:(br + 1) * DH], pts[x % 2][0:w, m * P + g * DH:m * P + (g + 1) * DH], v,
                                       start=(n == 0), stop=(n == 4 or kind == "c"), skip_group_check=True)
                return mm

            @block.tensor
            def _(pe):
                with pe.Fori(0, NB // 2) as i:
                    for j in range(2):
                        b = i * 2 + j
                        pe.wait_ge(kl[j], i * 64 + 64)
                        for n in range(NPG):
                            pe.transpose(bank(c, 0)[:, n * P:(n + 1) * P], kv[j][:, n, 0:P], const(c, "ident"))
                        pe.wait_ge(wnl, b * 16 + 16)
                        for n in range(NPG):
                            mm = pe.transpose(bank(c, 1)[:, n * P:(n + 1) * P], wn[:, n, 0:P], const(c, "ident"))
                        mm.then_inc(kt_, 1)
                        pe.wait_ge(ktc, b + 1)
                        pe.wait_ge(qc, b + 1)
                        pe.nop(nofuse=True)
                        for g in range(2):
                            rows = slice(g * DH, (g + 1) * DH)
                            for n in range(2):
                                pe.matmul(bank(c, 2 + n)[rows, :], qb[rows, :], kT[rows, n * PAST:(n + 1) * PAST], start=True, stop=True)
                            pe.matmul(bank(c, 4)[rows, 0:2 * TS], qb[rows, :], knew[rows, :], start=True, stop=True)
                            mm = pe.matmul(bank(c, 4)[rows, 2 * TS:2 * TS + NCMPS], qb[rows, :], kcb[rows, :], start=True, stop=True)
                        mm.then_inc(sc, 1)
                        pe.wait_ge(ex, b + 1)
                        pe.nop(nofuse=True)
                        for x, gr in enumerate(GR):
                            if x == 2:
                                pe.wait_ge(ev, b * 3 + 1)
                                pe.nop(nofuse=True)
                            for m, (kind, n, col, w) in enumerate(gr):
                                mm = pe.transpose(bank(c, 5 + x % 2)[0:w, m * P:(m + 1) * P], pb[:, col:col + w], const(c, "ident"))
                            mm.then_inc(tr, 1)
                            if x:
                                product(pe, j, b, x - 1)
                        product(pe, j, b, 2).then_inc(pv, 1)
                        pe.wait_ge(cb, b + 1)
                        pe.transpose(bank(c, 0)[:, 0:P], ob, const(c, "ident")).then_inc(ot, 1)
                        pe.wait_ge(od, b + 1)

            @block.vector
            def _(dve):
                CHAIN = 6
                with dve.Fori(0, NB) as b:
                    n_chain = [0]

                    def settle(ins):
                        n_chain[0] += 1
                        ins.then_inc(vc, 1)
                        dve.wait_ge(vc, b * CHAIN + n_chain[0])

                    dve.tensor_copy(qb.rearrange("p (h t) -> p h t", h=HG), a.qT[:, :, ds(b * TS + TP, TS)])
                    dve.tensor_copy(knew.rearrange("p (n t) -> p n t", n=2), a.kvT[:, 2:6:2, ds(b * TS + TP, TS)])
                    dve.tensor_copy(kcb, a.kc[:, ds(b * 32 + 64, NCMPS)])
                    dve.tensor_copy(vcb[0:NCMPS, :], a.vcs[0:NCMPS, ds(b * P, P)])
                    dve.tensor_copy(vnb[0:TS, :], a.vnew[0:TS, ds(b * (2 * P), 2 * P)]).then_inc(qc, 1)
                    dve.wait_ge(kt_, b + 1)
                    dve.tensor_copy(kT, c.ps[:, 0:1024]).then_inc(ktc, 1)
                    dve.wait_ge(sc, b + 1)
                    dve.tensor_copy(sb[:, 0:PAST], bank(c, 2))
                    dve.tensor_tensor(sb[:, PAST:SK], bank(c, 4)[:, 0:TS], const(c, "s_new_add"), ALU.add)
                    dve.tensor_tensor(sb[:, SK:SK + TS], bank(c, 3)[:, 0:TS], const(c, "s_far_add"), ALU.add)
                    dve.tensor_copy(sb[:, SK + TS:SK + PAST], bank(c, 3)[:, TS:PAST])
                    dve.tensor_tensor(sb[:, SK + PAST:2 * SK], bank(c, 4)[:, TS:2 * TS], const(c, "s_new_add"), ALU.add)
                    settle(dve.tensor_copy(sb[:, 2 * SK:], bank(c, 4)[:, 2 * TS:2 * TS + NCMPS]))
                    for br, (o, n) in enumerate(RANGE):
                        ins = dve.tensor_reduce(nmax[:, br:br + 1], sb[:, o:o + n], AX.X, ALU.max, negate=True)
                    ins.then_inc(mx, 1)
                    dve.wait_ge(ex, b + 1)
                    settle(dve.reciprocal(rc, rsum))
                    settle(dve.tensor_tensor(coef, rc, a.sgates[:, ds(b * 3, 3)], ALU.mult))
                    for x in range(3):
                        dve.wait_ge(tr, b * 3 + x + 1)
                        ws = [w for *_, w in GR[x]]
                        lo = 0
                        while lo < len(ws):
                            hi = lo
                            while hi < len(ws) and ws[hi] == ws[lo]:
                                hi += 1
                            ins = dve.tensor_copy(pts[x % 2][0:ws[lo], lo * P:hi * P], bank(c, 5 + x % 2)[0:ws[lo], lo * P:hi * P])
                            lo = hi
                        ins.then_inc(ev, 1)
                    dve.wait_ge(pv, b + 2)
                    acc = bank(c, 7)
                    settle(dve.tensor_scalar(ob[:, 0:DH], acc[:, 0:DH], coef[:, 0:1], None, ALU.mult))
                    for br in (1, 2):
                        settle(dve.scalar_tensor_tensor(out=ob[:, 0:DH], in0=acc[:, br * DH:(br + 1) * DH], scalar=coef[:, br:br + 1],
                                                        in1=ob[:, 0:DH], op0=ALU.mult, op1=ALU.add))
                    dve.tensor_copy(ob[:, DH:P], ob[:, 0:DH]).then_inc(cb, 1)
                    dve.wait_ge(ot, b + 1)
                    xo = c.xn[:, :, ds(b * TS + TP, TS)]
                    dve.tensor_copy(xo[0:DH], bank(c, 0)[0:DH, 0:NS].rearrange("p (h t) -> p h t", h=HG))
                    dve.tensor_copy(xo[DH:P], bank(c, 0)[DH:P, NS:P].rearrange("p (h t) -> p h t", h=HG)).then_inc(od, 1)
                    assert n_chain[0] == CHAIN, n_chain

            @block.scalar
            def _(act):
                with act.Fori(0, NB) as b:
                    act.wait_ge(mx, b + 1)
                    for br, (o, n) in enumerate(RANGE):
                        ins = act.activation(pb[:, o:o + n], sb[:, o:o + n], ACT.Exp, bias=nmax[:, br:br + 1], accum_out=rsum[:, br:br + 1])
                    ins.then_inc(ex, 1)


def nsa_layer(c):
    norm_stage(c, 1, c.xn, 0)
    a = nsa_buffers(c)
    nsa_project(c, a)
    compress_stage(c, a, 0)
    compress_stage(c, a, 1)
    prompt_attention(c, a)
    sample_attention(c, a)
    c.at = a.free
    wb = [take(c, KD * P).rearrange("p (k f) -> p k f", k=KD) for _ in range(2)]
    w_out = c.io["nsa_w_out"][0]

    def src(m, j):
        return [(wb[j][g * DH:(g + 1) * DH, :, :],
                 w_out[g * 512:(g + 1) * 512, ds(m * P, P)].rearrange("(h d) f -> d h f", d=DH)) for g in range(2)]

    out_stage(c, KD, src, c.xn, wb)


def hybrid_decoder_kernel(nc, io):
    with ExitStack() as ctx:
        c = open_core(nc, ctx, io)
        load_stage(c)
        norm_stage(c, 0, c.xn, 0)
        gate_stage(c)
        gdn_stage(c)
        ffn_stages(c, 0)
        recycle_semaphores(c)
        nsa_layer(c)
        recycle_semaphores(c)
        ffn_stages(c, 1)
        final_stage(c)


_INS = ['x_prompt', 'x_sample', 'cache_nsa_kv', 'cache_nsa_win', 'state_gdn', 'state_gdn_conv', 'page_table',
        'norm1_w', 'norm2_w', 'final_norm_w', 'gdn_w_in', 'gdn_conv_w', 'gdn_A_log', 'gdn_dt_bias', 'gdn_norm_w', 'gdn_w_out',
        'nsa_w_in', 'nsa_pe_k', 'nsa_pe_v', 'nsa_cmp_w1_k', 'nsa_cmp_w2_k', 'nsa_cmp_w1_v', 'nsa_cmp_w2_v', 'nsa_w_out',
        'ffn_w_in', 'ffn_w_out']
_OUTS = [(1, 1024, 1024), (8, 8, 1024), (1, 1, 1024, 4, 2, 64), (1, 8, 8, 4, 2, 64), (1, 1, 512, 2, 2, 64),
         (1, 8, 512, 2, 2, 64), (1, 1, 8, 128, 128), (1, 8, 8, 128, 128), (1, 1, 3, 3072), (1, 8, 3, 3072)]


def kernel(**inputs):
    import concourse.bacc as _bacc
    from concourse.bass_utils import run_bass_kernel_spmd as _run

    nc = _bacc.Bacc("TRN2", target_bir_lowering=False, num_devices=1)
    arrays, io = {}, {}
    for name in _INS:
        a = np.ascontiguousarray(inputs[name])
        arrays[f"in_{name}_dram"] = a
        io[name] = nc.dram_tensor(f"in_{name}_dram", a.shape, mybir.dt.from_np(a.dtype), kind="ExternalInput").ap()
    table = const_table()
    arrays["in_consts_dram"] = table
    io["consts"] = nc.dram_tensor("in_consts_dram", table.shape, F32, kind="ExternalInput").ap()
    for i, shape in enumerate(_OUTS):
        io[f"out{i}"] = nc.dram_tensor(f"out_{i}_dram", shape, F32, kind="ExternalOutput").ap()
    hybrid_decoder_kernel(nc, io)
    r = _run(nc, [arrays], core_ids=[0])
    return tuple(r.results[0][f"out_{i}_dram"] for i in range(len(_OUTS)))
```

```python
from contextlib import ExitStack

import numpy as np

import concourse.bass as bass
from concourse import mybir

F32 = mybir.dt.float32
I32 = mybir.dt.int32
ALU = mybir.AluOpType
ACT = mybir.ActivationFunctionType
AX = mybir.AxisListType
ds = bass.ds

P = 128
D = 1024
KD = D // P
TP = 1024
NB, TS = 8, 8
NS = NB * TS
NT = TP + NS
HG = 8
NC = TP // P
QKV = 3 * HG * P
PAST = 512
DFF = 2816
KF = DFF // P
NH = 16
DH = 64
NPG = 4
NPHYS = 40
NCMP = 63
NCMPS = 31
EPS = 1e-6
NEG = -1e30
CH = [(0, 363), (363, 363), (726, 362)]

CONST = {}


def const_table():
    cols = []

    def add(name, a):
        a = np.asarray(a, np.float32)
        full = np.zeros((P, a.shape[1]), np.float32)
        full[:a.shape[0]] = a
        CONST[name] = (sum(c.shape[1] for c in cols), a.shape[1])
        cols.append(full)

    i = np.arange(P)[:, None]
    j = np.arange(P)[None, :]
    add("ident", i == j)
    add("ones", np.ones((P, P)))
    add("upper", i <= j)
    add("strict", i > j)
    i8, j8 = i[:NS], j[:, :NS]
    same = (i8 // TS) == (j8 // TS)
    add("upper_s", same & (i8 <= j8))
    add("strict_s", same & (i8 > j8))
    add("same_s", same)
    add("batch_s", (i8 // TS) == np.arange(NB)[None, :])
    for s in (1, 2, 4, 8, 16, 32, 64):
        m = (i // (2 * s) == j // (2 * s)) & (i // s % 2 == 1) & (j // s % 2 == 0)
        add(f"mt{s}", m.T)
        if s == 1:
            add("m1", m)
    add("causal_add", np.where(j <= i, 0, NEG))
    add("far_add", np.where(j >= i, 0, NEG))
    n = np.arange(64)[None, :]
    for qt in range(TP // P):
        add(f"cmp_add{qt}", np.where(16 * n + 31 <= qt * P + i, 0, NEG)[:, :NCMP])
    add("row_has_cmp", i >= 31)
    t = i % TS
    k8 = np.arange(TS)[None, :]
    add("s_new_add", np.where(k8 <= t, 0, NEG))
    add("s_far_add", np.where(k8 >= t, 0, NEG))
    add("eps", np.full((P, 1), EPS))
    add("eps_dk", np.full((P, 1), EPS * P))
    add("one", np.ones((P, 1)))
    return np.concatenate(cols, 1)


const_table()
NCONST = sum(w for _, w in CONST.values())


class Core:
    pass


def open_core(nc, ctx, io):
    c = Core()
    c.nc, c.io = nc, io
    c.n = 0
    c.open_sems = []

    def sb(name, cols):
        return ctx.enter_context(nc.sbuf_tensor(name, [P, cols], F32))

    c.ct = sb("consts", NCONST)
    c.xT = sb("xT", KD * NT)[:, :].rearrange("p (k t) -> p k t", k=KD)
    c.xn = sb("xn", KD * NT)[:, :].rearrange("p (k t) -> p k t", k=KD)
    c.xTf = c.xT.rearrange("p k t -> p (k t)")
    c.xnf = c.xn.rearrange("p k t -> p (k t)")
    c.normw = sb("normw", P)[:, :]
    c.convw = sb("convw", 96)[:, :]
    c.W = 32900
    c.work = sb("work", c.W)
    c.tail = c.W - 24 * 24 - 24 * 27 - 54 * HG
    o = c.tail
    c.convT = c.work[:, o:o + 576].rearrange("p (k n) -> p k n", k=24)
    c.newconv = c.work[:, o + 576:o + 576 + 648]
    c.par = c.work[:, o + 1224:o + 1224 + 54 * HG]
    c.ps = ctx.enter_context(nc.psum_tensor("ps", [P, 4096], F32))
    c.pages = ctx.enter_context(nc.sbuf_tensor("pages", [1, NB * NPG], I32))
    c.at = 0
    return c


def const(c, name):
    o, w = CONST[name]
    return c.ct[:, o:o + w]


def take(c, cols):
    a = c.work[:, c.at:c.at + cols]
    c.at += cols
    assert c.at <= c.W, c.at
    return a


def bank(c, b, n=1):
    return c.ps[:, 512 * b:512 * (b + n)]


def proj_acc(c, first):
    return [bank(c, first + b)[:, 0:n] for b, (_, n) in enumerate(CH)]


def proj_psum(c, slot):
    o = 1536 * slot
    return [c.ps[:, o + 512 * b:o + 512 * b + n] for b, (_, n) in enumerate(CH)]


def proj_parts(c, first):
    o = 512 * first
    two = c.ps[:, o:o + 1024].rearrange("p (b n) -> p b n", b=2)[:, :, 0:CH[1][1]]
    return [(0, CH[2][0], two), (CH[2][0], CH[2][1], c.ps[:, o + 1024:o + 1024 + CH[2][1]])]


def like(a, acc):
    return a if len(acc.shape) == 2 else a.rearrange("p (b n) -> p b n", b=2)


def sems(nc, ctx, c, *names):
    c.n += 1
    new = [nc.alloc_semaphore(f"{n}_{c.n}") for n in names]
    c.open_sems += new
    return new


def recycle_semaphores(c):
    c.nc.all_engine_barrier()
    c.nc.clear_and_free_semaphores(c.open_sems)
    c.nc.all_engine_barrier()
    c.open_sems = []


def load_stage(c):
    nc, io = c.nc, c.io
    c.at = 0
    rows = take(c, 9 * D).rearrange("p (t d) -> p t d", t=9)
    cv = take(c, QKV)
    vec = take(c, 4 * P)
    with ExitStack() as ctx:
        ld, ldc, tr, ev, zero, cpy = sems(nc, ctx, c, "loaded", "consts_loaded", "turned", "evacuated", "zeroed", "zero2")
        with nc.Block() as block:
            @block.sync
            def _(sp):
                sp.dma_start(c.ct[:, :], io["consts"]).then_inc(ldc, 16)
                sp.dma_start(rows[:, 0:8, :], io["x_prompt"][0].rearrange("(t p) d -> p t d", p=P)).then_inc(ld, 16)
                sp.dma_start(rows[0:NS, 8, :], io["x_sample"].rearrange("b t d -> (b t) d")).then_inc(ld, 16)
                sp.dma_start(cv[0:24, :], io["state_gdn_conv"][0].rearrange("b r f -> (b r) f")).then_inc(ld, 16)
                sp.dma_start(c.pages[:, :], io["page_table"].rearrange("b (o n) -> o (b n)", o=1)).then_inc(ld, 16)
                sp.wait_ge(zero, 1)
                sp.dma_start(vec[0:16, 0:128], io["norm1_w"].rearrange("l (k p) -> (l k) p", p=P)).then_inc(ld, 16)
                sp.dma_start(vec[16:32, 0:128], io["norm2_w"].rearrange("l (k p) -> (l k) p", p=P)).then_inc(ld, 16)
                sp.dma_start(vec[32:40, 0:128], io["final_norm_w"].rearrange("(k p) -> k p", p=P)).then_inc(ld, 16)
                sp.dma_start(vec[40:41, 0:128], io["gdn_norm_w"]).then_inc(ld, 16)
                sp.dma_start(vec[0:96, 128:256], io["gdn_conv_w"][0].rearrange("r (k p) -> (r k) p", p=P)).then_inc(ld, 16)

            @block.gpsimd
            def _(pool):
                pool.memset(vec[:, :], 0.0).then_inc(zero, 1)

            jobs = [(rows[0:(P if t < 8 else NS), t, k * P:(k + 1) * P], c.xT[:, k, t * P:t * P + (P if t < 8 else NS)])
                    for t in range(9) for k in range(KD)]
            jobs += [(cv[0:24, k * P:(k + 1) * P], c.convT[:, k, :]) for k in range(24)]
            jobs += [(vec[:, 0:128], c.normw[:, :]), (vec[0:96, 128:256], c.convw[:, :])]

            @block.tensor
            def _(pe):
                pe.wait_ge(ldc, 16)
                pe.wait_ge(ld, 9 * 16)
                for n, (src, dst) in enumerate(jobs):
                    if n >= 8:
                        pe.wait_ge(ev, n - 7)
                    r = src.shape[0]
                    pe.transpose(bank(c, n % 8)[:, 0:r], src, const(c, "ident")[0:r, 0:r]).then_inc(tr, 1)

            @block.vector
            def _(dve):
                for n, (src, dst) in enumerate(jobs):
                    dve.wait_ge(tr, n + 1)
                    w = dst.shape[1]
                    dve.tensor_copy(dst, bank(c, n % 8)[:, 0:w]).then_inc(ev, 1)


def norm_stage(c, which, out, base):
    nc = c.nc
    c.at = base
    sq = take(c, 2 * NT).rearrange("p (s t) -> p s t", s=2)
    rt = take(c, NT)
    with ExitStack() as ctx:
        sqr, ss, root, inv, done = sems(nc, ctx, c, "squared", "summed", "rooted", "inverted", "normed")
        acc = proj_psum(c, 0)
        with nc.Block() as block:
            @block.scalar
            def _(act):
                for k in range(KD):
                    if k >= 2:
                        act.wait_ge(ss, k - 1)
                    act.activation(sq[:, k % 2, :], c.xT[:, k, :], ACT.Square).then_inc(sqr, 1)
                act.wait_ge(ss, KD)
                for (o, w), a in zip(CH, acc):
                    act.activation(rt[:, o:o + w], a, ACT.Sqrt, bias=const(c, "eps"), scale=1.0 / D).then_inc(root, 1)

            @block.tensor
            def _(pe):
                for k in range(KD):
                    pe.wait_ge(sqr, k + 1)
                    for n, ((o, w), a) in enumerate(zip(CH, acc)):
                        mm = pe.matmul(a, const(c, "ones"), sq[:, k % 2, o:o + w], start=(k == 0), stop=(k == KD - 1))
                    mm.then_inc(ss, 1)

            @block.vector
            def _(dve):
                dve.wait_ge(root, 3)
                dve.reciprocal(rt[:, :], rt[:, :]).then_inc(inv, 1)
                dve.wait_ge(inv, 1)
                for k in range(KD):
                    dve.scalar_tensor_tensor(out=out[:, k, :], in0=c.xT[:, k, :], scalar=c.normw[:, which * 8 + k:which * 8 + k + 1],
                                             in1=rt[:, :], op0=ALU.mult, op1=ALU.mult).then_inc(done, 1)


def mm_tile(pe, dst, w, rhs, nk):
    for (o, n), a in zip(CH, dst):
        for k in range(nk):
            mm = pe.matmul(a, w[:, k, :], rhs[:, k, o:o + n], start=(k == 0), stop=(k == nk - 1))
    return mm


def proj_stage(c, nk, tiles, src, rhs, wbuf, evac):
    nc = c.nc
    with ExitStack() as ctx:
        w0, w1, mm0, mm1, free0, free1 = sems(
            nc, ctx, c, "w0_loaded", "w1_loaded", "tile0_done", "tile1_done", "tile0_taken", "tile1_taken")
        wl, mmd, free = (w0, w1), (mm0, mm1), (free0, free1)
        npc = len(src(0, 0))
        with nc.Block() as block:
            @block.sync
            def _(sp):
                for j in range(2):
                    for dst, s in src(j, j):
                        sp.dma_start(dst, s).then_inc(wl[j], 16)
                with sp.Fori(0, tiles // 2 - 1) as i:
                    for j in range(2):
                        sp.wait_ge(mmd[j], i + 1)
                        for dst, s in src(2 * i + 2 + j, j):
                            sp.dma_start(dst, s).then_inc(wl[j], 16)

            @block.tensor
            def _(pe):
                with pe.Fori(0, tiles // 2) as i:
                    for j in range(2):
                        pe.wait_ge(wl[j], (i + 1) * (16 * npc))
                        pe.wait_ge(free[j], i * 2 + 1)
                        mm_tile(pe, proj_psum(c, j), wbuf[j], rhs, nk).then_inc(mmd[j], 1)

            @block.vector
            def _(dve):
                for j in range(2):
                    dve.sem_inc(free[j], 1)
                with dve.Fori(0, tiles // 2) as i:
                    for j in range(2):
                        dve.wait_ge(mmd[j], i + 1)
                        for ins in evac(dve, i * 2 + j, proj_parts(c, 3 * j)):
                            ins.then_inc(free[j], 1)


def out_stage(c, nk, src, rhs, wbuf):
    def evac(dve, m, parts):
        for o, n, acc in parts:
            x = like(c.xTf[:, ds(m * NT + o, n)], acc)
            yield dve.tensor_tensor(x, x, acc, ALU.add)

    proj_stage(c, nk, KD, src, rhs, wbuf, evac)


def ffn_stages(c, layer):
    nc, io = c.nc, c.io
    c.at = 0
    hid = take(c, KF * NT)
    hid3 = hid.rearrange("p (k t) -> p k t", k=KF)
    hbase = c.at
    norm_stage(c, 2 + layer, c.xn, 0)
    c.at = hbase
    sg = take(c, NT)
    wb = [take(c, KD * P).rearrange("p (k f) -> p k f", k=KD) for _ in range(4)]
    w_in = io["ffn_w_in"][layer].rearrange("(k p) f -> p k f", p=P)
    w_out = io["ffn_w_out"][layer].rearrange("(k p) f -> p k f", p=P)
    with ExitStack() as ctx:
        names = [f"{a}{j}" for a in ("gate_w_loaded", "up_w_loaded") for j in range(2)]
        gw0, gw1, uw0, uw1 = sems(nc, ctx, c, *names)
        gmm, umm, silu, prod = sems(nc, ctx, c, "gate_done", "up_done", "silu_done", "hidden_done")
        gw, uw = (gw0, gw1), (uw0, uw1)
        with nc.Block() as block:
            @block.sync
            def _(sp):
                for j in range(2):
                    sp.dma_start(wb[2 * j], w_in[:, :, j * P:(j + 1) * P]).then_inc(gw[j], 16)
                    sp.dma_start(wb[2 * j + 1], w_in[:, :, DFF + j * P:DFF + (j + 1) * P]).then_inc(uw[j], 16)
                with sp.Fori(0, KF // 2 - 1) as i:
                    for j in range(2):
                        sp.wait_ge(umm, i * 2 + j + 1)
                        o = (i + 1) * (2 * P) + j * P
                        sp.dma_start(wb[2 * j], w_in[:, :, ds(o, P)]).then_inc(gw[j], 16)
                        sp.dma_start(wb[2 * j + 1], w_in[:, :, ds(o + DFF, P)]).then_inc(uw[j], 16)

            @block.tensor
            def _(pe):
                with pe.Fori(0, KF // 2) as i:
                    for j in range(2):
                        pe.wait_ge(gw[j], (i + 1) * 16)
                        pe.wait_ge(silu, i * 4 + 2 * j + 1)
                        mm_tile(pe, proj_psum(c, 0), wb[2 * j], c.xn, KD).then_inc(gmm, 1)
                        pe.wait_ge(uw[j], (i + 1) * 16)
                        pe.wait_ge(prod, i * 4 + 2 * j + 1)
                        mm_tile(pe, proj_psum(c, 1), wb[2 * j + 1], c.xn, KD).then_inc(umm, 1)

            @block.scalar
            def _(act):
                act.sem_inc(silu, 1)
                with act.Fori(0, KF // 2) as i:
                    for j in range(2):
                        act.wait_ge(gmm, i * 2 + j + 1)
                        act.wait_ge(prod, i * 4 + 2 * j + 1)
                        for o, n, acc in proj_parts(c, 0):
                            act.activation(like(sg[:, o:o + n], acc), acc, ACT.Silu).then_inc(silu, 1)

            @block.vector
            def _(dve):
                dve.sem_inc(prod, 1)
                with dve.Fori(0, KF // 2) as i:
                    for j in range(2):
                        dve.wait_ge(umm, i * 2 + j + 1)
                        dve.wait_ge(silu, i * 4 + 2 * j + 3)
                        for o, n, acc in proj_parts(c, 3):
                            dve.tensor_tensor(like(hid[:, ds((i * 2 + j) * NT + o, n)], acc), like(sg[:, o:o + n], acc), acc,
                                              ALU.mult).then_inc(prod, 1)
    flat = c.xnf
    wo = [flat[:, j * KF * P:(j + 1) * KF * P].rearrange("p (k f) -> p k f", k=KF) for j in range(2)]
    out_stage(c, KF, lambda m, j: [(wo[j], w_out[:, :, ds(m * P, P)])], hid3, wo)


BETA, NBETA, GCUM, TAIL, ETOT, LOGA = range(6)
NPAR = 6 * 9


def gate_stage(c):
    nc, io = c.nc, c.io
    c.at = 0
    wba = take(c, KD * 16).rearrange("p (k f) -> p k f", k=KD)
    row = take(c, 16)
    ba = take(c, 144)
    t1, t2, t3 = take(c, 72), take(c, 72), take(c, 72)
    rb = take(c, 16)
    gs, tot = take(c, 72), take(c, 72)
    par = c.par.rearrange("p (h q c) -> p q c h", h=HG, q=6)
    ba3 = ba.rearrange("p (c n) -> p c n", c=9)

    def v(a):
        return a.rearrange("p (c h) -> p c h", c=9)

    with ExitStack() as ctx:
        ld, z, pm, step, a1, pg = sems(nc, ctx, c, "gate_inputs", "zeroed", "products", "vector_step", "scalar_step", "sums")
        with nc.Block() as block:
            @block.sync
            def _(sp):
                sp.dma_start(wba, io["gdn_w_in"][0].rearrange("(k p) f -> p k f", p=P)[:, :, 4096:4112]).then_inc(ld, 16)
                sp.dma_start(row[0:1, 0:8], io["gdn_dt_bias"]).then_inc(ld, 16)
                sp.dma_start(row[0:1, 8:16], io["gdn_A_log"]).then_inc(ld, 16)

            @block.gpsimd
            def _(pool):
                pool.memset(ba, 0.0).then_inc(z, 1)
                pool.memset(gs, 0.0).then_inc(z, 1)
                pool.memset(tot, 0.0).then_inc(z, 1)

            @block.tensor
            def _(pe):
                pe.wait_ge(ld, 48)
                for t in range(9):
                    n = P if t < 8 else NS
                    for k in range(KD):
                        pe.matmul(bank(c, 0)[0:n, 16 * t:16 * t + 16], c.xn[:, k, t * P:t * P + n], wba[:, k, :],
                                  start=(k == 0), stop=(k == KD - 1))
                pe.matmul(bank(c, 1)[:, 0:16], const(c, "ones")[0:1, :], row[0:1, :], start=True, stop=True).then_inc(pm, 1)
                pe.wait_ge(step, 8)
                la, las = t3[:, 0:64], t3[0:NS, 64:72]
                pe.matmul(bank(c, 2)[:, 0:64], const(c, "upper"), la, start=True, stop=True)
                pe.matmul(bank(c, 3)[0:NS, 0:8], const(c, "upper_s")[0:NS, :], las, start=True, stop=True)
                pe.matmul(bank(c, 4)[:, 0:64], const(c, "ones"), la, start=True, stop=True)
                pe.matmul(bank(c, 5)[0:NS, 0:8], const(c, "same_s")[0:NS, :], las, start=True, stop=True).then_inc(pg, 1)

            @block.scalar
            def _(act):
                act.wait_ge(step, 4)
                act.activation(par[:, BETA], ba3[:, :, 0:8], ACT.Sigmoid).then_inc(a1, 1)
                act.activation(rb[:, 8:16], rb[:, 8:16], ACT.Exp).then_inc(a1, 1)
                act.activation(t2, t2, ACT.Exp, scale=-1.0).then_inc(a1, 1)
                act.wait_ge(a1, 3)
                act.activation(t2, t2, ACT.Ln, bias=const(c, "one")).then_inc(a1, 1)
                act.wait_ge(step, 11)
                act.activation(par[:, TAIL], v(gs), ACT.Exp).then_inc(a1, 1)
                act.activation(par[:, ETOT], v(tot), ACT.Exp).then_inc(a1, 1)

            @block.vector
            def _(dve):
                dve.wait_ge(z, 3)
                dve.wait_ge(pm, 1)
                dve.tensor_copy(ba[:, 0:128], bank(c, 0)[:, 0:128])
                dve.tensor_copy(ba[0:NS, 128:144], bank(c, 0)[0:NS, 128:144])
                dve.tensor_copy(rb, bank(c, 1)[:, 0:16]).then_inc(step, 1)
                dve.wait_ge(step, 1)
                dve.tensor_tensor(v(t1), ba3[:, :, 8:16], rb[:, 0:8].rearrange("p (o h) -> p o h", o=1).to_broadcast([P, 9, 8]),
                                  ALU.add).then_inc(step, 1)
                dve.wait_ge(step, 2)
                dve.tensor_scalar(t3, t1, -1.0, None, ALU.mult).then_inc(step, 1)
                dve.wait_ge(step, 3)
                dve.tensor_tensor(t2, t1, t3, ALU.max).then_inc(step, 1)
                dve.tensor_scalar(t1, t1, 0.0, None, ALU.max).then_inc(step, 1)
                dve.wait_ge(a1, 4)
                dve.wait_ge(step, 5)
                dve.tensor_scalar(par[:, NBETA], par[:, BETA], -1.0, None, ALU.mult).then_inc(step, 1)
                dve.tensor_tensor(t1, t1, t2, ALU.add).then_inc(step, 1)
                dve.wait_ge(step, 7)
                dve.scalar_tensor_tensor(out=v(t3), in0=v(t1), scalar=-1.0,
                                         in1=rb[:, 8:16].rearrange("p (o h) -> p o h", o=1).to_broadcast([P, 9, 8]),
                                         op0=ALU.mult, op1=ALU.mult).then_inc(step, 1)
                dve.wait_ge(pg, 1)
                dve.wait_ge(step, 8)
                dve.tensor_copy(par[:, LOGA], v(t3))
                dve.tensor_copy(gs[:, 0:64], bank(c, 2)[:, 0:64])
                dve.tensor_copy(gs[0:NS, 64:72], bank(c, 3)[0:NS, 0:8])
                dve.tensor_copy(tot[:, 0:64], bank(c, 4)[:, 0:64])
                dve.tensor_copy(tot[0:NS, 64:72], bank(c, 5)[0:NS, 0:8]).then_inc(step, 1)
                dve.wait_ge(step, 9)
                dve.tensor_copy(par[:, GCUM], v(gs)).then_inc(step, 1)
                dve.wait_ge(step, 10)
                dve.tensor_tensor(gs, tot, gs, ALU.subtract).then_inc(step, 1)
                dve.wait_ge(a1, 6)


GRP_LEVELS = [(2, 4, 8, 16, 32, 64), (2, 4, 8, 16, 32, 64), (2, 4)]
NLV = sum(len(lv) for lv in GRP_LEVELS)
CONV_STEP = 4
STEPS = []
for _g in (0, 1):
    STEPS += [(n, _g) for n in ("p1", "p2", "p3")] + [(n, _g, _l) for _l in range(len(GRP_LEVELS[_g])) for n in ("P", "Y")]
for _k in range(NC):
    STEPS += [("kS", _k)] * (_k > 0) + [("u", _k), ("dS", _k)]
STEPS += [(n, 2) for n in ("p1", "p2", "p3")] + [(n, 2, _l) for _l in range(len(GRP_LEVELS[2])) for n in ("P", "Y")]
STEPS += [("kss",), ("kst2",), ("u2",), ("o2",), ("oss",)]
TILE_MM = KD * len(CH)
ROOT_PAUSE = 4
T_END = [TILE_MM, 2 * TILE_MM, 3 * TILE_MM]
SUM_END = [T_END[2] + len(CH) + 4, T_END[2] + 2 * len(CH) + 4 + ROOT_PAUSE]
T_END.append(SUM_END[1] + TILE_MM)
FILL = {"p1": 4, "p2": 8, "p3": 4, ("P", 0, 0): 8, ("P", 1, 0): 8, "P": 1, "Y": 1, "kS": 1, "u": 1, "dS": 1, ("P", 2): 3, ("Y", 2): 2,
        "kss": 3, "kst2": 3, "u2": 3, "o2": 3, None: 0}


def fill_count(step):
    return next(FILL[k] for k in (step, step[:2], step[0], None) if k in FILL)


def step_of(count):
    done = 0
    for n, s in enumerate(STEPS[:-1]):
        done += fill_count(s)
        if done >= count:
            return n
    return len(STEPS) - 1


def gdn_stage(c):
    nc, io = c.nc, c.io
    c.at = 0
    w = [take(c, KD * P).rearrange("p (k f) -> p k f", k=KD) for _ in range(4)]
    yT = take(c, HG * NT)
    qT, kT, vT, zT = [take(c, NT) for _ in range(4)]
    nxt = [take(c, NT) for _ in range(4)]
    cin = take(c, 3 + TP + NB * (3 + TS))
    sq = take(c, NT)
    rq = [take(c, NT) for _ in range(2)]
    s0 = take(c, NB * P)
    parh, st0, st1, us, kst, cw, eb = take(c, NPAR), take(c, P), take(c, P), take(c, P), take(c, NS), take(c, 12), take(c, NB)
    kt, bv = take(c, 9 * P), take(c, 9 * P)
    assert c.at <= c.tail, c.at
    eg, e1, e2, lt, ml, x, xt, pp = [c.xTf[:, n * NT:(n + 1) * NT] for n in range(8)]
    oS, osq_ = e1, xt
    sn, um = lt[:, 0:NB * P], ml[:, 0:NB * P]
    park = nc.dram_tensor("parked_residual", (P, KD * NT), F32).ap()
    st = [st0, st1]
    w_in = io["gdn_w_in"][0].rearrange("(k p) f -> p k f", p=P)
    A, B, C, Dp, E, PJ = 0, 512, 1024, 1536, 2048, 5


    def par(q, n, height):
        return parh[0:height, q * 9 + n:q * 9 + n + 1]

    GROUPS = [dict(n=4, r=P, o=0, c0=0, up="upper", lo="strict", lv=GRP_LEVELS[0], l0=0),
              dict(n=4, r=P, o=512, c0=4, up="upper", lo="strict", lv=GRP_LEVELS[1], l0=6),
              dict(n=1, r=NS, o=TP, c0=8, up="upper_s", lo="strict_s", lv=GRP_LEVELS[2], l0=12)]

    def blk(a, g, k, height=None):
        return a[0:(height or g["r"]), g["o"] + k * g["r"]:g["o"] + (k + 1) * g["r"]]

    def tok(a, g, k):
        return a[0:g["r"], (g["c0"] + k) * P:(g["c0"] + k + 1) * P]

    def ps(base, g, k, height=None, width=None):
        width = width or g["r"]
        return c.ps[0:(height or g["r"]), base + k * width:base + (k + 1) * width]

    def grp(a, g):
        return a[0:g["r"], g["o"]:g["o"] + g["n"] * g["r"]].rearrange("p (n f) -> p n f", n=g["n"])

    def psg(base, g):
        return c.ps[0:g["r"], base:base + g["n"] * g["r"]].rearrange("p (n f) -> p n f", n=g["n"])

    def mask(name, g):
        m = const(c, name)[0:g["r"], 0:g["r"]]
        return m.rearrange("p (o f) -> p o f", o=1).to_broadcast([g["r"], g["n"], g["r"]])

    def sview(a, lo, n):
        return a[:, 3 + TP:].rearrange("p (b t) -> p b t", b=NB)[:, :, lo:lo + n]

    class Turn:

        def __init__(self, parts, more):
            self.left = sorted(parts, key=lambda e: e[0]) if more else []

        def before(self, *step):
            while self.left and step_of(self.left[0][0]) <= STEPS.index(step):
                self.left.pop(0)[1]()

    with ExitStack() as ctx:
        names = ["parked", "states_loaded", "states_stored", "state_out"] + [f"w{j}_loaded" for j in range(4)]
        (parked, s0l, sns, sto, *wl) = sems(nc, ctx, c, *names)
        (pj, hist, raw, conv, sil, sqd, ssd, rooted, nconv, kq, vz, lnd) = sems(
            nc, ctx, c, "tile_projected", "history_set", "tile_copied", "conv_done", "activated",
            "squared", "summed", "root_ready", "conv_rows_kept", "key_query_ready", "gate_ready", "log_taken")
        (p1, p2, p3, a1, v1, a2, v2, v3, mlr, pr, psr, yr, xr) = sems(
            nc, ctx, c, "turned_products", "query_key", "l_turned", "tail_keys", "differences", "decays", "l_and_scores",
            "x_begun", "l_masked", "p_product", "p_copied", "y_products", "x_updated")
        (ksr, rr, ur, usr, dsr, str_) = sems(nc, ctx, c, "key_state", "rhs_ready", "u_product", "u_copied", "state_product", "state_ready")
        (kss, kstc, kst2, rs, u2, us2, um2, o2, oc2, sn2) = sems(
            nc, ctx, c, "s_key_state", "s_copied", "s_turned", "s_rhs", "s_u", "s_u_copied", "s_u_spread", "s_out", "s_out_copied", "s_states")
        (vt, oc, osq, oss, ort, yd, dc, pc, first_step) = sems(
            nc, ctx, c, "values_ready", "o_copied", "o_squared", "o_summed", "o_rooted", "y_done", "vector_chain", "params_copied", "first_conv_chain")
        with nc.Block() as block:
            @block.sync
            def _(sp):
                for s in (sto, sns):
                    sp.sem_inc(s, 1)
                sp.dma_start(park, c.xTf).then_inc(parked, 16)
                for j in range(4):
                    sp.dma_start(w[j], w_in[:, :, j * D:j * D + P]).then_inc(wl[j], 16)
                sp.dma_start(s0.rearrange("p (b v) -> p b v", b=NB), io["state_gdn"][0][:, 0].rearrange("b k v -> k b v")).then_inc(s0l, 16)
                for j in range(4):
                    sp.wait_ge(pj, j + 1)
                    sp.dma_start(w[j], w_in[:, :, P + j * D:2 * P + j * D]).then_inc(wl[j], 16)

                def head(i, more, weights):
                    if weights:
                        for j in range(4):
                            sp.wait_ge(pj, i * 4 + j + 5)
                            sp.dma_start(w[j], w_in[:, :, ds((i + 2) * P + j * D, P)]).then_inc(wl[j], 16)
                    sp.wait_ge(str_, i * 8 + 8)
                    sp.dma_start(io["out6"][0, 0][ds(i, 1)].rearrange("o k v -> k (o v)"), st[1]).then_inc(sto, 16)
                    sp.wait_ge(sn2, i + 2)
                    sp.dma_start(io["out7"][0][:, ds(i, 1)].rearrange("b o k v -> k (b o) v"),
                                 sn.rearrange("p (b v) -> p b v", b=NB)).then_inc(sns, 16)
                    if more:
                        sp.dma_start(s0.rearrange("p (b v) -> p b v", b=NB),
                                     io["state_gdn"][0][:, ds(i + 1, 1)].rearrange("b o k v -> k (b o) v")).then_inc(s0l, 16)

                with sp.Fori(0, HG - 2) as i:
                    head(i, True, True)
                head(HG - 2, True, False)
                head(HG - 1, False, False)
                sp.wait_ge(sto, 16 * HG + 1)
                sp.wait_ge(sns, 16 * HG + 1)

            @block.tensor
            def _(pe):
                pe.wait_ge(parked, 16)

                def alone():
                    pe.nop(nofuse=True)

                def tile_products(n, j, peeled):
                    pe.wait_ge(wl[j], n * 16 + 16)
                    if j == 3:
                        pe.wait_ge(lnd, n * 4 + 4)
                    elif j or not peeled:
                        pe.wait_ge(raw, n * 8 + 2 * j)
                    for m, ((o, cnt), acc) in enumerate(zip(CH, proj_acc(c, PJ))):
                        for k in range(KD):
                            mm = pe.matmul(acc, w[j][:, k, :], c.xn[:, k, o:o + cnt], start=(k == 0), stop=(k == KD - 1))
                            if k == KD - 1 and m == len(CH) - 1:
                                mm.then_inc(pj, 1)
                            yield

                def square_sums(n, j):
                    if j:
                        pe.wait_ge(lnd, n * 4 + 2)
                    else:
                        pe.wait_ge(raw, n * 8 + 6)
                    pe.wait_ge(sqd, n * 2 + j + 1)
                    for m, ((o, cnt), acc) in enumerate(zip(CH, proj_acc(c, PJ))):
                        mm = pe.matmul(acc, const(c, "ones"), sq[:, o:o + cnt], start=True, stop=True)
                        if m == len(CH) - 1:
                            mm.then_inc(ssd, 1)
                        yield

                def stream(n, peeled):
                    for j in range(3):
                        yield from tile_products(n, j, peeled)
                    for _ in range(4):
                        yield
                    yield from square_sums(n, 0)
                    for _ in range(ROOT_PAUSE):
                        yield
                    yield from square_sums(n, 1)
                    yield from tile_products(n, 3, peeled)

                def head(i, more):
                    ahead = stream(i + 1, False) if more else iter(())

                    def fill(*step):
                        for _ in range(fill_count(step)):
                            next(ahead, None)

                    pe.wait_ge(ort, i * 3 + 1)
                    pe.wait_ge(sn2, i + 1)
                    for gi, g in enumerate(GROUPS):
                        n, r = g["n"], g["r"]
                        fill("p1", gi)
                        if gi == 0:
                            pe.wait_ge(kq, i * 2 + 2)
                            pe.wait_ge(vt, i + 1)
                            pe.wait_ge(pc, i + 1)
                        elif gi == 1:
                            pe.wait_ge(xr, i * NLV + g["l0"])
                        alone()
                        for k in range(n):
                            pe.transpose(ps(A, g, k, width=P), blk(kT, g, k, P), const(c, "ident"))
                        for k in range(n):
                            pe.transpose(ps(B, g, k, width=P), blk(vT, g, k, P), const(c, "ident"))
                        for k in range(n):
                            pe.matmul(ps(C, g, k, P), par(LOGA, g["c0"] + k, r).to_broadcast([r, P]), const(c, g["up"])[0:r, 0:r],
                                      start=True, stop=True)
                        for k in range(n):
                            mm = pe.matmul(ps(Dp, g, k), blk(kT, g, k, P), blk(kT, g, k, P), start=True, stop=True)
                        mm.then_inc(p1, 1)
                        fill("p2", gi)
                        pe.wait_ge(a1, i * 3 + gi + 1)
                        alone()
                        for k in range(n):
                            mm = pe.matmul(ps(A, g, k), blk(kT, g, k, P), blk(qT, g, k, P), start=True, stop=True)
                        mm.then_inc(p2, 1)
                        fill("p3", gi)
                        pe.wait_ge(v2, i * 3 + gi + 1)
                        alone()
                        for k in range(n):
                            mm = pe.transpose(ps(B, g, k), blk(e1, g, k), const(c, "ident")[0:r, 0:r])
                        mm.then_inc(p3, 1)
                        for l, s in enumerate(g["lv"]):
                            q = i * NLV + g["l0"] + l
                            fill("P", gi, l)
                            if l == 0:
                                pe.wait_ge(v3, i * 3 + gi + 1)
                            else:
                                pe.wait_ge(xr, q)
                            pe.wait_ge(mlr, q + 1)
                            alone()
                            for k in range(n):
                                mm = pe.matmul(ps(C, g, k), blk(ml, g, k), blk(x, g, k), start=True, stop=True)
                            mm.then_inc(pr, 1)
                            fill("Y", gi, l)
                            pe.wait_ge(psr, q + 1)
                            alone()
                            if l < len(g["lv"]) - 1:
                                for k in range(n):
                                    pe.matmul(ps(Dp, g, k), blk(xt, g, k), blk(pp, g, k), start=True, stop=True)
                            for k in range(n):
                                mm = pe.matmul(ps(A, g, k), blk(pp, g, k), blk(xt, g, k), start=True, stop=True)
                            mm.then_inc(yr, 1)
                        if gi == 1:
                            recurrence(i, fill)
                    g = GROUPS[2]
                    pe.wait_ge(xr, i * NLV + NLV)
                    pe.wait_ge(s0l, i * 16 + 16)
                    fill("kss")
                    for b in range(NB):
                        mm = pe.matmul(c.ps[:, A + TS * b:A + TS * b + TS], s0[:, b * P:(b + 1) * P], kT[:, TP + TS * b:TP + TS * b + TS],
                                       start=True, stop=True)
                    mm.then_inc(kss, 1)
                    fill("kst2")
                    pe.wait_ge(kstc, i + 1)
                    alone()
                    pe.transpose(c.ps[0:NS, B:B + P], kst, const(c, "ident")).then_inc(kst2, 1)
                    fill("u2")
                    pe.wait_ge(rs, i + 1)
                    alone()
                    pe.matmul(c.ps[0:NS, C:C + P], blk(xt, g, 0), tok(bv, g, 0), start=True, stop=True).then_inc(u2, 1)
                    fill("o2")
                    pe.wait_ge(us2, i + 1)
                    alone()
                    pe.matmul(c.ps[:, Dp:Dp + NS], us[0:NS, :], blk(e2, g, 0), start=True, stop=False, skip_group_check=True)
                    for b in range(NB):
                        pe.matmul(c.ps[:, Dp + TS * b:Dp + TS * b + TS], s0[:, b * P:(b + 1) * P],
                                  qT[:, TP + TS * b:TP + TS * b + TS], start=False, stop=(b == NB - 1), skip_group_check=True)
                    pe.matmul(c.ps[:, E:E + NB], par(LOGA, 8, NS).to_broadcast([NS, P]), const(c, "batch_s")[0:NS, :], start=True, stop=True)
                    pe.wait_ge(um2, i + 1)
                    for hf in range(2):
                        mm = pe.matmul(c.ps[:, A + 512 * hf:A + 512 * hf + 512], tok(kt, g, 0), um[0:NS, 512 * hf:512 * hf + 512],
                                       start=True, stop=True)
                    mm.then_inc(o2, 1)
                    for _ in ahead:
                        pass
                    pe.wait_ge(osq, i + 1)
                    for (o, n), a in zip(CH, proj_acc(c, 2)):
                        mm = pe.matmul(a, const(c, "ones"), osq_[:, o:o + n], start=True, stop=True)
                    mm.then_inc(oss, 1)

                def recurrence(i, fill):
                    pe.wait_ge(xr, i * NLV + 12)
                    for k in range(NC):
                        g = GROUPS[k // 4]
                        out = ps(E if k < 4 else C, g, k % 4)
                        if k:
                            fill("kS", k)
                            pe.wait_ge(str_, i * 8 + k)
                            pe.matmul(c.ps[:, A:A + P], blk(kT, g, k % 4), st[(k - 1) % 2], start=True, stop=True).then_inc(ksr, 1)
                            pe.matmul(out, st[(k - 1) % 2], blk(qT, g, k % 4), start=True, stop=False)
                        fill("u", k)
                        if k:
                            pe.wait_ge(rr, i * 7 + k)
                        pe.matmul(c.ps[:, B:B + P], blk(xt, g, k % 4), tok(bv, g, k % 4), start=True, stop=True,
                                  skip_group_check=True).then_inc(ur, 1)
                        fill("dS", k)
                        pe.wait_ge(usr, i * 8 + k + 1)
                        pe.matmul(out, us, blk(e2, g, k % 4), start=(k == 0), stop=True)
                        pe.matmul(c.ps[:, Dp:Dp + P], tok(kt, g, k % 4), us, start=True, stop=True,
                                  skip_group_check=True).then_inc(dsr, 1)
                    pe.wait_ge(str_, i * 8 + 8)
                    pe.wait_ge(oc, i + 1)

                for _ in stream(0, True):
                    pass
                with pe.Fori(0, HG - 1) as i:
                    head(i, True)
                head(HG - 1, False)

            @block.scalar
            def _(act):
                act.wait_ge(parked, 16)
                act.sem_inc(ort, 1)

                def take_tile(n, j, peeled):
                    act.wait_ge(pj, n * 4 + j + 1)
                    (_, w0, acc), (o, w1, acc2) = proj_parts(c, PJ)
                    if j == 3:
                        act.activation(like(nxt[3][:, 0:w0], acc), acc, ACT.Copy).then_inc(raw, 1)
                        act.activation(nxt[3][:, o:o + w1], acc2, ACT.Copy).then_inc(raw, 1)
                        return
                    if j or not peeled:
                        act.wait_ge(conv, n * 3 + j)
                        act.wait_ge(nconv, n * 3 + j)
                    act.activation(like(cin[:, 3:3 + w0], acc), acc, ACT.Copy).then_inc(raw, 1)
                    act.activation(cin[:, 3 + o:3 + TP], acc2[:, 0:TP - o], ACT.Copy)
                    act.activation(sview(cin, 3, TS), acc2[:, TP - o:].rearrange("p (b t) -> p b t", b=NB), ACT.Copy).then_inc(raw, 1)

                def squares(n, j):
                    if j:
                        act.wait_ge(ssd, n * 2 + j)
                    act.activation(sq, nxt[j], ACT.Square).then_inc(sqd, 1)

                def silu(n, j):
                    act.wait_ge(conv, n * 3 + j + 1)
                    act.activation(nxt[j], nxt[j], ACT.Silu).then_inc(sil, 1)
                    act.wait_ge(sil, n * 3 + j + 1)

                def gate(n):
                    act.wait_ge(yd, n + 1)
                    act.wait_ge(raw, n * 8 + 8)
                    act.activation(zT, nxt[3], ACT.Silu).then_inc(vz, 1)

                def logs(n, j):
                    act.wait_ge(ssd, n * 2 + j + 1)
                    for o, cnt, acc in proj_parts(c, PJ):
                        act.activation(like(rq[j][:, o:o + cnt], acc), acc, ACT.Ln, bias=const(c, "eps_dk" if j == 0 else "eps"),
                                       scale=float(P) if j == 0 else 1.0).then_inc(lnd, 1)
                def roots_of_q(n):
                    logs(n, 0)
                    squares(n, 1)

                def roots_of_k(n):
                    logs(n, 1)
                    act.wait_ge(lnd, n * 4 + 4)
                    act.activation(rq[1], rq[1], ACT.Exp, scale=-0.5).then_inc(rooted, 1)

                def root_of_q(n):
                    act.activation(rq[0], rq[0], ACT.Exp, scale=-0.5).then_inc(rooted, 1)

                def head(i, more):
                    def roots_of_next_q():
                        act.wait_ge(kq, i * 2 + 2)
                        roots_of_q(i + 1)



                    turn = Turn([(T_END[0], lambda: take_tile(i + 1, 0, False)), (T_END[1], lambda: take_tile(i + 1, 1, False)),
                                 (T_END[1] + 16, lambda: gate(i)), (T_END[1] + 18, lambda: silu(i + 1, 0)),
                                 (T_END[1] + 20, lambda: silu(i + 1, 1)), (T_END[1] + 22, lambda: squares(i + 1, 0)),
                                 (T_END[2], lambda: take_tile(i + 1, 2, False)), (T_END[2] + 4, lambda: silu(i + 1, 2)),
                                 (SUM_END[0], roots_of_next_q), (SUM_END[1], lambda: roots_of_k(i + 1)),
                                 (SUM_END[1] + 1, lambda: root_of_q(i + 1)),
                                 (T_END[3], lambda: take_tile(i + 1, 3, False))], more)
                    for gi, g in enumerate(GROUPS):
                        turn.before("p1", gi)
                        act.wait_ge(p1, i * 3 + gi + 1)
                        act.wait_ge(pc, i + 1)
                        for k in range(g["n"]):
                            act.activation(tok(kt, g, k), ps(A, g, k, width=P), ACT.Copy, scale=par(TAIL, g["c0"] + k, g["r"]))
                        act.activation(eg[:, g["o"]:g["o"] + g["n"] * g["r"]], c.ps[:, C:C + g["n"] * g["r"]], ACT.Exp).then_inc(a1, 1)
                        act.wait_ge(v1, i * 3 + gi + 1)
                        act.activation(grp(e1, g), grp(e1, g), ACT.Exp, scale=-1.0)
                        act.activation(grp(e2, g), grp(e2, g), ACT.Exp).then_inc(a2, 1)
                        for l, s in enumerate(g["lv"]):
                            turn.before("P", gi, l)
                            act.wait_ge(pr, i * NLV + g["l0"] + l + 1)
                            act.activation(grp(pp, g), psg(C, g), ACT.Copy).then_inc(psr, 1)
                        if gi == 1:
                            for k in range(NC):
                                turn.before("u", k)
                                act.wait_ge(ur, i * 8 + k + 1)
                                act.activation(us, c.ps[:, B:B + P], ACT.Copy).then_inc(usr, 1)
                            turn.before("dS", NC - 1)
                            act.wait_ge(dsr, i * 8 + 8)
                            act.activation(osq_[:, 0:512], c.ps[:, E:E + 512], ACT.Square)
                            act.activation(osq_[:, 512:TP], c.ps[:, C:C + 512], ACT.Square)
                            act.activation(oS[:, 0:512], c.ps[:, E:E + 512], ACT.Copy)
                            act.activation(oS[:, 512:TP], c.ps[:, C:C + 512], ACT.Copy).then_inc(oc, 1)
                    turn.before("kss")
                    if not more:
                        gate(i)
                    act.wait_ge(kss, i + 1)
                    act.activation(kst, c.ps[:, A:A + NS], ACT.Copy).then_inc(kstc, 1)
                    turn.before("kst2")
                    if more:
                        act.activation(vT, nxt[2], ACT.Copy).then_inc(vt, 1)
                    turn.before("u2")
                    act.wait_ge(u2, i + 1)
                    act.activation(us[0:NS, :], c.ps[0:NS, C:C + P], ACT.Copy).then_inc(us2, 1)
                    turn.before("o2")
                    act.wait_ge(o2, i + 1)
                    act.activation(eb, c.ps[:, E:E + NB], ACT.Exp)
                    act.activation(oS[:, TP:NT], c.ps[:, Dp:Dp + NS], ACT.Copy).then_inc(oc2, 1)
                    act.activation(osq_[:, TP:NT], c.ps[:, Dp:Dp + NS], ACT.Square).then_inc(osq, 1)
                    turn.before("oss")
                    act.wait_ge(oss, i + 1)
                    for o, cnt, acc in proj_parts(c, 2):
                        act.activation(like(pp[:, o:o + cnt], acc), acc, ACT.Ln, bias=const(c, "eps"), scale=1.0 / P).then_inc(ort, 1)
                    act.wait_ge(ort, i * 3 + 3)
                    act.activation(pp, pp, ACT.Exp, scale=-0.5).then_inc(ort, 1)

                for j in range(3):
                    take_tile(0, j, True)
                for j in range(3):
                    silu(0, j)
                squares(0, 0)
                act.activation(vT, nxt[2], ACT.Copy).then_inc(vt, 1)
                roots_of_q(0)
                roots_of_k(0)
                root_of_q(0)
                take_tile(0, 3, True)
                with act.Fori(0, HG - 1) as i:
                    head(i, True)
                head(HG - 1, False)

            @block.vector
            def _(dve):
                dve.wait_ge(parked, 16)
                dve.sem_inc(sn2, 1)
                dve.sem_inc(yd, 1)
                CHAIN = 20

                def conv_tap(n, j, t, settle, first=False):
                    y = nxt[j][:, 0:TP]
                    ys = nxt[j][:, TP:NT].rearrange("p (b t) -> p b t", b=NB)
                    tap = cw[:, 3 * t + j:3 * t + j + 1]
                    if t == 0:
                        dve.wait_ge(hist, n * 3 + j + 1)
                        dve.wait_ge(raw, n * 8 + 2 * j + 2)
                        if j == 2 and not first:
                            dve.wait_ge(vt, n)
                        dve.tensor_scalar(y, cin[:, 0:TP], tap, None, ALU.mult)
                        settle(dve.tensor_scalar(ys, sview(cin, 0, TS), tap, None, ALU.mult))
                        return
                    dve.scalar_tensor_tensor(out=y, in0=cin[:, t:t + TP], scalar=tap, in1=y, op0=ALU.mult, op1=ALU.add)
                    ins = dve.scalar_tensor_tensor(out=ys, in0=sview(cin, t, TS), scalar=tap, in1=ys, op0=ALU.mult, op1=ALU.add)
                    if t < 3:
                        settle(ins)
                    else:
                        ins.then_inc(conv, 1)

                def normed(n, j):
                    dve.wait_ge(rooted, n * 2 + 2)
                    dve.tensor_tensor((qT, kT)[j], nxt[j], rq[j], ALU.mult).then_inc(kq, 1)

                def head(i, more):
                    n_chain = [0]

                    def settle(ins):
                        n_chain[0] += 1
                        ins.then_inc(dc, 1)
                        dve.wait_ge(dc, i * CHAIN + n_chain[0])

                    def one_tap(j, t):
                        return (T_END[j] + (CONV_STEP * t if j < 2 else t), lambda: conv_tap(i + 1, j, t, settle))

                    turn = Turn([one_tap(j, t) for j in range(3) for t in range(4)], more)
                    dve.tensor_copy(parh, c.par[:, ds(i * NPAR, NPAR)]).then_inc(pc, 1)
                    if more:
                        dve.wait_ge(conv, i * 3 + 3)
                        settle(dve.tensor_copy(cw, c.convw[:, ds(i + 1, 89)][:, 0:89:8]))
                    dve.wait_ge(pc, i + 1)
                    for gi, g in enumerate(GROUPS):
                        turn.before("p1", gi)
                        dve.wait_ge(p1, i * 3 + gi + 1)
                        for k in range(g["n"]):
                            dve.tensor_scalar(tok(bv, g, k), ps(B, g, k, width=P), par(BETA, g["c0"] + k, g["r"]), None, ALU.mult)
                        dve.wait_ge(a1, i * 3 + gi + 1)
                        for k in range(g["n"]):
                            gc = par(GCUM, g["c0"] + k, g["r"])
                            dve.tensor_scalar(blk(e1, g, k), ps(C, g, k), gc, 0.0, ALU.subtract, ALU.max)
                            ins = dve.tensor_scalar(blk(e2, g, k), ps(C, g, k), gc, 0.0, ALU.subtract, ALU.min)
                        ins.then_inc(v1, 1)
                        turn.before("p2", gi)
                        dve.wait_ge(a2, i * 3 + gi + 1)
                        dve.wait_ge(v1, i * 3 + gi + 1)
                        dve.tensor_tensor(grp(e1, g), grp(e1, g), mask(g["lo"], g), ALU.mult)
                        settle(dve.tensor_tensor(grp(e2, g), grp(e2, g), mask(g["up"], g), ALU.mult))
                        for k in range(g["n"]):
                            dve.scalar_tensor_tensor(out=blk(e1, g, k), in0=ps(Dp, g, k), scalar=par(BETA, g["c0"] + k, g["r"]),
                                                     in1=blk(e1, g, k), op0=ALU.mult, op1=ALU.mult)
                        dve.wait_ge(p2, i * 3 + gi + 1)
                        dve.tensor_tensor(grp(e2, g), psg(A, g), grp(e2, g), ALU.mult).then_inc(v2, 1)
                        cols = slice(g["o"], g["o"] + g["n"] * g["r"])
                        dve.tensor_tensor(kT[:, cols], kT[:, cols], eg[:, cols], ALU.mult)
                        dve.tensor_tensor(qT[:, cols], qT[:, cols], eg[:, cols], ALU.mult)
                        dve.wait_ge(v2, i * 3 + gi + 1)
                        dve.tensor_tensor(grp(x, g), grp(e1, g), mask("m1", g), ALU.mult)
                        turn.before("p3", gi)
                        dve.wait_ge(p3, i * 3 + gi + 1)
                        if gi == 0:
                            dve.wait_ge(sns, i * 16 + 1)
                        settle(dve.tensor_copy(grp(lt, g), psg(B, g)))
                        dve.tensor_tensor(grp(x, g), mask("ident", g), grp(x, g), ALU.subtract)
                        settle(dve.tensor_tensor(grp(xt, g), grp(lt, g), mask("mt1", g), ALU.mult))
                        dve.tensor_tensor(grp(xt, g), mask("ident", g), grp(xt, g), ALU.subtract).then_inc(v3, 1)
                        dve.wait_ge(v3, i * 3 + gi + 1)
                        for l, s in enumerate(g["lv"]):
                            turn.before("Y", gi, l)
                            q = i * NLV + g["l0"] + l + 1
                            dve.wait_ge(yr, q)
                            if l < len(g["lv"]) - 1:
                                dve.tensor_tensor(grp(x, g), grp(x, g), psg(Dp, g), ALU.subtract)
                            dve.tensor_tensor(grp(xt, g), grp(xt, g), psg(A, g), ALU.subtract).then_inc(xr, 1)
                            dve.wait_ge(xr, q)
                        if gi == 1:
                            for k in range(NC):
                                gk = GROUPS[k // 4]
                                if k:
                                    turn.before("kS", k)
                                    dve.wait_ge(ksr, i * 7 + k)
                                    dve.scalar_tensor_tensor(out=tok(bv, gk, k % 4), in0=c.ps[:, A:A + P], scalar=par(NBETA, k, P),
                                                             in1=tok(bv, gk, k % 4), op0=ALU.mult, op1=ALU.add).then_inc(rr, 1)
                                turn.before("dS", k)
                                dve.wait_ge(dsr, i * 8 + k + 1)
                                if k == 0:
                                    dve.wait_ge(sto, i * 16 + 1)
                                    dve.tensor_copy(st[0], c.ps[:, Dp:Dp + P]).then_inc(str_, 1)
                                else:
                                    dve.wait_ge(str_, i * 8 + k)
                                    dve.scalar_tensor_tensor(out=st[k % 2], in0=st[(k - 1) % 2], scalar=par(ETOT, k, P),
                                                             in1=c.ps[:, Dp:Dp + P], op0=ALU.mult, op1=ALU.add).then_inc(str_, 1)
                    turn.before("kss")
                    g = GROUPS[2]
                    dve.wait_ge(kst2, i + 1)
                    dve.scalar_tensor_tensor(out=tok(bv, g, 0), in0=c.ps[0:NS, B:B + P], scalar=par(NBETA, 8, NS),
                                             in1=tok(bv, g, 0), op0=ALU.mult, op1=ALU.add).then_inc(rs, 1)
                    dve.wait_ge(us2, i + 1)
                    dve.tensor_tensor(um[0:NS, :].rearrange("p (b v) -> p b v", b=NB),
                                      us[0:NS, :].rearrange("p (o v) -> p o v", o=1).to_broadcast([NS, NB, P]),
                                      const(c, "batch_s")[0:NS, :].rearrange("p (b o) -> p b o", o=1).to_broadcast([NS, NB, P]),
                                      ALU.mult).then_inc(um2, 1)
                    if more:
                        normed(i + 1, 1)
                    dve.wait_ge(oc2, i + 1)
                    for b in range(NB):
                        ins = dve.scalar_tensor_tensor(out=sn[:, b * P:(b + 1) * P], in0=s0[:, b * P:(b + 1) * P], scalar=eb[:, b:b + 1],
                                                       in1=c.ps[:, A + P * b:A + P * b + P], op0=ALU.mult, op1=ALU.add)
                    ins.then_inc(sn2, 1)
                    if more:
                        normed(i + 1, 0)
                    dve.wait_ge(ort, i * 3 + 4)
                    dve.wait_ge(oc, i + 1)
                    dve.wait_ge(vz, i + 1)
                    settle(dve.tensor_tensor(oS, oS, pp, ALU.mult))
                    dve.scalar_tensor_tensor(out=yT[:, ds(i * NT, NT)], in0=oS, scalar=c.normw[:, 40:41], in1=zT,
                                             op0=ALU.mult, op1=ALU.mult).then_inc(yd, 1)
                    assert n_chain[0] == (CHAIN if more else CHAIN - 10), n_chain

                n_first = [0]

                def settle_first(ins):
                    n_first[0] += 1
                    ins.then_inc(first_step, 1)
                    dve.wait_ge(first_step, n_first[0])

                settle_first(dve.tensor_copy(cw, c.convw[:, 0:89:8]))
                for j in range(3):
                    for t in range(4):
                        conv_tap(0, j, t, settle_first, first=True)
                normed(0, 1)
                normed(0, 0)
                with dve.Fori(0, HG - 1) as i:
                    head(i, True)
                head(HG - 1, False)

            @block.gpsimd
            def _(pool):
                pool.wait_ge(parked, 16)
                pool.memset(cin[:, 0:3], 0.0)

                def conv_edges(n, j, peeled):
                    tile = n + j * 8
                    if j or not peeled:
                        pool.wait_ge(conv, n * 3 + j)
                    pool.tensor_copy(sview(cin, 0, 3),
                                     c.convT.rearrange("p k n -> p (k n)")[:, ds(tile * 24, 24)].rearrange("p (b r) -> p b r", b=NB)
                                     ).then_inc(hist, 1)
                    pool.wait_ge(raw, n * 8 + 2 * j + 2)
                    pool.tensor_copy(c.newconv[:, ds(tile * 27, 3)], cin[:, TP:TP + 3])
                    pool.tensor_copy(c.newconv[:, ds(tile * 27 + 3, 24)].rearrange("p (b r) -> p b r", b=NB),
                                     sview(cin, TS, 3)).then_inc(nconv, 1)

                def head(i, more):
                    turn = Turn([(T_END[j], lambda j=j: conv_edges(i + 1, j, False)) for j in range(3)], more)
                    for gi, g in enumerate(GROUPS):
                        turn.before("p3", gi)
                        pool.wait_ge(v3, i * 3 + gi + 1)
                        for l, s in enumerate(g["lv"]):
                            if l:
                                turn.before("P", gi, l - 1)
                                pool.wait_ge(pr, i * NLV + g["l0"] + l)
                            pool.tensor_tensor(grp(ml, g), grp(lt, g), mask(f"mt{s}", g), ALU.mult).then_inc(mlr, 1)
                        if gi == 1:
                            for k in range(NC):
                                if k:
                                    turn.before("kS", k)
                                turn.before("u", k)
                                turn.before("dS", k)
                    turn.before("kss")

                for j in range(3):
                    conv_edges(0, j, True)
                with pool.Fori(0, HG - 1) as i:
                    head(i, True)
                head(HG - 1, False)

    c.at = 0
    conv_rows = take(c, QKV)
    with ExitStack() as ctx:
        back, tr, ev, st_ = sems(nc, ctx, c, "residual_back", "turned", "evacuated", "conv_stored")
        with nc.Block() as block:
            @block.sync
            def _(sp):
                sp.dma_start(c.xTf, park).then_inc(back, 16)
                sp.wait_ge(ev, 24)
                sp.dma_start(io["out8"][0, 0], conv_rows[0:3, :]).then_inc(st_, 16)
                sp.dma_start(io["out9"][0].rearrange("b r f -> (b r) f"), conv_rows[3:27, :]).then_inc(st_, 16)
                sp.wait_ge(st_, 32)
                sp.wait_ge(back, 16)

            @block.tensor
            def _(pe):
                for n in range(24):
                    if n >= 8:
                        pe.wait_ge(ev, n - 7)
                    pe.transpose(bank(c, n % 8)[0:27, 0:P], c.newconv[:, n * 27:(n + 1) * 27], const(c, "ident")).then_inc(tr, 1)

            @block.vector
            def _(dve):
                for n in range(24):
                    dve.wait_ge(tr, n + 1)
                    dve.tensor_copy(conv_rows[0:27, n * P:(n + 1) * P], bank(c, n % 8)[0:27, 0:P]).then_inc(ev, 1)

    wo = [conv_rows[:, j * 1024:(j + 1) * 1024].rearrange("p (k f) -> p k f", k=KD) for j in range(2)]
    w_out = io["gdn_w_out"][0].rearrange("(k p) f -> p k f", p=P)
    out_stage(c, KD, lambda m, j: [(wo[j], w_out[:, :, ds(m * P, P)])], yT.rearrange("p (k t) -> p k t", k=HG), wo)


def final_stage(c):
    nc, io = c.nc, c.io
    norm_stage(c, 4, c.xn, 0)
    c.at = 0
    rows = take(c, 9 * D).rearrange("p (t d) -> p t d", t=9)
    jobs = [(t, k) for t in range(9) for k in range(KD)]
    with ExitStack() as ctx:
        tr, ev, st_ = sems(nc, ctx, c, "turned", "evacuated", "rows_stored")
        with nc.Block() as block:
            @block.tensor
            def _(pe):
                for n, (t, k) in enumerate(jobs):
                    if n >= 8:
                        pe.wait_ge(ev, n - 7)
                    r = P if t < 8 else NS
                    pe.transpose(bank(c, n % 8)[0:r, 0:P], c.xn[:, k, t * P:t * P + r], const(c, "ident")).then_inc(tr, 1)

            @block.vector
            def _(dve):
                for n, (t, k) in enumerate(jobs):
                    dve.wait_ge(tr, n + 1)
                    r = P if t < 8 else NS
                    dve.tensor_copy(rows[0:r, t, k * P:(k + 1) * P], bank(c, n % 8)[0:r, 0:P]).then_inc(ev, 1)

            @block.sync
            def _(sp):
                for t in range(9):
                    sp.wait_ge(ev, 8 * t + 8)
                    if t < 8:
                        sp.dma_start(io["out0"][0, t * P:(t + 1) * P, :], rows[:, t, :]).then_inc(st_, 16)
                    else:
                        sp.dma_start(io["out1"].rearrange("b t d -> (b t) d"), rows[0:NS, t, :]).then_inc(st_, 16)
                sp.wait_ge(st_, 9 * 16)


class Nsa:
    pass


def nsa_buffers(c):
    c.at = 0
    a = Nsa()
    a.qTf = take(c, HG * NT)
    a.qT = a.qTf.rearrange("p (k t) -> p k t", k=HG)
    a.kvT = take(c, 6 * NT).rearrange("p (k t) -> p k t", k=6)
    a.rows = take(c, 9 * 6 * P).rearrange("p (t f) -> p t f", t=9)
    a.gates = take(c, 9 * 48).rearrange("p (t f) -> p t f", t=9)
    a.kc = take(c, 320)
    a.vcp = take(c, P)
    a.vcs = take(c, NB * P)
    a.vnew = take(c, NB * 2 * P)
    a.sgates = take(c, NB * 3)
    a.free = c.at
    return a


def nsa_project(c, a):
    nc, io = c.nc, c.io
    c.at = a.free
    w_in = io["nsa_w_in"][0].rearrange("(k p) f -> p k f", p=P)
    wb = [take(c, KD * P).rearrange("p (k f) -> p k f", k=KD) for _ in range(2)]
    wg = take(c, KD * 48).rearrange("p (k f) -> p k f", k=KD)

    def q_src(m, j):
        return [(wb[j][:, :, g * DH:(g + 1) * DH], w_in[:, :, ds(m * DH + g * HG * DH, DH)]) for g in range(2)]

    def q_evac(dve, m, parts):
        for o, n, acc in parts:
            yield dve.tensor_scalar(like(a.qTf[:, ds(m * NT + o, n)], acc), acc, DH ** -0.5, None, ALU.mult)

    proj_stage(c, KD, HG, q_src, c.xn, wb, q_evac)
    kvf = a.kvT.rearrange("p k t -> p (k t)")

    def kv_evac(dve, m, parts):
        for o, n, acc in parts:
            yield dve.tensor_copy(like(kvf[:, ds(m * NT + o, n)], acc), acc)

    proj_stage(c, KD, 6, lambda m, j: [(wb[j], w_in[:, :, ds(m * P + D, P)])], c.xn, wb, kv_evac)

    park = nc.dram_tensor("decode_gates", (NS, 48), F32).ap()
    jobs = [(t, k) for t in range(9) for k in range(6)]
    with ExitStack() as ctx:
        wl, gm, gd, tr, ev, gst, vn, st = sems(nc, ctx, c, "gate_w_loaded", "gates_multiplied", "gates_done", "turned", "evacuated",
                                               "gates_parked", "new_rows_placed", "rows_stored")
        with nc.Block() as block:
            @block.sync
            def _(sp):
                sp.dma_start(wg, w_in[:, :, 1792:1840]).then_inc(wl, 16)
                sp.dma_start(io["out5"][0].rearrange("b r k g d -> b r (k g d)")[:, 0:PAST - TS],
                             io["cache_nsa_win"][0].rearrange("b r k g d -> b r (k g d)")[:, TS:PAST]).then_inc(st, 16)
                sp.wait_ge(gd, 2)
                sp.dma_start(park, a.gates[0:NS, 8, :]).then_inc(gst, 16)
                sp.wait_ge(gst, 16)
                for gh in range(NH):
                    sp.dma_start(a.sgates[gh * TS:(gh + 1) * TS, :].rearrange("t (b r) -> t b r", b=NB),
                                 park[:, gh * 3:gh * 3 + 3].rearrange("(b t) r -> t b r", b=NB)).then_inc(vn, 16)
                sp.wait_ge(ev, len(jobs))
                for b in range(NB):
                    for n, k in enumerate((3, 5)):
                        o = (b * 2 + n) * P
                        sp.dma_start(a.vnew[0:TS, o:o + P], a.rows[b * TS:(b + 1) * TS, 8, k * P:(k + 1) * P]).then_inc(vn, 16)
                sp.dma_start(io["out2"][0, 0].rearrange("(t p) k g d -> p t (k g d)", p=P), a.rows[:, 0:8, 0:512]).then_inc(st, 16)
                sp.dma_start(io["out3"][0].rearrange("b t k g d -> (b t) (k g d)"), a.rows[0:NS, 8, 0:512]).then_inc(st, 16)
                sp.dma_start(io["out4"][0, 0].rearrange("(t p) k g d -> p t (k g d)", p=P), a.rows[:, 4:8, 512:768]).then_inc(st, 16)
                for b in range(NB):
                    sp.dma_start(io["out5"][0, b].rearrange("r k g d -> r (k g d)")[PAST - TS:PAST],
                                 a.rows[b * TS:(b + 1) * TS, 8, 512:768]).then_inc(st, 16)
                sp.wait_ge(st, 16 * (4 + NB))
                sp.wait_ge(vn, 16 * (NH + 2 * NB))

            @block.tensor
            def _(pe):
                pe.wait_ge(wl, 16)
                for t in range(9):
                    n = P if t < 8 else NS
                    for k in range(KD):
                        mm = pe.matmul(bank(c, 0)[0:n, 48 * t:48 * t + 48], c.xn[:, k, t * P:t * P + n], wg[:, k, :],
                                       start=(k == 0), stop=(k == KD - 1))
                mm.then_inc(gm, 1)
                for n, (t, k) in enumerate(jobs):
                    if n >= 7:
                        pe.wait_ge(ev, n - 6)
                    r = P if t < 8 else NS
                    pe.transpose(bank(c, 1 + n % 7)[0:r, 0:P], a.kvT[:, k, t * P:t * P + r], const(c, "ident")).then_inc(tr, 1)

            @block.scalar
            def _(act):
                act.wait_ge(gm, 1)
                act.activation(a.gates[:, 0:8, :], bank(c, 0)[:, 0:384].rearrange("p (t f) -> p t f", t=8), ACT.Sigmoid).then_inc(gd, 1)
                act.activation(a.gates[0:NS, 8, :], bank(c, 0)[0:NS, 384:432], ACT.Sigmoid).then_inc(gd, 1)

            @block.vector
            def _(dve):
                for n, (t, k) in enumerate(jobs):
                    dve.wait_ge(tr, n + 1)
                    r = P if t < 8 else NS
                    dve.tensor_copy(a.rows[0:r, t, k * P:(k + 1) * P], bank(c, 1 + n % 7)[0:r, 0:P]).then_inc(ev, 1)


def compress_stage(c, a):
    nc, io = c.nc, c.io
    c.at = a.free
    NPAIR = TP // 2 + NB * PAST // 2
    NW = NPAIR // 8
    LJ = 16
    xp = take(c, 2 * (NPAIR + LJ)).rearrange("p (g n) -> p g n", g=2)
    hid = take(c, 4 * NW).rearrange("p (n m) -> p n m", n=4)
    w2 = take(c, 4 * DH).rearrange("p (k n f) -> p k n f", k=2, n=2)
    bias = take(c, 4)
    SLOTS = NB * NPG // 2
    ring = c.xnf[:, 0:SLOTS * 256].rearrange("p (s q f) -> p s q f", s=SLOTS, q=2)
    w1 = c.xnf[:, 4096:8192].rearrange("p (j f) -> p j f", j=LJ)
    pos = c.xnf[0:LJ, 8192:8192 + 2 * P].rearrange("p (k f) -> p k f", k=2)
    pool_d = io["cache_nsa_kv"][0].rearrange("n (t q) k f d -> n k t q (f d)", q=2)
    PIECES, JOBS = 4, 11
    LP = LJ // PIECES
    with ExitStack() as ctx:
        wl = sems(nc, ctx, c, *[f"w1_piece{q}_loaded" for q in range(PIECES)])
        pgl = sems(nc, ctx, c, *[f"pages{q}_loaded" for q in range(4)])
        w2l, pel, tr, kept, pm, bc, hd, om, od = sems(
            nc, ctx, c, "w2_loaded", "positions_loaded", "turned", "pairs_kept", "piece_multiplied", "bias_copied",
            "hidden_done", "out_product", "out_copied")
        with nc.Block() as block:
            @block.sync
            def _(sp):
                for kind, name in enumerate("kv"):
                    sp.dma_start(pos[:, kind, :], io[f"nsa_pe_{name}"][0].rearrange("(j q) d -> j (q d)", q=2)).then_inc(pel, 16)
                    sp.dma_start(w2[:, kind], io[f"nsa_cmp_w2_{name}"][0].rearrange("(n p) f -> p n f", p=P)).then_inc(w2l, 16)
                for kind, name in enumerate("kv"):
                    w1_d = io[f"nsa_cmp_w1_{name}"][0].rearrange("(j p) f -> p j f", p=P)
                    for q in range(PIECES):
                        if kind:
                            sp.wait_ge(pm, q + 1)
                        sp.dma_start(w1[:, q * LP:(q + 1) * LP, :], w1_d[:, q * LP:(q + 1) * LP, :]).then_inc(wl[q], 16)


            @block.gpsimd
            def _(pool):
                for kind in range(2):
                    for q in range(4):
                        if kind:
                            pool.wait_ge(tr, 5 + 2 * q)
                        with pool.Fori(0, 4) as i:
                            for hf in range(2):
                                page = pool.value_load(c.pages[0:1, ds(i * 2 + (q * 8 + hf), 1)], min_val=0, max_val=NPHYS - 1)
                                dst = c.xnf[hf * 64:hf * 64 + 64, ds(i * 256 + q * 1024, 256)].rearrange("p (q f) -> p q f", q=2)
                                pool.dma_start(dst, pool_d[ds(page, 1), kind].rearrange("o t q f -> (o t) q f")).then_inc(pgl[q], 16)

            @block.tensor
            def _(pe):
                def pairs(kind):
                    pe.wait_ge(pel, 32)
                    for n in range(JOBS):
                        if n >= 4:
                            pe.wait_ge(kept, kind * JOBS + n - 3)
                        b = bank(c, 4 + n % 4)
                        if n < 2:
                            for q in range(2):
                                mm = pe.matmul(b[q * DH:(q + 1) * DH, :], const(c, "ident")[:, n * DH:(n + 1) * DH], a.kvT[:, kind, q:TP:2],
                                               start=True, stop=True)
                        elif n == 2:
                            mm = pe.transpose(b[:, 0:LJ], pos[:, kind, :], const(c, "ident")[0:LJ, 0:LJ])
                        else:
                            q, g = (n - 3) // 2, (n - 3) % 2
                            pe.wait_ge(pgl[q], 128 * (kind + 1))
                            for s in range(4):
                                for par in range(2):
                                    mm = pe.matmul(b[par * DH:(par + 1) * DH, s * P:(s + 1) * P],
                                                   ring[:, 4 * q + s, par, g * DH:(g + 1) * DH], const(c, "ident"), start=True, stop=True)
                        mm.then_inc(tr, 1)

                def hidden(kind):
                    pe.wait_ge(kept, (kind + 1) * JOBS)
                    if kind:
                        pe.wait_ge(hd, 1)
                    for j in range(LJ):
                        if j % LP == 0:
                            pe.wait_ge(wl[j // LP], 16 * (kind + 1))
                        for g in range(2):
                            for hf in range(2):
                                mm = pe.matmul(bank(c, g * 2 + hf)[:, 0:NW + 1], w1[:, j, hf * P:(hf + 1) * P], xp[:, g, j:j + 8 * NW + 1:8],
                                               start=(j == 0), stop=(j == LJ - 1))
                        if j % LP == LP - 1:
                            mm.then_inc(pm, 1)

                pairs(0)
                hidden(0)
                pairs(1)
                pe.wait_ge(hd, 1)
                pe.wait_ge(w2l, 32)
                pe.wait_ge(kept, 2 * JOBS)
                for g in range(2):
                    for hf in range(2):
                        mm = pe.matmul(bank(c, 4)[g * DH:(g + 1) * DH, 0:NW], w2[:, 0, hf, :], hid[:, g * 2 + hf, :],
                                       start=(hf == 0), stop=(hf == 1))
                mm.then_inc(om, 1)
                hidden(1)
                pe.wait_ge(hd, 2)
                pe.wait_ge(od, 1)
                for n in range(9):
                    m, o = (NCMP, 0) if n == 0 else (NCMPS, 64 + 32 * (n - 1))
                    for g in range(2):
                        for hf in range(2):
                            mm = pe.matmul(bank(c, 4 + n // 4)[0:m, (n % 4) * P + g * DH:(n % 4) * P + (g + 1) * DH],
                                           hid[:, g * 2 + hf, o:o + m], w2[:, 1, hf, :], start=(hf == 0), stop=(hf == 1))
                mm.then_inc(om, 1)

            @block.vector
            def _(dve):
                def keep_pairs(kind):
                    if kind:
                        dve.wait_ge(pm, PIECES)
                    for n in range(JOBS):
                        dve.wait_ge(tr, kind * JOBS + n + 1)
                        b = bank(c, 4 + n % 4)
                        if n < 2:
                            dve.tensor_copy(xp[:, n, 0:512], b).then_inc(kept, 1)
                        elif n == 2:
                            dve.tensor_copy(xp[:, 0, NPAIR:], b[:, 0:LJ])
                            dve.tensor_copy(xp[:, 1, NPAIR:], b[:, 0:LJ]).then_inc(kept, 1)
                        else:
                            q, g = (n - 3) // 2, (n - 3) % 2
                            dve.tensor_copy(xp[:, g, 512 * (q + 1):512 * (q + 2)], b).then_inc(kept, 1)

                def keep_bias(kind):
                    dve.wait_ge(pm, PIECES * (kind + 1))
                    if kind:
                        dve.wait_ge(hd, 1)
                    for n in range(4):
                        ins = dve.tensor_copy(bias[:, n:n + 1], bank(c, n)[:, NW:NW + 1])
                    ins.then_inc(bc, 1)

                keep_pairs(0)
                keep_bias(0)
                keep_pairs(1)
                dve.wait_ge(om, 1)
                dve.tensor_copy(a.kc, bank(c, 4)[:, 0:NW]).then_inc(od, 1)
                keep_bias(1)
                dve.wait_ge(om, 2)
                dve.tensor_copy(a.vcp[0:NCMP, :], bank(c, 4)[0:NCMP, 0:P])
                dve.tensor_copy(a.vcs[0:NCMPS, 0:3 * P], bank(c, 4)[0:NCMPS, P:4 * P])
                dve.tensor_copy(a.vcs[0:NCMPS, 3 * P:7 * P], bank(c, 5)[0:NCMPS, :])
                dve.tensor_copy(a.vcs[0:NCMPS, 7 * P:], bank(c, 6)[0:NCMPS, 0:P]).then_inc(od, 1)

            @block.scalar
            def _(act):
                for kind in range(2):
                    act.wait_ge(bc, kind + 1)
                    if kind:
                        act.wait_ge(om, 1)
                    for n in range(4):
                        ins = act.activation(hid[:, n, :], bank(c, n)[:, 0:NW], ACT.Silu, bias=bias[:, n:n + 1])
                    ins.then_inc(hd, 1)


def prompt_attention(c, a):
    nc = c.nc
    c.at = a.free
    qs = [a.kvT[:, n, 0:TP] for n in range(2)]
    pr = [take(c, 1024 + 640 + 64) for _ in range(2)]
    pts = [take(c, 512) for _ in range(2)]
    ot = [take(c, P) for _ in range(2)]
    nmax, rsum, rc, coef = take(c, 6), take(c, 6), take(c, 6), take(c, 6)
    QT = TP // P
    UNITS = [(i, g) for i in range(QT) for g in range(2)]
    NU = len(UNITS)
    NHALF = 2 * NU

    def blocks(k):
        i, g = UNITS[k // 2]
        w0 = max(0, i - 4)
        if k % 2 == 0:
            return [("s", n, 128 * n, P) for n in range(i + 1)]
        return [("w", n, 1024 + 128 * (n - w0), P) for n in range(w0, i + 1)] + [("c", 0, 1664, NCMP)]

    FLOW = []
    for k in range(NHALF):
        bl = blocks(k)
        FLOW += [(k, bl[n:n + 4]) for n in range(0, len(bl), 4)]
        if k % 4 == 1 and k > 4:
            FLOW.append(((k - 5) // 4, None))
    FLOW.append((QT - 1, None))
    NF = len(FLOW)
    taken = [x for x in range(NF) if FLOW[x][1]]
    outs = [x for x in range(NF) if not FLOW[x][1]]
    NT_, NO = len(taken), len(outs)
    S, W = 0, 1024

    with ExitStack() as ctx:
        qc, sc, mx, ex, tr, kept, okept, pv, cb, dc, mc = sems(
            nc, ctx, c, "queries_copied", "scores_done", "maxima_ready", "probs_ready", "group_turned", "group_kept", "output_kept",
            "unit_multiplied", "combined", "vector_chain", "masked")

        with nc.Block() as block:
            @block.tensor
            def _(pe):
                def scores(t, k):
                    i, g = UNITS[k // 2]
                    q = qs[g][:, i * P:(i + 1) * P]
                    w0, n = (max(0, i - 4), i + 1) if k % 2 else (0, i + 1)
                    base, tile = (W, 4) if k % 2 else (S, 2)
                    cols = (n - w0) * P
                    for o in range(0, cols, 512):
                        m = min(512, cols - o)
                        mm = pe.matmul(c.ps[:, base + o:base + o + m], q, a.kvT[:, tile, w0 * P + o:w0 * P + o + m], start=True, stop=True)
                    if k % 2:
                        mm = pe.matmul(c.ps[:, W + 640:W + 640 + NCMP], q, a.kc[:, 0:NCMP], start=True, stop=True)
                    mm.then_inc(sc, 1)

                def products(t, x):
                    k, gr = FLOW[x]
                    if gr is None:
                        return
                    u, g = k // 2, UNITS[k // 2][1]
                    o = c.ps[:, 3072 + 512 * (u % 2):3072 + 512 * (u % 2) + 384]
                    pe.wait_ge(kept, t * NT_ + taken.index(x) + 1)
                    for m, b in enumerate(gr):
                        kind, kb, col, w = b
                        same = [y for y in blocks(k) if y[0] == kind]
                        br = "csw".index(kind)
                        v = a.vcp[0:NCMP, :] if kind == "c" else a.rows[:, kb, 384:512] if kind == "s" else a.rows[:, kb, 640:768]
                        mm = pe.matmul(o[:, br * P:(br + 1) * P], pts[x % 2][0:w, m * P:(m + 1) * P], v, start=(b == same[0]), stop=(b == same[-1]))
                    if k % 2 and gr[-1][0] == "c":
                        mm.then_inc(pv, 1)

                with pe.Fori(0, HG) as t:
                    pe.wait_ge(qc, t + 1)
                    scores(t, 0)
                    scores(t, 1)
                    for x, (k, gr) in enumerate(FLOW):
                        turned = c.ps[:, 2048 + 512 * (x % 2):2048 + 512 * (x % 2) + 512]
                        if gr is None:
                            if x == NF - 1:
                                products(t, x - 1)
                            pe.wait_ge(cb, t * NU + 2 * k + 2)
                            pe.transpose(turned[:, 0:P], ot[k % 2], const(c, "ident")).then_inc(tr, 1)
                            if x < NF - 1:
                                products(t, x - 1)
                            continue
                        if gr[0] == blocks(k)[0]:
                            pe.wait_ge(ex, t * NHALF + k + 1)
                            if k + 2 < NHALF:
                                scores(t, k + 2)
                        if x >= 2 and FLOW[x - 2][1] is None:
                            pe.wait_ge(okept, t * NO + outs.index(x - 2) + 1)
                        if gr[0][0] == "c":
                            pe.nop(nofuse=True)
                        for m, (kind, kb, col, w) in enumerate(gr):
                            mm = pe.transpose(turned[0:w, m * P:(m + 1) * P], pr[(k // 2) % 2][:, col:col + w], const(c, "ident"))
                        mm.then_inc(tr, 1)
                        if gr[0] == blocks(k)[0] and k % 2 == 0 and k >= 4:
                            pe.wait_ge(cb, t * NU + k // 2 - 1)
                        if x:
                            products(t, x - 1)

            @block.scalar
            def _(act):
                def exps(t, k):
                    i, g = UNITS[k // 2]
                    p = pr[(k // 2) % 2]
                    o = 3 * ((k // 2) % 2)
                    act.wait_ge(mx, t * NHALF + k + 1)
                    if k % 2:
                        n = i + 1 - max(0, i - 4)
                        act.activation(p[:, 1664:1664 + NCMP], c.ps[:, W + 640:W + 640 + NCMP], ACT.Exp, bias=nmax[:, o:o + 1], accum_out=rsum[:, o:o + 1])
                        act.activation(p[:, 1024:1024 + n * P], c.ps[:, W:W + n * P], ACT.Exp, bias=nmax[:, o + 2:o + 3],
                                       accum_out=rsum[:, o + 2:o + 3]).then_inc(ex, 1)
                    else:
                        n = i + 1
                        act.activation(p[:, 0:n * P], c.ps[:, S:S + n * P], ACT.Exp, bias=nmax[:, o + 1:o + 2], accum_out=rsum[:, o + 1:o + 2]).then_inc(ex, 1)

                with act.Fori(0, HG) as t:
                    exps(t, 0)
                    exps(t, 1)
                    for k in range(NHALF):
                        for x in range(NF):
                            if FLOW[x][1] is None or FLOW[x][0] != k:
                                continue
                            gr = FLOW[x][1]
                            act.wait_ge(tr, t * NF + x + 1)
                            src = c.ps[:, 2048 + 512 * (x % 2):2048 + 512 * (x % 2) + 512]
                            full = len(gr) - (gr[-1][0] == "c")
                            if full:
                                ins = act.activation(pts[x % 2][:, 0:full * P], src[:, 0:full * P], ACT.Copy)
                            if full < len(gr):
                                cols = slice(full * P, (full + 1) * P)
                                ins = act.activation(pts[x % 2][0:NCMP, cols], src[0:NCMP, cols], ACT.Copy)
                            ins.then_inc(kept, 1)
                        if k + 2 < NHALF:
                            exps(t, k + 2)

            @block.vector
            def _(dve):
                def maxima(t, k):
                    i, g = UNITS[k // 2]
                    o = 3 * ((k // 2) % 2)
                    dve.wait_ge(sc, t * NHALF + k + 1)
                    if k % 2:
                        n = i + 1 - max(0, i - 4)
                        d = c.ps[:, W + (n - 1) * P:W + n * P]
                        dve.tensor_tensor(d, d, const(c, "causal_add"), ALU.add)
                        if i >= 4:
                            d = c.ps[:, W:W + P]
                            dve.tensor_tensor(d, d, const(c, "far_add"), ALU.add)
                        d = c.ps[:, W + 640:W + 640 + NCMP]
                        dve.tensor_tensor(d, d, const(c, f"cmp_add{i}"), ALU.add).then_inc(mc, 1)
                        dve.wait_ge(mc, t * NHALF + k + 1)
                        dve.tensor_reduce(nmax[:, o:o + 1], d, AX.X, ALU.max, negate=True)
                        dve.tensor_reduce(nmax[:, o + 2:o + 3], c.ps[:, W:W + n * P], AX.X, ALU.max, negate=True).then_inc(mx, 1)
                    else:
                        n = i + 1
                        d = c.ps[:, S + i * P:S + n * P]
                        dve.tensor_tensor(d, d, const(c, "causal_add"), ALU.add).then_inc(mc, 1)
                        dve.wait_ge(mc, t * NHALF + k + 1)
                        dve.tensor_reduce(nmax[:, o + 1:o + 2], c.ps[:, S:S + n * P], AX.X, ALU.max, negate=True).then_inc(mx, 1)

                CHAIN = 4 * NU + 2
                dve.memset(qs[0][DH:P, :], 0.0)
                dve.memset(qs[1][0:DH, :], 0.0)
                with dve.Fori(0, HG) as t:
                    n_chain = [0]

                    def settle(ins):
                        n_chain[0] += 1
                        ins.then_inc(dc, 1)
                        dve.wait_ge(dc, t * CHAIN + n_chain[0])

                    def coefficients(u):
                        i, g = UNITS[u]
                        o = 3 * (u % 2)
                        dve.wait_ge(ex, t * NHALF + 2 * u + 2)
                        settle(dve.reciprocal(rc[:, o:o + 3], rsum[:, o:o + 3]))
                        ins = dve.tensor_tensor(coef[:, o:o + 3], rc[:, o:o + 3],
                                                a.gates.rearrange("p t f -> p (t f)")[:, ds(t * 3 + (i * 48 + g * 24), 3)], ALU.mult)
                        if u == 0 or u == 1:
                            settle(ins)
                            ins = dve.tensor_tensor(coef[:, o:o + 1], coef[:, o:o + 1], const(c, "row_has_cmp"), ALU.mult)
                        settle(ins)

                    def combine(u):
                        i, g = UNITS[u]
                        o = 3 * (u % 2)
                        dve.wait_ge(pv, t * NU + u + 1)
                        out = ot[i % 2][:, g * DH:(g + 1) * DH]
                        acc = [c.ps[:, 3072 + 512 * (u % 2) + br * P + g * DH:3072 + 512 * (u % 2) + br * P + (g + 1) * DH] for br in range(3)]
                        settle(dve.tensor_scalar(out, acc[0], coef[:, o:o + 1], None, ALU.mult))
                        settle(dve.scalar_tensor_tensor(out=out, in0=acc[1], scalar=coef[:, o + 1:o + 2], in1=out, op0=ALU.mult, op1=ALU.add))
                        dve.scalar_tensor_tensor(out=out, in0=acc[2], scalar=coef[:, o + 2:o + 3], in1=out,
                                                 op0=ALU.mult, op1=ALU.add).then_inc(cb, 1)

                    def keep_output(x):
                        i = FLOW[x][0]
                        dve.wait_ge(tr, t * NF + x + 1)
                        dve.tensor_copy(c.xnf[:, ds(t * NT + i * P, P)], c.ps[:, 2048 + 512 * (x % 2):2048 + 512 * (x % 2) + P]).then_inc(okept, 1)

                    dve.tensor_copy(qs[0][0:DH, :], a.qTf[0:DH, ds(t * NT, TP)])
                    dve.tensor_copy(qs[1][DH:P, :], a.qTf[DH:P, ds(t * NT, TP)]).then_inc(qc, 1)
                    maxima(t, 0)
                    maxima(t, 1)
                    for k in range(NHALF):
                        if k + 2 < NHALF:
                            maxima(t, k + 2)
                        if k % 2:
                            coefficients(k // 2)
                        elif k >= 2:
                            combine(k // 2 - 1)
                        if k % 4 == 1 and k > 4:
                            keep_output(outs[(k - 5) // 4])
                    combine(NU - 1)
                    keep_output(outs[-1])
                    assert n_chain[0] == 4 * NU + 2, n_chain


def sample_attention(c, a):
    nc, io = c.nc, c.io
    c.at = a.free
    SK = PAST + TS
    kv = [take(c, NPG * 2 * P).rearrange("p (n f) -> p n f", n=NPG) for _ in range(2)]
    wn = take(c, NPG * 2 * P).rearrange("p (n f) -> p n f", n=NPG)
    kT = take(c, 2 * PAST)
    qb, knew, kcb, vcb, vnb = take(c, NS), take(c, 2 * TS), take(c, NCMPS), take(c, P), take(c, 2 * P)
    pts = [take(c, 512) for _ in range(2)]
    small = take(c, 12)
    nmax, rsum, rc, coef = [small[:, 3 * n:3 * n + 3] for n in range(4)]
    ob = take(c, P)
    dead = a.kvT[:, 0:2, :].rearrange("p k t -> p (k t)")
    sb = dead[:, 0:2 * SK + NCMPS]
    pb = dead[:, 2 * SK + NCMPS:2 * (2 * SK + NCMPS)] if 2 * (2 * SK + NCMPS) <= 2 * NT else take(c, 2 * SK + NCMPS)
    pool_d = io["cache_nsa_kv"][0].rearrange("n p k g d -> n p (k g d)")
    win_d = io["cache_nsa_win"][0].rearrange("b (n p) k g d -> b p n (k g d)", p=P)
    BL = [("s", n, 128 * n, P) for n in range(4)] + [("s", 4, PAST, TS)]
    BL += [("w", n, SK + 128 * n, P) for n in range(4)] + [("w", 4, SK + PAST, TS)] + [("c", 0, 2 * SK, NCMPS)]
    GR = [BL[0:4], BL[4:8], BL[8:11]]
    RANGE = [(2 * SK, NCMPS), (0, SK), (SK, SK)]

    with ExitStack() as ctx:
        kl0, kl1, wnl, kt_, ktc, qc, sc, scp, mx, ex, cf, tr, ev, pv, cb, ot, od, vc, used = sems(
            nc, ctx, c, "pages0_loaded", "pages1_loaded", "window_loaded", "keys_turned", "keys_copied", "inputs_copied", "scores_done",
            "scores_copied", "maxima_ready", "probs_ready", "coefficients", "probs_turned", "turned_kept", "outputs_done", "combined",
            "out_turned", "out_kept", "vector_chain", "rows_used")
        kl = [kl0, kl1]
        with nc.Block() as block:
            @block.gpsimd
            def _(pool):
                pool.sem_inc(pv, 1)
                with pool.Fori(0, NB // 2) as i:
                    for j in range(2):
                        pool.wait_ge(pv, i * 2 + 1)
                        for n in range(NPG):
                            page = pool.value_load(c.pages[0:1, ds(i * 8 + j * 4 + n, 1)], min_val=0, max_val=NPHYS - 1)
                            pool.dma_start(kv[j][:, n, :], pool_d[ds(page, 1), :, 256:512].rearrange("o p f -> p (o f)")).then_inc(kl[j], 16)

            @block.sync
            def _(sp):
                sp.dma_start(wn, win_d[0]).then_inc(wnl, 16)
                with sp.Fori(0, NB - 1) as b:
                    sp.wait_ge(pv, b + 2)
                    sp.dma_start(wn, win_d[ds(b + 1, 1)].rearrange("o p n f -> p (o n) f")).then_inc(wnl, 16)

            def product(pe, j, b, x):
                pe.wait_ge(ev, b * 3 + x + 1)
                pe.nop(nofuse=True)
                for m, (kind, n, col, w) in enumerate(GR[x]):
                    br = "csw".index(kind)
                    for g in range(2):
                        f = slice(g * DH, (g + 1) * DH)
                        if kind == "c":
                            v = vcb[0:NCMPS, f]
                        elif n == 4:
                            v = vnb[0:TS, "sw".index(kind) * P + g * DH:"sw".index(kind) * P + (g + 1) * DH]
                        else:
                            v = (kv[j] if kind == "s" else wn)[:, n, P + g * DH:P + (g + 1) * DH]
                        mm = pe.matmul(bank(c, 7)[f, br * DH:(br + 1) * DH], pts[x % 2][0:w, m * P + g * DH:m * P + (g + 1) * DH], v,
                                       start=(n == 0), stop=(n == 4 or kind == "c"), skip_group_check=True)
                return mm

            @block.tensor
            def _(pe):
                with pe.Fori(0, NB // 2) as i:
                    for j in range(2):
                        b = i * 2 + j
                        pe.wait_ge(kl[j], i * 64 + 64)
                        for n in range(NPG):
                            pe.transpose(bank(c, 0)[:, n * P:(n + 1) * P], kv[j][:, n, 0:P], const(c, "ident"))
                        pe.wait_ge(wnl, b * 16 + 16)
                        for n in range(NPG):
                            mm = pe.transpose(bank(c, 1)[:, n * P:(n + 1) * P], wn[:, n, 0:P], const(c, "ident"))
                        mm.then_inc(kt_, 1)
                        pe.wait_ge(ktc, b + 1)
                        pe.wait_ge(qc, b + 1)
                        pe.nop(nofuse=True)
                        for g in range(2):
                            rows = slice(g * DH, (g + 1) * DH)
                            for n in range(2):
                                pe.matmul(bank(c, 2 + n)[rows, :], qb[rows, :], kT[rows, n * PAST:(n + 1) * PAST], start=True, stop=True)
                            pe.matmul(bank(c, 4)[rows, 0:2 * TS], qb[rows, :], knew[rows, :], start=True, stop=True)
                            mm = pe.matmul(bank(c, 4)[rows, 2 * TS:2 * TS + NCMPS], qb[rows, :], kcb[rows, :], start=True, stop=True)
                        mm.then_inc(sc, 1)
                        pe.wait_ge(ex, b + 1)
                        pe.nop(nofuse=True)
                        for x, gr in enumerate(GR):
                            if x == 2:
                                pe.wait_ge(ev, b * 3 + 1)
                                pe.nop(nofuse=True)
                            for m, (kind, n, col, w) in enumerate(gr):
                                mm = pe.transpose(bank(c, 5 + x % 2)[0:w, m * P:(m + 1) * P], pb[:, col:col + w], const(c, "ident"))
                            mm.then_inc(tr, 1)
                            if x:
                                product(pe, j, b, x - 1)
                        product(pe, j, b, 2).then_inc(pv, 1)
                        pe.wait_ge(cb, b + 1)
                        pe.transpose(bank(c, 0)[:, 0:P], ob, const(c, "ident")).then_inc(ot, 1)
                        pe.wait_ge(od, b + 1)

            @block.vector
            def _(dve):
                CHAIN = 6
                with dve.Fori(0, NB) as b:
                    n_chain = [0]

                    def settle(ins):
                        n_chain[0] += 1
                        ins.then_inc(vc, 1)
                        dve.wait_ge(vc, b * CHAIN + n_chain[0])

                    dve.tensor_copy(qb.rearrange("p (h t) -> p h t", h=HG), a.qT[:, :, ds(b * TS + TP, TS)])
                    dve.tensor_copy(knew.rearrange("p (n t) -> p n t", n=2), a.kvT[:, 2:6:2, ds(b * TS + TP, TS)])
                    dve.tensor_copy(kcb, a.kc[:, ds(b * 32 + 64, NCMPS)])
                    dve.tensor_copy(vcb[0:NCMPS, :], a.vcs[0:NCMPS, ds(b * P, P)])
                    dve.tensor_copy(vnb[0:TS, :], a.vnew[0:TS, ds(b * (2 * P), 2 * P)]).then_inc(qc, 1)
                    dve.wait_ge(kt_, b + 1)
                    dve.tensor_copy(kT, c.ps[:, 0:1024]).then_inc(ktc, 1)
                    dve.wait_ge(sc, b + 1)
                    dve.tensor_copy(sb[:, 0:PAST], bank(c, 2))
                    dve.tensor_tensor(sb[:, PAST:SK], bank(c, 4)[:, 0:TS], const(c, "s_new_add"), ALU.add)
                    dve.tensor_tensor(sb[:, SK:SK + TS], bank(c, 3)[:, 0:TS], const(c, "s_far_add"), ALU.add)
                    dve.tensor_copy(sb[:, SK + TS:SK + PAST], bank(c, 3)[:, TS:PAST])
                    dve.tensor_tensor(sb[:, SK + PAST:2 * SK], bank(c, 4)[:, TS:2 * TS], const(c, "s_new_add"), ALU.add)
                    settle(dve.tensor_copy(sb[:, 2 * SK:], bank(c, 4)[:, 2 * TS:2 * TS + NCMPS]))
                    for br, (o, n) in enumerate(RANGE):
                        ins = dve.tensor_reduce(nmax[:, br:br + 1], sb[:, o:o + n], AX.X, ALU.max, negate=True)
                    ins.then_inc(mx, 1)
                    dve.wait_ge(ex, b + 1)
                    settle(dve.reciprocal(rc, rsum))
                    settle(dve.tensor_tensor(coef, rc, a.sgates[:, ds(b * 3, 3)], ALU.mult))
                    for x in range(3):
                        dve.wait_ge(tr, b * 3 + x + 1)
                        ws = [w for *_, w in GR[x]]
                        lo = 0
                        while lo < len(ws):
                            hi = lo
                            while hi < len(ws) and ws[hi] == ws[lo]:
                                hi += 1
                            ins = dve.tensor_copy(pts[x % 2][0:ws[lo], lo * P:hi * P], bank(c, 5 + x % 2)[0:ws[lo], lo * P:hi * P])
                            lo = hi
                        ins.then_inc(ev, 1)
                    dve.wait_ge(pv, b + 2)
                    acc = bank(c, 7)
                    settle(dve.tensor_scalar(ob[:, 0:DH], acc[:, 0:DH], coef[:, 0:1], None, ALU.mult))
                    for br in (1, 2):
                        settle(dve.scalar_tensor_tensor(out=ob[:, 0:DH], in0=acc[:, br * DH:(br + 1) * DH], scalar=coef[:, br:br + 1],
                                                        in1=ob[:, 0:DH], op0=ALU.mult, op1=ALU.add))
                    dve.tensor_copy(ob[:, DH:P], ob[:, 0:DH]).then_inc(cb, 1)
                    dve.wait_ge(ot, b + 1)
                    xo = c.xn[:, :, ds(b * TS + TP, TS)]
                    dve.tensor_copy(xo[0:DH], bank(c, 0)[0:DH, 0:NS].rearrange("p (h t) -> p h t", h=HG))
                    dve.tensor_copy(xo[DH:P], bank(c, 0)[DH:P, NS:P].rearrange("p (h t) -> p h t", h=HG)).then_inc(od, 1)
                    assert n_chain[0] == CHAIN, n_chain

            @block.scalar
            def _(act):
                with act.Fori(0, NB) as b:
                    act.wait_ge(mx, b + 1)
                    for br, (o, n) in enumerate(RANGE):
                        ins = act.activation(pb[:, o:o + n], sb[:, o:o + n], ACT.Exp, bias=nmax[:, br:br + 1], accum_out=rsum[:, br:br + 1])
                    ins.then_inc(ex, 1)


def nsa_layer(c):
    norm_stage(c, 1, c.xn, 0)
    a = nsa_buffers(c)
    nsa_project(c, a)
    compress_stage(c, a)
    prompt_attention(c, a)
    sample_attention(c, a)
    c.at = a.free
    wb = [take(c, KD * P).rearrange("p (k f) -> p k f", k=KD) for _ in range(2)]
    w_out = c.io["nsa_w_out"][0]

    def src(m, j):
        return [(wb[j][g * DH:(g + 1) * DH, :, :],
                 w_out[g * 512:(g + 1) * 512, ds(m * P, P)].rearrange("(h d) f -> d h f", d=DH)) for g in range(2)]

    out_stage(c, KD, src, c.xn, wb)


def hybrid_decoder_kernel(nc, io):
    with ExitStack() as ctx:
        c = open_core(nc, ctx, io)
        load_stage(c)
        norm_stage(c, 0, c.xn, 0)
        gate_stage(c)
        gdn_stage(c)
        ffn_stages(c, 0)
        recycle_semaphores(c)
        nsa_layer(c)
        recycle_semaphores(c)
        ffn_stages(c, 1)
        final_stage(c)


_INS = ['x_prompt', 'x_sample', 'cache_nsa_kv', 'cache_nsa_win', 'state_gdn', 'state_gdn_conv', 'page_table',
        'norm1_w', 'norm2_w', 'final_norm_w', 'gdn_w_in', 'gdn_conv_w', 'gdn_A_log', 'gdn_dt_bias', 'gdn_norm_w', 'gdn_w_out',
        'nsa_w_in', 'nsa_pe_k', 'nsa_pe_v', 'nsa_cmp_w1_k', 'nsa_cmp_w2_k', 'nsa_cmp_w1_v', 'nsa_cmp_w2_v', 'nsa_w_out',
        'ffn_w_in', 'ffn_w_out']
_OUTS = [(1, 1024, 1024), (8, 8, 1024), (1, 1, 1024, 4, 2, 64), (1, 8, 8, 4, 2, 64), (1, 1, 512, 2, 2, 64),
         (1, 8, 512, 2, 2, 64), (1, 1, 8, 128, 128), (1, 8, 8, 128, 128), (1, 1, 3, 3072), (1, 8, 3, 3072)]


def kernel(**inputs):
    import concourse.bacc as _bacc
    from concourse.bass_utils import run_bass_kernel_spmd as _run

    nc = _bacc.Bacc("TRN2", target_bir_lowering=False, num_devices=1)
    arrays, io = {}, {}
    for name in _INS:
        a = np.ascontiguousarray(inputs[name])
        arrays[f"in_{name}_dram"] = a
        io[name] = nc.dram_tensor(f"in_{name}_dram", a.shape, mybir.dt.from_np(a.dtype), kind="ExternalInput").ap()
    table = const_table()
    arrays["in_consts_dram"] = table
    io["consts"] = nc.dram_tensor("in_consts_dram", table.shape, F32, kind="ExternalInput").ap()
    for i, shape in enumerate(_OUTS):
        io[f"out{i}"] = nc.dram_tensor(f"out_{i}_dram", shape, F32, kind="ExternalOutput").ap()
    hybrid_decoder_kernel(nc, io)
    r = _run(nc, [arrays], core_ids=[0])
    return tuple(r.results[0][f"out_{i}_dram"] for i in range(len(_OUTS)))
```
